# Optimizing a Trainium2 kernel written in Bass

```python
import math
import jax, jax.numpy as jnp
from jax import lax
import numpy as np

D_MODEL = 1024
BATCH = 1
SEQ = 512
DEPTH = 2
DEC_BATCH = 8
DEC_SEQ = 1
PAST_LEN = 4096
PAGE_SIZE = 128

N_MEM = 256
E_SSM = D_MODEL // 2
SSM_GROUP = 16
N_SSM_GROUPS = E_SSM // SSM_GROUP
SSM_STATE = 64
DT_MIN = 1e-3
DT_MAX = 1e-1
E_CONV = D_MODEL // 2
CONV_WIDTH = 31
E_XATT = D_MODEL // 2
N_XHEADS = 4
XHEAD_DIM = E_XATT // N_XHEADS
EPS = 1e-6

IN_SIZES = (E_SSM, E_SSM, 2 * E_CONV, E_CONV, E_XATT, E_XATT, D_MODEL, D_MODEL, D_MODEL)
IN_TOTAL = int(sum(IN_SIZES))
IN_SPLITS = [int(v) for v in np.cumsum(IN_SIZES)[:-1]]

kernel_name = "s5_conformer_memxattn_gated_hybrid_step"

def rmsnorm(x, g):
    xf = x.astype(jnp.float32)
    y = xf * lax.rsqrt(jnp.mean(xf * xf, axis=-1, keepdims=True) + EPS) * g.astype(jnp.float32)
    return y.astype(x.dtype)

def layernorm(x, g, b):
    xf = x.astype(jnp.float32)
    mu = jnp.mean(xf, axis=-1, keepdims=True)
    var = jnp.mean(jnp.square(xf - mu), axis=-1, keepdims=True)
    y = (xf - mu) * lax.rsqrt(var + EPS) * g.astype(jnp.float32) + b.astype(jnp.float32)
    return y.astype(x.dtype)

def _to_c(re, im):
    return lax.complex(re.astype(jnp.float32), im.astype(jnp.float32))

def _lin_rec(e1, e2):
    a1, b1 = e1
    a2, b2 = e2
    return a1 * a2, a2 * b1 + b2

def s5_branch(u, s0, a_re, a_im, log_dt, b_re, b_im, c_re, c_im, d):
    bsz, L, _ = u.shape
    uf = u.astype(jnp.float32).reshape(bsz, L, N_SSM_GROUPS, SSM_GROUP)
    lam = _to_c(a_re, a_im)
    dt = jnp.exp(log_dt.astype(jnp.float32))[:, None]
    lam_bar = jnp.exp(lam * dt)
    b_bar = ((lam_bar - 1.0) / lam)[..., None] * _to_c(b_re, b_im)
    bu = jnp.einsum('blgh,gph->blgp', uf.astype(jnp.complex64), b_bar)
    a = jnp.broadcast_to(lam_bar, bu.shape)
    a_cum, xs = lax.associative_scan(_lin_rec, (a, bu), axis=1)
    xs = xs + a_cum * s0[:, None]
    y = jnp.einsum('blgp,ghp->blgh', xs, _to_c(c_re, c_im)).real
    y = y + d.astype(jnp.float32).reshape(N_SSM_GROUPS, SSM_GROUP) * uf
    return y.reshape(bsz, L, E_SSM), xs[:, -1]

def causal_depthwise_conv(v, buf, w, b):
    full = jnp.concatenate([buf.astype(v.dtype), v], axis=1)
    out = lax.conv_general_dilated(full, w.astype(v.dtype)[:, None, :], window_strides=(1,), padding='VALID',
                                   dimension_numbers=('NWC', 'WIO', 'NWC'), feature_group_count=E_CONV)
    return out + b.astype(v.dtype), full[:, -(CONV_WIDTH - 1):]

def mem_kv(mem, g, w_k, w_v):
    hm = rmsnorm(mem, g)
    bsz = mem.shape[0]
    k = (hm @ w_k).reshape(bsz, N_MEM, N_XHEADS, XHEAD_DIM)
    v = (hm @ w_v).reshape(bsz, N_MEM, N_XHEADS, XHEAD_DIM)
    return k, v

def mixer_layer(x, s0_re, s0_im, conv_buf, mk, mv, p):
    bsz, L, _ = x.shape
    h = rmsnorm(x, p['norm_g'])
    u_a, z_a, u_b, z_b, q, z_x, g_a, g_b, g_x = jnp.split(h @ p['w_in'], IN_SPLITS, axis=-1)
    s0 = _to_c(s0_re, s0_im)
    y_a, s_new = s5_branch(u_a, s0, p['a_re'], p['a_im'], p['log_dt'], p['b_re'], p['b_im'],
                           p['c_re'], p['c_im'], p['d'])
    y_a = jax.nn.gelu(y_a).astype(x.dtype)
    y_a = y_a * jax.nn.sigmoid(y_a @ p['w_glu'] + p['b_glu'])
    o_a = (y_a * jax.nn.silu(z_a)) @ p['w_br_ssm']
    v_b = u_b[..., :E_CONV] * jax.nn.sigmoid(u_b[..., E_CONV:])
    c_b, buf_new = causal_depthwise_conv(v_b, conv_buf, p['conv_w'], p['conv_b'])
    c_b = jax.nn.silu(layernorm(c_b, p['ln_g'], p['ln_b']))
    o_b = (c_b * jax.nn.silu(z_b)) @ p['w_br_conv']
    qh = q.reshape(bsz, L, N_XHEADS, XHEAD_DIM).astype(jnp.float32)
    s = jnp.einsum('blhd,bmhd->bhlm', qh, mk.astype(jnp.float32)) * (1.0 / math.sqrt(XHEAD_DIM))
    prob = jax.nn.softmax(s, axis=-1).astype(mv.dtype)
    o_x = jnp.einsum('bhlm,bmhd->blhd', prob, mv).reshape(bsz, L, E_XATT).astype(x.dtype)
    o_x = (o_x * jax.nn.silu(z_x)) @ p['w_br_xatt']
    m = jax.nn.sigmoid(g_a) * o_a + jax.nn.sigmoid(g_b) * o_b + jax.nn.sigmoid(g_x) * o_x
    x = x + (m @ p['w_out']).astype(x.dtype)
    return x, jnp.real(s_new), jnp.imag(s_new), buf_new

def setup_inputs(seed: int = 0) -> dict:
    key = jax.random.key(seed)
    ks = jax.random.split(key, 40)
    f32 = jnp.float32
    nrm = lambda k, shape, scale: (jax.random.normal(k, shape, f32) * scale)
    G, P, H = N_SSM_GROUPS, SSM_STATE, SSM_GROUP
    inp = {}
    inp['x_prompt'] = nrm(ks[0], (BATCH, SEQ, D_MODEL), 1.0)
    inp['x_sample'] = nrm(ks[1], (DEC_BATCH, DEC_SEQ, D_MODEL), 1.0)
    inp['mem_prompt'] = nrm(ks[2], (BATCH, N_MEM, D_MODEL), 1.0)
    inp['state_ssm_re'] = nrm(ks[3], (DEPTH, DEC_BATCH, G, P), 0.1)
    inp['state_ssm_im'] = nrm(ks[4], (DEPTH, DEC_BATCH, G, P), 0.1)
    inp['state_conv'] = nrm(ks[5], (DEPTH, DEC_BATCH, CONV_WIDTH - 1, E_CONV), 1.0)
    inp['cache_mem_k'] = nrm(ks[6], (DEPTH, DEC_BATCH, N_MEM, N_XHEADS, XHEAD_DIM), 1.0)
    inp['cache_mem_v'] = nrm(ks[7], (DEPTH, DEC_BATCH, N_MEM, N_XHEADS, XHEAD_DIM), 1.0)
    inp['norm_g'] = 1.0 + nrm(ks[8], (DEPTH, D_MODEL), 0.02)
    inp['w_in'] = nrm(ks[9], (DEPTH, D_MODEL, IN_TOTAL), D_MODEL ** -0.5)
    inp['ssm_a_re'] = -0.5 + nrm(ks[10], (DEPTH, G, P), 0.01)
    inp['ssm_a_im'] = math.pi * jnp.broadcast_to(jnp.arange(P, dtype=f32), (DEPTH, G, P)) + nrm(ks[11], (DEPTH, G, P), 0.01)
    inp['ssm_log_dt'] = jax.random.uniform(ks[12], (DEPTH, G), f32, math.log(DT_MIN), math.log(DT_MAX))
    inp['ssm_b_re'] = nrm(ks[13], (DEPTH, G, P, H), (2 * H) ** -0.5)
    inp['ssm_b_im'] = nrm(ks[14], (DEPTH, G, P, H), (2 * H) ** -0.5)
    inp['ssm_c_re'] = nrm(ks[15], (DEPTH, G, H, P), (2 * P) ** -0.5 * 4.0)
    inp['ssm_c_im'] = nrm(ks[16], (DEPTH, G, H, P), (2 * P) ** -0.5 * 4.0)
    inp['ssm_d'] = nrm(ks[17], (DEPTH, E_SSM), 1.0)
    inp['w_glu'] = nrm(ks[18], (DEPTH, E_SSM, E_SSM), E_SSM ** -0.5)
    inp['b_glu'] = nrm(ks[19], (DEPTH, E_SSM), 0.01)
    inp['w_br_ssm'] = nrm(ks[20], (DEPTH, E_SSM, D_MODEL), E_SSM ** -0.5)
    inp['conv_w'] = nrm(ks[21], (DEPTH, CONV_WIDTH, E_CONV), CONV_WIDTH ** -0.5)
    inp['conv_b'] = nrm(ks[22], (DEPTH, E_CONV), 0.01)
    inp['conv_ln_g'] = 1.0 + nrm(ks[23], (DEPTH, E_CONV), 0.02)
    inp['conv_ln_b'] = nrm(ks[24], (DEPTH, E_CONV), 0.01)
    inp['w_br_conv'] = nrm(ks[25], (DEPTH, E_CONV, D_MODEL), E_CONV ** -0.5)
    inp['mem_norm_g'] = 1.0 + nrm(ks[26], (DEPTH, D_MODEL), 0.02)
    inp['w_k'] = nrm(ks[27], (DEPTH, D_MODEL, E_XATT), D_MODEL ** -0.5)
    inp['w_v'] = nrm(ks[28], (DEPTH, D_MODEL, E_XATT), D_MODEL ** -0.5)
    inp['w_br_xatt'] = nrm(ks[29], (DEPTH, E_XATT, D_MODEL), E_XATT ** -0.5)
    inp['w_out'] = nrm(ks[30], (DEPTH, D_MODEL, D_MODEL), D_MODEL ** -0.5)
    inp['final_norm_g'] = 1.0 + nrm(ks[31], (D_MODEL,), 0.02)
    return inp

def reference(x_prompt, x_sample, mem_prompt, state_ssm_re, state_ssm_im, state_conv, cache_mem_k, cache_mem_v,
              norm_g, w_in, ssm_a_re, ssm_a_im, ssm_log_dt, ssm_b_re, ssm_b_im, ssm_c_re, ssm_c_im, ssm_d,
              w_glu, b_glu, w_br_ssm, conv_w, conv_b, conv_ln_g, conv_ln_b, w_br_conv,
              mem_norm_g, w_k, w_v, w_br_xatt, w_out, final_norm_g):
    bp = x_prompt.shape[0]
    xp, xs = x_prompt, x_sample
    p_re, p_im, p_conv, p_k, p_v = [], [], [], [], []
    s_re, s_im, s_conv = [], [], []
    for l in range(DEPTH):
        prm = {'norm_g': norm_g[l], 'w_in': w_in[l], 'a_re': ssm_a_re[l], 'a_im': ssm_a_im[l],
               'log_dt': ssm_log_dt[l], 'b_re': ssm_b_re[l], 'b_im': ssm_b_im[l], 'c_re': ssm_c_re[l],
               'c_im': ssm_c_im[l], 'd': ssm_d[l], 'w_glu': w_glu[l], 'b_glu': b_glu[l],
               'w_br_ssm': w_br_ssm[l], 'conv_w': conv_w[l], 'conv_b': conv_b[l], 'ln_g': conv_ln_g[l],
               'ln_b': conv_ln_b[l], 'w_br_conv': w_br_conv[l], 'w_br_xatt': w_br_xatt[l], 'w_out': w_out[l]}
        mk, mv = mem_kv(mem_prompt, mem_norm_g[l], w_k[l], w_v[l])
        z_state = jnp.zeros((bp, N_SSM_GROUPS, SSM_STATE), jnp.float32)
        z_buf = jnp.zeros((bp, CONV_WIDTH - 1, E_CONV), xp.dtype)
        xp, r, i, b = mixer_layer(xp, z_state, z_state, z_buf, mk, mv, prm)
        p_re.append(r); p_im.append(i); p_conv.append(b); p_k.append(mk); p_v.append(mv)
        xs, r, i, b = mixer_layer(xs, state_ssm_re[l], state_ssm_im[l], state_conv[l],
                                  cache_mem_k[l], cache_mem_v[l], prm)
        s_re.append(r); s_im.append(i); s_conv.append(b)
    y_prompt = rmsnorm(xp, final_norm_g)
    y_sample = rmsnorm(xs, final_norm_g)
    return (y_prompt, y_sample, jnp.stack(p_re), jnp.stack(p_im), jnp.stack(p_conv), jnp.stack(p_k), jnp.stack(p_v),
            jnp.stack(s_re), jnp.stack(s_im), jnp.stack(s_conv))


_drawn_inputs = setup_inputs


def setup_inputs(seed=0):
    import zlib

    import numpy as np

    out = dict(_drawn_inputs(seed))
    spreads = {}
    factors = {'ssm_a_re': 15.351,
     'b_glu': 64.0,
     'conv_b': 8.0,
     'conv_ln_g': 8.0,
     'conv_ln_b': 35.577,
     'mem_norm_g': 8.364,
     'final_norm_g': 8.355,
     'cache_mem_k': 3.753,
     'cache_mem_v': 2.816,
     'ssm_c_re': 2.907,
     'ssm_c_im': 2.907}
    for name, (base, spread) in spreads.items():
        noise = np.random.default_rng([zlib.crc32(name.encode()), seed]).standard_normal(out[name].shape)
        drawn = base * np.exp(spread * noise) if base else spread * noise
        out[name] = __import__('jax').numpy.asarray(drawn.astype(out[name].dtype))
    for name, factor in factors.items():
        out[name] = (out[name] * factor).astype(out[name].dtype)
    return out
```

```python
from contextlib import ExitStack

import concourse.bass as bass
from concourse import mybir

F32 = mybir.dt.float32
F32R = mybir.dt.float32r
ALU = mybir.AluOpType
ACT = mybir.ActivationFunctionType
AX = mybir.AxisListType

P = 128
D = 1024
SEQ = 512
LAYERS = 2
NB = 8
MEM = 256
KT = D // P
E = 512
ET = E // P
HEADS = 4
G, H, S = 32, 16, 64
Q = G // 2
QH = Q // 2
T = 8
C = SEQ // T
TAPS = 31
HC = 4 * C + 4
EPS = 1e-6
SCALE = P ** -0.5
XC = NB + 1 + C
UC = NB + C + NB
YC = NB + C
UNITS = 60
TWO_PI = 6.283185307179586
PI2_HI, PI2_MID = 6.28125, 0.0019350051879882812
PI2_LO = TWO_PI - PI2_HI - PI2_MID
PI_BELOW = 3.1415925
ROUND = 12582912.0


class Steps:

    def __init__(self, eng, sem):
        self.eng, self.sem, self.n = eng, sem, 0

    def run(self, ins):
        self.n += 1
        ins.then_inc(self.sem, 1)
        self.eng.wait_ge(self.sem, self.n)

    def clear(self):
        self.eng.sem_clear(self.sem)
        self.n = 0


def build(nc, x_prompt, x_sample, mem_prompt, state_ssm_re, state_ssm_im, state_conv, cache_mem_k,
          cache_mem_v, norm_g, w_in, ssm_a_re, ssm_a_im, ssm_log_dt, ssm_b_re, ssm_b_im, ssm_c_re,
          ssm_c_im, ssm_d, w_glu, b_glu, w_br_ssm, conv_w, conv_b, conv_ln_g, conv_ln_b, w_br_conv,
          mem_norm_g, w_k, w_v, w_br_xatt, w_out, final_norm_g, y_prompt, y_sample, ssm_re_p, ssm_im_p,
          conv_p, mem_k_p, mem_v_p, ssm_re_s, ssm_im_s, conv_s):
    ctx = ExitStack()

    def sb(name, shape, dt=F32):
        return ctx.enter_context(nc.sbuf_tensor(name, shape, dt))

    def sem(name):
        return ctx.enter_context(nc.semaphore(name))

    with ctx:
        xT = sb("xT", [P, KT, 2, HC])
        h_hi = sb("h_hi", [P, KT, 2, HC], F32R)
        h_lo = sb("h_lo", [P, KT, 2, HC], F32R)
        w_hi = sb("w_hi", [P, 2, KT * P], F32R)
        w_lo = sb("w_lo", [P, 2, KT * P], F32R)
        w_st = sb("w_st", [P, 2, KT * P])
        w_dir = sb("w_dir", [P, 2, 12 * P])
        q = sb("q", [P, ET, 2, HC])
        sg = sb("sg", [P, 2, 2, HC])
        ident = sb("ident", [P, P])
        ones = sb("ones", [P, P])
        vec = sb("vec", [P, 88])
        cw = sb("cw", [P, TAPS * ET])
        dcol = sb("dcol", [H, G])
        pw = sb("pw", [P, 2, Q, T + 1])
        lv = sb("lv", [P, 6, 2, Q])
        tiny = sb("tiny", [P, 12, Q])
        stat = sb("stat", [P, 64])
        s0 = sb("s0", [P, 2, NB, Q])
        sn = sb("sn", [P, 2, NB, Q])
        sf = sb("sf", [P, 2, Q])
        v_s = sb("v_s", [P, ET, NB])
        v_last = sb("v_last", [P, ET, 32])

        z_at = nc.sbuf_base
        zreg = sb("zreg", [P, 12 * 2 * HC])
        v_at = nc.sbuf_base
        vreg = sb("vreg", [P, ET * 16 * (C + 4)])
        u_at = nc.sbuf_base
        ureg = sb("ureg", [P, ET * 2 * HC])
        r_at = nc.sbuf_base
        rlen = 13312
        rreg = sb("rreg", [P, rlen])
        assert v_at == z_at + 4 * 12 * 2 * HC

        def at(base, off, limit, name, shape, dt=F32):
            n = 1
            for d in shape[1:]:
                n *= d
            assert off + n <= limit, (name, off + n, limit)
            return nc.alloc_sbuf_tensor_at(name, shape, dt, offset=base + 4 * off)

        def zr(name, off, shape):
            return at(z_at, off, 12 * 2 * HC, name, shape)

        def ur(name, off, shape):
            return at(u_at, off, ET * 2 * HC, name, shape)

        def rr(name, off, shape):
            return at(r_at, off, rlen, name, shape)

        z = zr("z", 0, [P, 3, ET, 2, HC])
        m_hi = at(z_at, 0, 10**6, "m_hi", [P, KT, 2, HC], F32R)
        m_lo = at(z_at, KT * 2 * HC, 10**6, "m_lo", [P, KT, 2, HC], F32R)
        assert 2 * KT * 2 * HC <= 12 * 2 * HC + ET * 16 * (C + 4)
        vx = at(v_at, 0, 10**6, "vx", [P, ET, 16, C + 4])
        u = ur("u", 0, [P, ET, 2, HC])
        prow = ur("prow", 0, [88, P])
        cwrow = ur("cwrow", 128, [TAPS * ET, P])
        crow = ur("crow", 256, [P, 2, 2, P])
        srow = ur("srow", 768, [P, 2, P])
        drow = ur("drow", 1024, [G, H])
        dtrow = ur("dtrow", 1040, [80, 2])
        bT = zr("bT", 0, [P, 2, Q, H])
        bb = zr("bb", 512, [P, 2, Q, H])
        cT = zr("cT", 1024, [P, 2, Q, H])
        wt = zr("wt", 1536, [P, 2, QH, T * H])
        kt = zr("kt", 1536, [H, G // 2, T * H])
        xrow = rr("xrow", 0, [P, 4, D])
        mrow = rr("mrow", 4096, [P, 2, D])
        xsrow = rr("xsrow", 6144, [NB, D])
        memn0 = rr("memn0", 7168, [P, KT, MEM])
        memn = rr("memn", 0, [P, KT, MEM])
        memg = rr("memg", 2048, [P, KT, MEM])
        kb = rr("kb", 0, [P, 2, 2, E])
        kbT = rr("kbT", 2048, [P, HEADS, MEM])
        qm = rr("qm", 3072, [P, NB * HEADS, 32])
        ktok = rr("ktok", 4096, [P, 2, E])
        ps = rr("ps", 4096, [32, MEM])
        pm = zr("pm", 3584, [P, 2, NB, 32])
        vtok = rr("vtok", 5120, [P, 2, E])
        kT = rr("kT", 6144, [P, HEADS, MEM])
        pr = rr("pr", 7168, [P, 2, HEADS, MEM])
        oxs = rr("oxs", 7168, [32, E])
        pT = rr("pT", 9216, [P, HEADS, 2, SEQ])
        sq = rr("sq", 9216, [P, 4, 2, HC])
        ht = rr("ht", 9216 + 2080, [P, 2, 2, HC])
        rs = rr("rs", 9216 + 3120, [P, 2, HC])
        U = rr("U", 0, [P, Q, 2, UC])
        wl = rr("wl", 2560, [P, 2, QH, P])
        V = rr("V", 4608, [P, 2, QH, T + 1, H])
        Mt = rr("Mt", 6912, [P, G // 2, T * H])
        X = rr("X", 8960, [P, 2, QH, XC])
        ss = rr("ss", 10128, [P, 2, QH, NB])
        t1 = rr("t1", 10256, [P, QH * (T + 1) * H])
        t2 = rr("t2", 11408, [P, QH * (T + 1) * H])
        br = rr("br", 0, [P, 3, ET, 2, HC])
        acc = rr("acc", 6240, [P, ET, 2, HC])
        cs = rr("cs", 8320, [P, ET, NB, TAPS])
        cst = rr("cst", 9312, [P, NB, TAPS])
        crw = rr("crw", 9560, [120, 2, E])
        lsq = rr("lsq", 10584, [P, 2, 2, HC])
        lst = rr("lst", 11624, [P, 2, HC])
        mj = rr("mj", 12144, [P, 2, HC])
        cacc = rr("cacc", 10584, [P, 2, T, C])
        so = rr("so", 12664, [P, 4, P])
        nst = rr("nst", 11624, [32, E])
        nss = rr("nss", 12144, [NB, E])
        tj = rr("tj", 11624, [P, 2, HC])
        yrow = rr("yrow", 0, [P, 2, D])
        ysr = rr("ysr", 2048, [NB, D])
        xsc = rr("xsc", 3072, [P, KT, NB])

        acc_ps = [ctx.enter_context(nc.psum_tensor(f"acc{i}", [P, 2, 512], F32)) for i in range(2)]
        mp = ctx.enter_context(nc.psum_tensor("mp", [P, 4, 512], F32))

        u_dram = nc.dram_tensor("u_scratch", (E, 2, HC), F32).ap()
        y_dram = nc.dram_tensor("y_scratch", (E, 2, HC), F32).ap()
        k_dram = nc.dram_tensor("k_scratch", (G, H, T * H), F32).ap()
        m_dram = nc.dram_tensor("m_scratch", (P, KT * MEM), F32).ap()

        w_loaded = [sem(f"w_loaded{i}") for i in range(2)]
        w_staged_free = sem("w_staged_free")
        w_hi_done = sem("w_hi_done")
        w_lo_done = sem("w_lo_done")
        layer_left = {e: sem(f"layer_left_{e}") for e in ("sp", "pe", "act")}
        layer_go = sem("layer_go")
        layers_begun = sem("layers_begun")
        dve_steps = sem("dve_steps")
        act_steps = sem("act_steps")
        loop_steps = sem("loop_steps")

        sm = {n: sem(n) for n in """
            x_in mem_in consts x_tr x_ev mem_sq mem_var mem_rt mem_nrm mem_tr mem_ev mem_out fin_sq fin_used
            fin_var fin_rt fin_y fin_tr fin_ev fin_out0 fin_out1 fin_out2 fin_out3 fin_out_s""".split()}
        entered = {e: sem(f"entered_{e}") for e in ("sp", "pe")}

        per = """
            dt_in=16 dt_wide=1 p_in=176 c_in=128 b_in=64 s_in=32 mg_in=16 sq_done=8 sq_used=8 var_done=1
            rstd_done=1 ht_done=8 hhi_done=8 h_done=1 par_tr=1 par_ev=1 s0_tr=1 s0_ev=1 memg_done=1
            kv_used=6 kv_ev=2 kT_tr=1 kT_ev=1 kv_out=32 q_ev=4 dt_exp=1 sin_arg=1 par_act=1 sc_done=4
            nb_done=4 exp_done=4 p_norm=4 pT_tr=4 pT_ev=4 pv_done=1 pv_ev=1 kb_in0=128 kb_in1=128 kbT_tr=8
            kbT_ev=8 qm_done=1 scs_done=8 nbs_done=1 exps_done=1 ps_norm=1 psT_tr=1 pm_ev=1 pvs_done=8
            oxs_ev=1 oxT_tr=1 ox_done=1 u_ev=4 u_out=16 U_clear=1 U_in=192 val_ev=8 v_done=4 v_last_done=1
            wt_done=2 w_tr=2 wl_ev=2 s_done=2 s_free=2 V_done=2 k_done=2 k_free=2 k_ev=2 k_out=32 m_clear=1
            m_in=256 x_done=2 y_done=2 y_ev=8 y_out=160 y_in=16 sn_done=1 sfin_tr=1 sfin_ev=1 sfin_out=64
            st_in=32 st_tr=1 st_ev=1 vs_tr=2 vs_ev=1 vo_out=48 conv_tile=8 acc_done=8 mean_done=1
            cent_done=4 lsq_done=4 lsq_used=4 lvar_done=1 lrstd_done=1 ln_done=4 ln_silu=4 br_b_done=4
            br_x_done=1 glu_sg=4 br_a_done=4 gate_sg=24 sg_free=32 m_done=8 x_sum=8 z_ev=1 acc_ready0=45
            acc_ready1=45 acc_free0=45 acc_free1=45 d_loaded0=272 d_loaded1=272""".split()
        per = {n: int(k) for n, k in (x.split("=") for x in per)}
        sm.update({n: sem(n) for n in per})
        acc_ready, acc_free, d_loaded = ([sm[f"{n}{i}"] for i in range(2)] for n in ("acc_ready", "acc_free", "d_loaded"))

        def wait(eng, l, name, value):
            eng.wait_ge(sm[name], l * per[name] + value)

        use, n = {}, 0
        for name, k in (("kv", 2), ("q", 4), ("u", 4), ("v", 8), ("zx", 4), ("za", 4), ("zb", 4),
                        ("glu", 4), ("gates", 48), ("out", 8)):
            use[name] = n
            n += k
        unit, n = {}, 0
        for name, k in (("q", 4), ("u", 4), ("v", 8), ("zx", 4), ("za", 4), ("zb", 4), ("gates", 24),
                        ("out", 8)):
            unit[name] = n
            n += k
        assert n == UNITS

        def g3(ap):
            return ap[:, :, :, 0:4 * C]

        block = ctx.enter_context(nc.Block())

        @block.sync
        def _(sp):
            xp = x_prompt[0].rearrange("(c i s) d -> s c i d", s=2, i=4)
            for s in range(2):
                sp.dma_start(xrow[s * C:(s + 1) * C, :, :], xp[s]).then_inc(sm["x_in"], 16)
            sp.dma_start(xsrow[:, :], x_sample[:, 0, :]).then_inc(sm["x_in"], 16)
            sp.dma_start(mrow[:, :, :], mem_prompt[0].rearrange("(m p) d -> p m d", p=P)).then_inc(sm["mem_in"], 16)
            sp.wait_ge(sm["mem_ev"], 2)
            sp.dma_start(m_dram, memn0[:, :, :].rearrange("p k m -> p (k m)")).then_inc(sm["mem_out"], 16)
            sp.wait_ge(sm["mem_out"], 16)

            def ring_load(src, slot, n):
                sp.wait_ge(w_staged_free, n + 1)
                sp.dma_start(w_st[:, slot, :].rearrange("p (k c) -> p k c", c=P), src).then_inc(w_loaded[slot], 16)

            with sp.Fori(0, LAYERS) as l:
                sp.drain().then_inc(layer_left["sp"], 1)
                sp.wait_ge(layer_go, l + 1)
                sp.dma_start(dtrow[64:80, :], ssm_log_dt[l].rearrange("(q e) -> q e", e=2)).then_inc(sm["dt_in"], 16)
                win = w_in[l].rearrange("(k p) c -> p k c", p=P)
                wo = w_out[l].rearrange("(k p) c -> p k c", p=P)

                def section(name, pairs, cols, first=0, src=win):
                    sp.sem_inc(entered["sp"], 1)
                    with sp.Fori(first, first + pairs) as it:
                        for k, col in enumerate(cols):
                            ring_load(src[:, :, bass.ds(col(it), P)], k, l * UNITS + unit[name] + it * 2 + k)

                def straight(c0):
                    return [lambda it, k=k: (it * 2 + k) * P + c0 for k in range(2)]

                section("q", 1, straight(5 * E))
                sp.dma_start(memn[:, :, :].rearrange("p k m -> p (k m)"), m_dram).then_inc(sm["mg_in"], 16)
                rows = ((0, 16, ssm_a_re[l].rearrange("(q e) p -> q (e p)", e=2)),
                        (16, 4, b_glu[l].rearrange("(k p) -> k p", p=P)),
                        (20, 4, conv_b[l].rearrange("(k p) -> k p", p=P)),
                        (24, 4, conv_ln_g[l].rearrange("(k p) -> k p", p=P)),
                        (28, 4, conv_ln_b[l].rearrange("(k p) -> k p", p=P)),
                        (32, 16, ssm_a_im[l].rearrange("(q e) p -> q (e p)", e=2)),
                        (48, 8, norm_g[l].rearrange("(k p) -> k p", p=P)),
                        (56, 8, mem_norm_g[l].rearrange("(k p) -> k p", p=P)),
                        (80, 8, final_norm_g.rearrange("(k p) -> k p", p=P)))
                for r0, n, src in rows:
                    sp.dma_start(prow[r0:r0 + n, :], src).then_inc(sm["p_in"], 16)
                sp.dma_start(cwrow[:, :], conv_w[l].rearrange("k (i c) -> (k i) c", c=P)).then_inc(sm["p_in"], 16)
                sp.dma_start(drow[:, :], ssm_d[l].rearrange("(g h) -> g h", h=H)).then_inc(sm["p_in"], 16)

                def kv_load(i):
                    src = (w_k, w_v)[i // 4][l].rearrange("(k p) c -> p k c", p=P)
                    if i >= 2:
                        if i - 2 == 3:
                            wait(sp, l, "acc_ready0", 1)
                        else:
                            wait(sp, l, "kv_used", i - 1 - (i > 5))
                    sp.dma_start(w_dir[:, i % 2, 0:2 * E].rearrange("p (k c) -> p k c", c=E),
                                 src[:, 2 * (i % 4):2 * (i % 4) + 2, :]).then_inc(d_loaded[i % 2], 16)

                kv_load(0)
                kv_load(1)
                for ri, src in enumerate((ssm_c_re, ssm_c_im)):
                    for half in range(2):
                        for e in range(2):
                            cv = src[l].rearrange("(f q e) h p -> f e q h p", e=2, f=2)[half, e]
                            sp.dma_start(crow[:, ri, half, e * S:(e + 1) * S], cv).then_inc(sm["c_in"], 16)
                for ri, src in enumerate((ssm_b_re, ssm_b_im)):
                    bv = src[l].rearrange("(q e) p h -> e p q h", e=2)
                    for e in range(2):
                        sp.dma_start(bT[e * S:(e + 1) * S, ri, :, :], bv[e]).then_inc(sm["b_in"], 16)
                for ri, src in enumerate((state_ssm_re, state_ssm_im)):
                    sp.dma_start(srow[:, ri, :], src[l].rearrange("b (q e) p -> (b q) (e p)", e=2)).then_inc(sm["s_in"], 16)
                for i in range(2, 8):
                    kv_load(i)
                section("q", 1, straight(5 * E), first=1)
                wait(sp, l, "kv_ev", 2)
                sp.dma_start(mem_k_p[l, 0].rearrange("(m p) h d -> p m (h d)", p=P), ktok[:, :, :]).then_inc(sm["kv_out"], 16)
                sp.dma_start(mem_v_p[l, 0].rearrange("(m p) h d -> p m (h d)", p=P), vtok[:, :, :]).then_inc(sm["kv_out"], 16)
                section("u", 2, straight(0))

                def cache_load(i, cache, b):
                    sp.dma_start(kb[:, b % 2, :, :], cache[l, b].rearrange("(m p) h d -> p m (h d)", p=P)).then_inc(sm[f"kb_in{i % 2}"], 16)

                wait(sp, l, "acc_ready1", 1)
                cache_load(0, cache_mem_k, 0)
                cache_load(1, cache_mem_k, 1)
                v_cols = [lambda it: 3 * E + it * P, lambda it: 2 * E + it * P]
                section("v", 2, v_cols)
                wait(sp, l, "u_ev", 4)
                sp.dma_start(u_dram.rearrange("(i p) a c -> p i (a c)", p=P), u[:, :, :, :].rearrange("p i a c -> p i (a c)")).then_inc(sm["u_out"], 16)
                section("v", 1, v_cols, first=2)
                for b in range(2, NB):
                    wait(sp, l, "kbT_tr", b - 1)
                    cache_load(b, cache_mem_k, b)
                section("v", 1, v_cols, first=3)
                section("zx", 1, straight(6 * E))
                for b in range(NB):
                    if b < 2:
                        wait(sp, l, "kbT_tr", NB - 1 + b)
                    else:
                        wait(sp, l, "pvs_done", b - 1)
                    cache_load(b, cache_mem_v, b)
                wait(sp, l, "u_out", 16)
                wait(sp, l, "U_clear", 1)
                ug = u_dram.rearrange("(g h) a c -> h g a c", h=H)
                Ug = U[:, :, :, :].rearrange("p q e c -> p (q e) c")
                for t in range(T):
                    sp.dma_start(Ug[t * H:(t + 1) * H, :, NB:NB + C], ug[:, :, t // 4, (t % 4) * C:(t % 4 + 1) * C]).then_inc(sm["U_in"], 16)
                for a in range(2):
                    sp.dma_start(Ug[0:H, :, 4 * a:4 * a + 4], ug[:, :, a, 4 * C:HC]).then_inc(sm["U_in"], 16)
                    sp.dma_start(Ug[7 * H:P, :, YC + 4 * a:YC + 4 * a + 4], ug[:, :, a, 4 * C:HC]).then_inc(sm["U_in"], 16)

                def toeplitz(half):
                    wait(sp, l, "k_ev", half + 1)
                    kg = k_dram[half * (G // 2):(half + 1) * (G // 2)].rearrange("g h x -> h g x")
                    sp.dma_start(kg, kt[:, :, :]).then_inc(sm["k_out"], 16)
                    wait(sp, l, "k_out", 16 * (half + 1))
                    if half == 0:
                        wait(sp, l, "m_clear", 1)
                    else:
                        wait(sp, l, "y_done", 1)
                    for s in range(T):
                        sp.dma_start(Mt[s * H:(s + 1) * H, :, s * H:], kg[:, :, 0:(T - s) * H]).then_inc(sm["m_in"], 16)

                toeplitz(0)
                section("zx", 1, straight(6 * E), first=1)
                section("za", 1, straight(E))
                toeplitz(1)
                section("za", 1, straight(E), first=1)
                section("zb", 1, straight(4 * E))
                sp.dma_start(conv_s[l, :, 0:TAPS - 2, :], state_conv[l, :, 1:TAPS - 1, :]).then_inc(sm["vo_out"], 16)
                wait(sp, l, "y_ev", 8)
                yg = y_dram.rearrange("(g h) a c -> h g a c", h=H)
                for t in range(T):
                    sp.dma_start(yg[:, :, t // 4, (t % 4) * C:(t % 4 + 1) * C], Ug[t * H:(t + 1) * H, :, NB:YC]).then_inc(sm["y_out"], 16)
                for a in range(2):
                    sp.dma_start(yg[:, :, a, 4 * C:HC], Ug[0:H, :, 4 * a:4 * a + 4]).then_inc(sm["y_out"], 16)
                wait(sp, l, "y_out", 160)
                sp.dma_start(u[:, :, :, :].rearrange("p i a c -> p i (a c)"), y_dram.rearrange("(i p) a c -> p i (a c)", p=P)).then_inc(sm["y_in"], 16)
                section("zb", 1, straight(4 * E), first=1)
                for r in range(2):
                    sp.dma_start(crw[:, r, :], state_conv[l].rearrange("(r b) k c -> r (b k) c", r=2)[r]).then_inc(sm["st_in"], 16)
                for g in range(2):
                    sp.dma_start(w_dir[:, g, 0:2 * E].rearrange("p (k c) -> p k c", c=2 * P),
                                 w_glu[l].rearrange("(k p) c -> p k c", p=P)[:, :, g * 2 * P:(g + 1) * 2 * P]).then_inc(d_loaded[g], 16)
                branch_w = (w_br_ssm, w_br_conv, w_br_xatt)

                def branch_load(it, jj):
                    wait(sp, l, "acc_ready1", it * 6 + use["gates"] // 2 - 1 + jj)
                    sp.sem_inc(entered["sp"], 1)
                    for x in range(3):
                        sp.dma_start(w_dir[:, jj, x * 4 * P:(x + 1) * 4 * P].rearrange("p (k c) -> p k c", c=P),
                                     branch_w[x][l].rearrange("(k p) c -> p k c", p=P)[:, :, bass.ds((it * 2 + jj) * P, P)]).then_inc(d_loaded[jj], 16)

                def gate_load(it, m):
                    it, m = it + m // 6, m % 6
                    ring_load(win[:, :, bass.ds(7 * E + (m % 3) * D + (it * 2 + m // 3) * P, P)], m % 2,
                              l * UNITS + unit["gates"] + it * 6 + m)

                gate_load(0, 0)
                gate_load(0, 1)
                wait(sp, l, "sfin_ev", 1)
                sp.dma_start(ssm_re_p[l, 0].rearrange("(q e) p -> q (e p)", e=2), so[0:Q, 0, :]).then_inc(sm["sfin_out"], 16)
                sp.dma_start(ssm_im_p[l, 0].rearrange("(q e) p -> q (e p)", e=2), so[0:Q, 1, :]).then_inc(sm["sfin_out"], 16)
                sp.dma_start(ssm_re_s[l].rearrange("b (q e) p -> (b q) (e p)", e=2), so[:, 2, :]).then_inc(sm["sfin_out"], 16)
                sp.dma_start(ssm_im_s[l].rearrange("b (q e) p -> (b q) (e p)", e=2), so[:, 3, :]).then_inc(sm["sfin_out"], 16)
                wait(sp, l, "vs_ev", 1)
                sp.dma_start(conv_p[l, 0], nst[2:32, :]).then_inc(sm["vo_out"], 16)
                sp.dma_start(conv_s[l, :, TAPS - 2, :], nss[:, :]).then_inc(sm["vo_out"], 16)

                with sp.Fori(0, 3) as it:
                    branch_load(it, 0)
                    gate_load(it, 2)
                    gate_load(it, 3)
                    branch_load(it, 1)
                    for m in range(4, 8):
                        gate_load(it, m)
                branch_load(3, 0)
                gate_load(3, 2)
                gate_load(3, 3)
                branch_load(3, 1)
                gate_load(3, 4)
                gate_load(3, 5)
                section("out", 4, straight(0), src=wo)
                wait(sp, l, "kv_out", 32)
                wait(sp, l, "sfin_out", 64)
                wait(sp, l, "vo_out", 48)
                sp.sem_inc(entered["sp"], 1)

            yp = y_prompt[0].rearrange("(c i s) d -> s i c d", s=2, i=4)
            for i in range(4):
                sp.wait_ge(sm["fin_ev"], i + 1)
                for s in range(2):
                    sp.dma_start(yp[s, i], yrow[s * C:(s + 1) * C, i % 2, :]).then_inc(sm[f"fin_out{i}"], 16)
            sp.wait_ge(sm["fin_ev"], 5)
            sp.dma_start(y_sample[:, 0, :], ysr[:, :]).then_inc(sm["fin_out_s"], 16)
            for i in range(4):
                sp.wait_ge(sm[f"fin_out{i}"], 32)
            sp.wait_ge(sm["fin_out_s"], 16)

        @block.gpsimd
        def _(pool):
            pool.memset(ones[:, :], 1.0).then_inc(sm["consts"], 1)
            pool.memset(ident[:, :], 0.0).then_inc(sm["consts"], 1)
            pool.wait_ge(sm["consts"], 2)
            pool.affine_select(out=ident[:, :], in_=ident[:, :], compare_op=ALU.not_equal, fill=1.0, base=0,
                               pattern=[[-1, P]], channel_multiplier=1).then_inc(sm["consts"], 1)
            pool.sem_inc(w_staged_free, 2)

            with pool.Fori(0, LAYERS) as l:
                def low(slot, n):
                    pool.wait_ge(w_hi_done, n + 1)
                    pool.tensor_tensor(w_lo[:, slot, :], w_st[:, slot, :], w_hi[:, slot, :].bitcast(F32),
                                       ALU.subtract).then_inc(w_staged_free, 1)

                def pairs(name, first, count):
                    with pool.Fori(first, first + count) as it:
                        for k in range(2):
                            low(k, l * UNITS + unit[name] + it * 2 + k)

                def glu_v(i):
                    wait(pool, l, "val_ev", 2 * i + 2)
                    for a in range(2):
                        blk = vx[:, bass.ds(i, 1), 8 + 4 * a:12 + 4 * a, 4:4 + C].rearrange("p i b c -> p (i b) c")
                        pool.tensor_tensor(blk, blk, sg[:, i % 2, a, 0:4 * C].rearrange("p (b c) -> p b c", c=C), ALU.mult)
                    s = v_s[:, i, :].rearrange("p (a c) -> p a c", a=2)
                    pool.tensor_tensor(s, s, sg[:, i % 2, :, 4 * C:HC], ALU.mult).then_inc(sm["v_done"], 1)
                    wait(pool, l, "v_done", i + 1)
                    pool.sem_inc(sm["sg_free"], 1)

                pairs("q", 0, 2)
                pairs("u", 0, 2)
                pairs("v", 0, 1)
                for i in range(3):
                    pairs("v", i + 1, 1)
                    glu_v(i)
                pairs("zx", 0, 1)
                glu_v(3)
                pairs("zx", 1, 1)
                pairs("za", 0, 2)
                pairs("zb", 0, 2)
                pairs("gates", 0, 12)
                pairs("out", 0, 4)

        @block.tensor
        def _(pe):
            def transpose(out, in_, n):
                return pe.transpose(out, in_, ident[0:n, 0:n])

            pe.wait_ge(sm["consts"], 3)
            pe.wait_ge(sm["x_in"], 48)
            for i in range(4):
                if i >= 2:
                    pe.wait_ge(sm["x_ev"], i - 1)
                for k in range(KT):
                    last = transpose(mp[:, 2 * (i % 2) + k // 4, (k % 4) * P:(k % 4 + 1) * P], xrow[:, i, k * P:(k + 1) * P], P)
                last.then_inc(sm["x_tr"], 1)
            pe.wait_ge(sm["x_ev"], 3)
            for k in range(KT):
                last = transpose(mp[:, 0, k * NB:(k + 1) * NB], xsrow[:, k * P:(k + 1) * P], NB)
            last.then_inc(sm["x_tr"], 1)
            pe.wait_ge(sm["mem_nrm"], 2)
            for m in range(2):
                if m == 0:
                    pe.wait_ge(sm["x_ev"], 4)
                else:
                    pe.wait_ge(sm["x_ev"], 5)
                for k in range(KT):
                    last = transpose(mp[:, 2 * (1 - m) + k // 4, (k % 4) * P:(k % 4 + 1) * P], mrow[:, m, k * P:(k + 1) * P], P)
                last.then_inc(sm["mem_tr"], 1)
            pe.wait_ge(sm["mem_ev"], 2)

            with pe.Fori(0, LAYERS) as l:
                pe.drain().then_inc(layer_left["pe"], 1)
                pe.wait_ge(layer_go, l + 1)

                def split_product(pair, use_n, slot, n, hi, lo):
                    pe.wait_ge(w_staged_free, n + 3)
                    wait(pe, l, f"acc_free{pair}", use_n + 1)
                    for k in range(KT):
                        for p, (w, x) in enumerate(((w_hi, hi), (w_lo, hi), (w_hi, lo))):
                            for a in range(2):
                                last = pe.matmul(acc_ps[pair][:, a, 0:HC], w[:, slot, k * P:(k + 1) * P], x[:, k, a, :],
                                                 start=(k == 0 and p == 0), stop=(k == KT - 1 and p == 2))
                    last.then_inc(acc_ready[pair], 1)

                def in_section(name, first, pairs):
                    pe.sem_inc(entered["pe"], 1)
                    with pe.Fori(first, first + pairs) as it:
                        for k in range(2):
                            split_product(k, it + use[name] // 2, k, l * UNITS + unit[name] + it * 2 + k, h_hi, h_lo)

                for k in range(KT):
                    wait(pe, l, "sq_done", k + 1)
                    for a in range(2):
                        last = pe.matmul(mp[:, a, 0:HC], ones[:, :], sq[:, k % 4, a, :], start=(k == 0), stop=(k == KT - 1))
                    last.then_inc(sm["sq_used"], 1)
                wait(pe, l, "dt_wide", 1)
                wait(pe, l, "p_in", 16 * 11)
                wait(pe, l, "c_in", 16 * 8)
                transpose(mp[:, 2, 0:88], prow[:, :], 88)
                transpose(mp[:, 2, P:P + TAPS * ET], cwrow[:, :], TAPS * ET)
                transpose(mp[0:H, 2, 256:256 + G], drow[:, :], G)
                for ri in range(2):
                    for f in range(2):
                        last = transpose(mp[:, 3, (2 * ri + f) * P:(2 * ri + f + 1) * P], crow[:, ri, f, :], P)
                last.then_inc(sm["par_tr"], 1)
                wait(pe, l, "var_done", 1)
                wait(pe, l, "s_in", 32)
                for ri in range(2):
                    last = transpose(mp[:, 0, ri * P:(ri + 1) * P], srow[:, ri, :], P)
                last.then_inc(sm["s0_tr"], 1)
                wait(pe, l, "memg_done", 1)
                for i in range(8):
                    wait(pe, l, f"d_loaded{i % 2}", 16 * (i // 2 + 1))
                    if i % 4 == 0:
                        wait(pe, l, f"acc_free{i // 4}", 1)
                    for kk in range(2):
                        k = 2 * (i % 4) + kk
                        for m in range(2):
                            last = pe.matmul(acc_ps[i // 4][:, m, :], memg[:, k, m * P:(m + 1) * P],
                                             w_dir[:, i % 2, kk * E:(kk + 1) * E], start=(k == 0), stop=(k == KT - 1))
                    if i % 4 == 3:
                        last.then_inc(acc_ready[i // 4], 1)
                    else:
                        last.then_inc(sm["kv_used"], 1)
                wait(pe, l, "kv_ev", 1)
                wait(pe, l, "par_ev", 1)
                for hd in range(HEADS):
                    for m in range(2):
                        j = 2 * hd + m
                        last = transpose(mp[:, 2 + j // 4, (j % 4) * P:(j % 4 + 1) * P], ktok[:, m, hd * P:(hd + 1) * P], P)
                last.then_inc(sm["kT_tr"], 1)
                wait(pe, l, "h_done", 1)
                in_section("q", 0, 2)

                def scores(i):
                    if i < 2:
                        wait(pe, l, "q_ev", 4)
                        wait(pe, l, "kT_ev", 1)
                        wait(pe, l, "s0_ev", 1)
                    else:
                        wait(pe, l, "pT_ev", i - 1)
                    for hd in range(HEADS):
                        last = pe.matmul(mp[:, 2 * (i % 2) + hd // 2, (hd % 2) * MEM:(hd % 2 + 1) * MEM],
                                         q[:, hd, i // 2, (i % 2) * P:(i % 2 + 1) * P], kT[:, hd, :], start=True, stop=True)
                    last.then_inc(sm["sc_done"], 1)

                def turn_probabilities(i):
                    wait(pe, l, "p_norm", i + 1)
                    for hd in range(HEADS):
                        for m in range(2):
                            j = 2 * hd + m
                            last = transpose(mp[:, 2 * (i % 2) + j // 4, (j % 4) * P:(j % 4 + 1) * P],
                                             pr[:, i % 2, hd, m * P:(m + 1) * P], P)
                    last.then_inc(sm["pT_tr"], 1)

                scores(0)
                scores(1)
                in_section("u", 0, 2)
                turn_probabilities(0)
                turn_probabilities(1)
                scores(2)
                scores(3)
                in_section("v", 0, 2)
                turn_probabilities(2)
                turn_probabilities(3)
                for hd in range(HEADS):
                    wait(pe, l, "pT_ev", 3 if hd < 2 else 4)
                    if hd == 0:
                        wait(pe, l, "pT_ev", 4)
                    for m in range(2):
                        last = pe.matmul(mp[:, hd, :], vtok[:, m, hd * P:(hd + 1) * P], pT[:, hd, m, :], start=(m == 0), stop=(m == 1))
                last.then_inc(sm["pv_done"], 1)

                wait(pe, l, "pv_ev", 1)
                wait(pe, l, "qm_done", 1)
                for b in range(NB):
                    wait(pe, l, f"kb_in{b % 2}", 16 * (b // 2 + 1))
                    if b:
                        wait(pe, l, "kbT_ev", b)
                    for hd in range(HEADS):
                        for m in range(2):
                            j = 2 * hd + m
                            last = transpose(mp[:, j // 4, (j % 4) * P:(j % 4 + 1) * P], kb[:, b % 2, m, hd * P:(hd + 1) * P], P)
                    last.then_inc(sm["kbT_tr"], 1)
                    wait(pe, l, "kbT_ev", b + 1)
                    for hd in range(HEADS):
                        last = pe.matmul(mp[0:32, 2, 0:MEM], qm[:, b * HEADS + hd, :], kbT[:, hd, :],
                                         start=(b == 0 and hd == 0), stop=(b == NB - 1 and hd == HEADS - 1))
                    last.then_inc(sm["scs_done"], 1)
                in_section("v", 2, 2)
                wait(pe, l, "ps_norm", 1)
                pe.sem_inc(entered["pe"], 1)
                for m in range(2):
                    last = transpose(mp[:, 3, m * 32:(m + 1) * 32], ps[:, m * P:(m + 1) * P], 32)
                last.then_inc(sm["psT_tr"], 1)
                wait(pe, l, "pm_ev", 1)
                for b in range(NB):
                    wait(pe, l, f"kb_in{b % 2}", 16 * (NB // 2 + b // 2 + 1))
                    for m in range(2):
                        last = pe.matmul(mp[0:32, 2, :], pm[:, m, b, :], kb[:, b % 2, m, :],
                                         start=(b == 0 and m == 0), stop=(b == NB - 1 and m == 1))
                    last.then_inc(sm["pvs_done"], 1)
                wait(pe, l, "oxs_ev", 1)
                pe.sem_inc(entered["pe"], 1)
                for hd in range(HEADS):
                    last = transpose(mp[:, 3, hd * 32:(hd + 1) * 32], oxs[:, hd * P:(hd + 1) * P], 32)
                last.then_inc(sm["oxT_tr"], 1)

                def state_inputs(f):
                    wait(pe, l, "wt_done", f + 1)
                    if f == 0:
                        wait(pe, l, "ox_done", 1)
                    else:
                        wait(pe, l, "y_ev", 4)
                    for ri in range(2):
                        for r in range(QH):
                            j = ri * QH + r
                            last = transpose(mp[:, j // 4, (j % 4) * P:(j % 4 + 1) * P], wt[:, ri, r, :], P)
                    last.then_inc(sm["w_tr"], 1)
                    wait(pe, l, "wl_ev", f + 1)
                    wait(pe, l, "U_in", 16 * 12)
                    for e in range(2):
                        for ri in range(2):
                            for r in range(QH):
                                last = pe.matmul(mp[e * S:(e + 1) * S, 2 * ri + r // 4, (r % 4) * YC:(r % 4 + 1) * YC],
                                                 wl[:, ri, r, e * S:(e + 1) * S], U[:, f * QH + r, e, NB:UC], start=True, stop=True)
                    last.then_inc(sm["s_done"], 1)

                def lag_matrices(f):
                    wait(pe, l, "V_done", f + 1)
                    wait(pe, l, "s_free", f + 1)
                    pe.sem_inc(entered["pe"], 1)
                    for e in range(2):
                        for r in range(QH):
                            for ri in range(2):
                                last = pe.matmul(mp[0:H, 2 * e + r // 4, (r % 4) * P:(r % 4 + 1) * P],
                                                 bb[e * S:(e + 1) * S, ri, f * QH + r, :],
                                                 V[e * S:(e + 1) * S, ri, r, 0:T, :].rearrange("p t h -> p (t h)"),
                                                 start=(ri == 0), stop=(ri == 1))
                    last.then_inc(sm["k_done"], 1)

                def outputs(f):
                    wait(pe, l, "m_in", 128 * (f + 1))
                    wait(pe, l, "x_done", f + 1)
                    wait(pe, l, "k_free", f + 1)
                    for e in range(2):
                        for r in range(QH):
                            out = mp[:, 2 * e + r // 4, (r % 4) * YC:(r % 4 + 1) * YC]
                            pe.matmul(out, Mt[:, 2 * r + e, :], U[:, f * QH + r, e, 0:YC], start=True, stop=False)
                            for ri in range(2):
                                last = pe.matmul(out, V[e * S:(e + 1) * S, ri, r, 1:T + 1, :].rearrange("p t h -> p (t h)"),
                                                 X[e * S:(e + 1) * S, ri, r, 0:YC], start=False, stop=(ri == 1))
                    last.then_inc(sm["y_done"], 1)

                state_inputs(0)
                lag_matrices(0)
                in_section("zx", 0, 2)
                outputs(0)
                state_inputs(1)
                lag_matrices(1)
                in_section("za", 0, 2)
                outputs(1)
                in_section("zb", 0, 2)

                wait(pe, l, "y_ev", 8)
                wait(pe, l, "sn_done", 1)
                for ri in range(2):
                    transpose(mp[0:Q, 0, ri * P:(ri + 1) * P], sf[:, ri, :], P)
                for ri in range(2):
                    last = transpose(mp[:, 0, (2 + ri) * P:(3 + ri) * P], sn[:, ri, :, :].rearrange("p b q -> p (b q)"), P)
                last.then_inc(sm["sfin_tr"], 1)
                wait(pe, l, "st_in", 32)
                for r in range(2):
                    for i in range(ET):
                        last = transpose(mp[:, 1 + r, i * 120:(i + 1) * 120], crw[:, r, i * P:(i + 1) * P], 120)
                last.then_inc(sm["st_tr"], 1)
                wait(pe, l, "v_last_done", 1)
                for i in range(ET):
                    last = transpose(mp[0:32, 3, i * P:(i + 1) * P], v_last[:, i, :], P)
                last.then_inc(sm["vs_tr"], 1)
                wait(pe, l, "sfin_ev", 1)
                for i in range(ET):
                    last = transpose(mp[0:NB, 0, i * P:(i + 1) * P], v_s[:, i, :], P)
                last.then_inc(sm["vs_tr"], 1)

                wait(pe, l, "y_in", 16)
                for g in range(2):
                    wait(pe, l, f"d_loaded{g}", 80)
                    for j in range(2):
                        wait(pe, l, f"acc_free{j}", use["glu"] // 2 + g + 1)
                        for k in range(ET):
                            for a in range(2):
                                last = pe.matmul(acc_ps[j][:, a, 0:HC], w_dir[:, g, k * 2 * P + j * P:k * 2 * P + (j + 1) * P],
                                                 u[:, k, a, :], start=(k == 0), stop=(k == ET - 1))
                        last.then_inc(acc_ready[j], 1)
                wait(pe, l, "acc_done", 2 * ET)
                wait(pe, l, "st_ev", 1)
                wait(pe, l, "vs_ev", 1)
                for i in range(ET):
                    for a in range(2):
                        last = pe.matmul(mp[:, a, 0:HC], ones[:, :], acc[:, i, a, :], start=(i == 0), stop=(i == ET - 1))
                last.then_inc(sm["mean_done"], 1)
                for i in range(ET):
                    wait(pe, l, "lsq_done", i + 1)
                    for a in range(2):
                        last = pe.matmul(mp[:, 2 + a, 0:HC], ones[:, :], lsq[:, i % 2, a, :], start=(i == 0), stop=(i == ET - 1))
                    last.then_inc(sm["lsq_used"], 1)

                wait(pe, l, "br_a_done", 4)
                wait(pe, l, "br_b_done", 4)
                wait(pe, l, "br_x_done", 1)
                pe.sem_inc(entered["pe"], 1)
                with pe.Fori(0, 4) as it:
                    for jj in range(2):
                        for x in range(3):
                            m = jj * 3 + x
                            un = it * 6 + use["gates"] // 2 + m
                            split_product(0, un, m % 2, l * UNITS + unit["gates"] + it * 6 + m, h_hi, h_lo)
                            if x == 0:
                                wait(pe, l, f"d_loaded{jj}", it * 48 + 80 + 48)
                            wait(pe, l, "acc_free1", un + 1)
                            for k in range(ET):
                                for a in range(2):
                                    last = pe.matmul(acc_ps[1][:, a, 0:HC], w_dir[:, jj, (x * 4 + k) * P:(x * 4 + k + 1) * P],
                                                     br[:, x, k, a, :], start=(k == 0), stop=(k == ET - 1))
                            last.then_inc(acc_ready[1], 1)
                wait(pe, l, "m_done", 8)
                pe.sem_inc(entered["pe"], 1)
                with pe.Fori(0, 4) as it:
                    for k in range(2):
                        split_product(k, it + use["out"] // 2, k, l * UNITS + unit["out"] + it * 2 + k, m_hi, m_lo)

            for k in range(KT):
                pe.wait_ge(sm["fin_sq"], k + 1)
                for a in range(2):
                    last = pe.matmul(mp[:, a, 0:HC], ones[:, :], sq[:, k % 4, a, :], start=(k == 0), stop=(k == KT - 1))
                last.then_inc(sm["fin_used"], 1)
            pe.wait_ge(sm["fin_y"], KT + 1)
            for i in range(4):
                if i < 2:
                    pe.wait_ge(sm["fin_var"], 1)
                else:
                    pe.wait_ge(sm["fin_ev"], i - 1)
                for k in range(KT):
                    last = transpose(mp[:, 2 * (i % 2) + k // 4, (k % 4) * P:(k % 4 + 1) * P],
                                     xT[:, k, i // 2, (i % 2) * P:(i % 2 + 1) * P], P)
                last.then_inc(sm["fin_tr"], 1)
            pe.wait_ge(sm["fin_ev"], 3)
            for k in range(KT):
                last = transpose(mp[0:NB, k // 4, (k % 4) * P:(k % 4 + 1) * P], xsc[:, k, :], P)
            last.then_inc(sm["fin_tr"], 1)

        @block.scalar
        def _(act):
            steps = Steps(act, act_steps)
            act.wait_ge(sm["mem_in"], 16)
            for m in range(2):
                steps.run(act.activation(memn0[:, 0:4, :].rearrange("p k m -> p (k m)"), mrow[:, m, :], ACT.Square,
                                         accum_out=stat[:, m:m + 1]))
            act.sem_inc(sm["mem_sq"], 1)
            act.wait_ge(sm["mem_var"], 1)
            act.activation(stat[:, 2:4], stat[:, 4:6], ACT.Sqrt).then_inc(sm["mem_rt"], 1)
            for i in range(4):
                act.wait_ge(sm["x_tr"], i + 1)
                act.activation(xT[:, :, i // 2, (i % 2) * P:(i % 2 + 1) * P],
                               mp[:, 2 * (i % 2):2 * (i % 2) + 2, :].rearrange("p b (k c) -> p (b k) c", c=P), ACT.Copy).then_inc(sm["x_ev"], 1)
            act.wait_ge(sm["x_tr"], 5)
            act.activation(xT[:, :, :, 4 * C:HC], mp[:, 0, 0:KT * NB].rearrange("p (k a c) -> p k a c", a=2, c=4), ACT.Copy).then_inc(sm["x_ev"], 1)
            for m in range(2):
                act.wait_ge(sm["mem_tr"], m + 1)
                act.activation(memn0[:, :, m * P:(m + 1) * P],
                               mp[:, 2 * (1 - m):2 * (1 - m) + 2, :].rearrange("p b (k c) -> p (b k) c", c=P), ACT.Copy).then_inc(sm["mem_ev"], 1)
            act.wait_ge(sm["mem_ev"], 2)
            steps.clear()

            with act.Fori(0, LAYERS) as l:
                act.drain().then_inc(layer_left["act"], 1)
                act.wait_ge(layer_go, l + 1)

                def high(slot, loads):
                    act.wait_ge(w_loaded[slot], loads * 16)
                    act.copy(w_hi[:, slot, :], w_st[:, slot, :]).then_inc(w_hi_done, 1)

                def section(name, first, pairs, evac, bump=None):
                    with act.Fori(first, first + pairs) as it:
                        for k in range(2):
                            wait(act, l, f"acc_ready{k}", it + use[name] // 2 + 1)
                            high(k, l * (UNITS // 2) + unit[name] // 2 + it + 2)
                            evac(it, k)

                high(0, l * (UNITS // 2) + 1)
                high(1, l * (UNITS // 2) + 1)
                for k in range(KT):
                    if k >= 4:
                        wait(act, l, "sq_used", k - 3)
                    act.activation(sq[:, k % 4, :, :], xT[:, k, :, :], ACT.Square).then_inc(sm["sq_done"], 1)
                wait(act, l, "var_done", 1)
                act.activation(rs[:, :, :], rs[:, :, :], ACT.Sqrt).then_inc(sm["rstd_done"], 1)
                for k in range(KT):
                    wait(act, l, "ht_done", k + 1)
                    act.copy(h_hi[:, k, :, :], ht[:, k % 2, :, :]).then_inc(sm["hhi_done"], 1)
                wait(act, l, "par_ev", 1)
                act.activation(tiny[:, 0, :], vec[:, 64:80], ACT.Exp).then_inc(sm["dt_exp"], 1)
                wait(act, l, "sin_arg", 1)
                act.activation(tiny[:, 3, :], tiny[:, 1, :], ACT.Exp)
                act.activation(tiny[:, 7:9, :], tiny[:, 5:7, :], ACT.Sin).then_inc(sm["par_act"], 1)
                wait(act, l, "acc_ready0", 1)
                act.copy(ktok[:, :, :], acc_ps[0][:, :, :]).then_inc(sm["kv_ev"], 1)
                wait(act, l, "kv_ev", 1)
                act.sem_inc(acc_free[0], 1)
                wait(act, l, "acc_ready1", 1)
                act.copy(vtok[:, :, :], acc_ps[1][:, :, :]).then_inc(sm["kv_ev"], 1)
                wait(act, l, "kv_ev", 2)
                act.sem_inc(acc_free[1], 1)
                wait(act, l, "kT_tr", 1)
                act.copy(kT[:, :, :].rearrange("p h m -> p (h m)"), mp[:, 2:4, :].rearrange("p b c -> p (b c)")).then_inc(sm["kT_ev"], 1)

                def tile(ap, i):
                    return ap[:, bass.ds(i, 1), :, :].rearrange("p i a c -> p (i a) c")

                def to_q(it, k):
                    act.copy(tile(q, it * 2 + k), acc_ps[k][:, :, 0:HC]).then_inc(acc_free[k], 1)

                section("q", 0, 2, to_q)
                wait(act, l, "acc_free1", use["u"] // 2 + 1)
                act.sem_inc(sm["q_ev"], 4)

                def exps(i):
                    wait(act, l, "nb_done", i + 1)
                    if i >= 2:
                        wait(act, l, "pT_tr", i - 1)
                    for hd in range(HEADS):
                        last = act.activation(pr[:, i % 2, hd, :], mp[:, 2 * (i % 2) + hd // 2, (hd % 2) * MEM:(hd % 2 + 1) * MEM],
                                              ACT.Exp, bias=stat[:, 16 + 4 * i + hd:17 + 4 * i + hd], scale=SCALE,
                                              accum_out=stat[:, 32 + 4 * i + hd:33 + 4 * i + hd])
                    last.then_inc(sm["exp_done"], 1)

                def keep_probabilities(i):
                    wait(act, l, "pT_tr", i + 1)
                    act.copy(pT[:, :, :, i * P:(i + 1) * P],
                             mp[:, 2 * (i % 2):2 * (i % 2) + 2, :].rearrange("p b (n c) -> p (b n) c", c=P)
                             .rearrange("p (h m) c -> p h m c", m=2)).then_inc(sm["pT_ev"], 1)

                exps(0)
                exps(1)
                wait(act, l, "s0_ev", 1)
                wait(act, l, "par_ev", 1)

                def to_u(it, k):
                    act.copy(tile(u, it * 2 + k), acc_ps[k][:, :, 0:HC]).then_inc(acc_free[k], 1)

                section("u", 0, 2, to_u)
                wait(act, l, "acc_free1", use["v"] // 2 + 1)
                act.sem_inc(sm["u_ev"], 4)
                keep_probabilities(0)
                keep_probabilities(1)
                exps(2)
                exps(3)

                def to_v(i):
                    base = l * (UNITS // 2) + unit["v"] // 2 + i + 2
                    wait(act, l, "acc_ready0", use["v"] // 2 + i + 1)
                    high(0, base)
                    wait(act, l, "sg_free", i + 1)
                    act.activation(sg[:, i % 2, :, :], acc_ps[0][:, :, 0:HC], ACT.Sigmoid).then_inc(sm["val_ev"], 1)
                    wait(act, l, "val_ev", 2 * i + 1)
                    act.sem_inc(acc_free[0], 1)
                    wait(act, l, "acc_ready1", use["v"] // 2 + i + 1)
                    high(1, base)
                    for a in range(2):
                        act.copy(vx[:, i, 8 + 4 * a:12 + 4 * a, 4:4 + C], acc_ps[1][:, a, 0:4 * C].rearrange("p (b c) -> p b c", c=C))
                    act.copy(v_s[:, i, :].rearrange("p (a c) -> p a c", a=2), acc_ps[1][:, :, 4 * C:HC]).then_inc(sm["val_ev"], 1)
                    wait(act, l, "val_ev", 2 * i + 2)
                    act.sem_inc(acc_free[1], 1)

                to_v(0)
                to_v(1)
                keep_probabilities(2)
                keep_probabilities(3)
                wait(act, l, "pv_done", 1)
                act.copy(g3(q), mp[:, :, :].rearrange("p h (a c) -> p h a c", a=2)).then_inc(sm["pv_ev"], 1)
                for b in range(NB):
                    wait(act, l, "kbT_tr", b + 1)
                    if b:
                        wait(act, l, "scs_done", b)
                    act.copy(kbT[:, :, :].rearrange("p h m -> p (h m)"), mp[:, 0:2, :].rearrange("p b c -> p (b c)")).then_inc(sm["kbT_ev"], 1)
                to_v(2)
                to_v(3)
                wait(act, l, "nbs_done", 1)
                act.activation(ps[:, :], mp[0:32, 2, 0:MEM], ACT.Exp, bias=stat[0:32, 48:49], scale=SCALE,
                               accum_out=stat[0:32, 49:50]).then_inc(sm["exps_done"], 1)
                wait(act, l, "pvs_done", NB)
                act.copy(oxs[:, :], mp[0:32, 2, :]).then_inc(sm["oxs_ev"], 1)

                def turned_inputs(f):
                    wait(act, l, "w_tr", f + 1)
                    act.copy(wl[:, :, :, :].rearrange("p a q s -> p (a q s)"), mp[:, :, :].rearrange("p b c -> p (b c)")).then_inc(sm["wl_ev"], 1)

                def gelu_outputs(f):
                    wait(act, l, "y_done", f + 1)
                    for e in range(2):
                        for b in range(2):
                            act.activation(U[:, f * QH + 4 * b:f * QH + 4 * b + 4, e, 0:YC],
                                           mp[:, 2 * e + b, 0:4 * YC].rearrange("p (q c) -> p q c", c=YC),
                                           ACT.Gelu_apprx_tanh).then_inc(sm["y_ev"], 1)

                def to_z(x):
                    def evac(it, k):
                        act.activation(tile(z[:, x, :, :, :], it * 2 + k), acc_ps[k][:, :, 0:HC], ACT.Silu).then_inc(acc_free[k], 1)
                    return evac

                turned_inputs(0)
                section("zx", 0, 2, to_z(2))
                gelu_outputs(0)
                turned_inputs(1)
                wait(act, l, "k_out", 32)
                wait(act, l, "k_free", 2)
                section("za", 0, 2, to_z(0))
                gelu_outputs(1)
                section("zb", 0, 2, to_z(1))
                wait(act, l, "acc_free1", use["glu"] // 2 + 1)
                act.sem_inc(sm["z_ev"], 1)

                for i in range(ET):
                    wait(act, l, "conv_tile", 2 * i + 1)
                    act.activation(g3(acc)[:, i], cacc[:, i % 2, :, :].rearrange("p (a b) c -> p a (b c)", a=2), ACT.Identity,
                                   bias=vec[:, 20 + i:21 + i]).then_inc(sm["acc_done"], 1)
                    wait(act, l, "conv_tile", 2 * i + 2)
                    act.activation(acc[:, i, :, 4 * C:HC], v_s[:, i, :].rearrange("p (a c) -> p a c", a=2), ACT.Identity,
                                   bias=vec[:, 20 + i:21 + i]).then_inc(sm["acc_done"], 1)
                for i in range(ET):
                    wait(act, l, f"acc_ready{i % 2}", use["glu"] // 2 + i // 2 + 1)
                    wait(act, l, "sg_free", 4 + i + 1)
                    act.activation(sg[:, i % 2, :, :], acc_ps[i % 2][:, :, 0:HC], ACT.Sigmoid,
                                   bias=vec[:, 16 + i:17 + i]).then_inc(sm["glu_sg"], 1)
                    wait(act, l, "glu_sg", i + 1)
                    act.sem_inc(acc_free[i % 2], 1)
                for i in range(ET):
                    wait(act, l, "cent_done", i + 1)
                    if i >= 2:
                        wait(act, l, "lsq_used", i - 1)
                    act.activation(lsq[:, i % 2, :, :], acc[:, i, :, :], ACT.Square).then_inc(sm["lsq_done"], 1)
                wait(act, l, "lvar_done", 1)
                act.activation(lst[:, :, :], lst[:, :, :], ACT.Sqrt).then_inc(sm["lrstd_done"], 1)
                for i in range(ET):
                    wait(act, l, "ln_done", i + 1)
                    act.activation(acc[:, i, :, :], acc[:, i, :, :], ACT.Silu, bias=vec[:, 28 + i:29 + i]).then_inc(sm["ln_silu"], 1)
                with act.Fori(0, 4) as it:
                    for m in range(6):
                        wait(act, l, "acc_ready0", it * 6 + use["gates"] // 2 + m + 1)
                        high(m % 2, l * (UNITS // 2) + unit["gates"] // 2 + it * 3 + m // 2 + 2)
                        wait(act, l, "sg_free", it * 6 + 8 + m + 1)
                        act.activation(sg[:, m % 2, :, :], acc_ps[0][:, :, 0:HC], ACT.Sigmoid).then_inc(sm["gate_sg"], 1)
                        wait(act, l, "gate_sg", it * 6 + m + 1)
                        act.sem_inc(acc_free[0], 1)
                with act.Fori(0, 3) as it:
                    for k in range(2):
                        wait(act, l, f"acc_ready{k}", it + use["out"] // 2 + 1)
                        high(k, l * (UNITS // 2) + unit["out"] // 2 + it + 2)

            act.wait_ge(sm["x_sum"], 8 * LAYERS)
            for k in range(KT):
                if k >= 4:
                    act.wait_ge(sm["fin_used"], k - 3)
                act.activation(sq[:, k % 4, :, :], xT[:, k, :, :], ACT.Square).then_inc(sm["fin_sq"], 1)
            act.wait_ge(sm["fin_var"], 1)
            act.activation(rs[:, :, :], rs[:, :, :], ACT.Sqrt).then_inc(sm["fin_rt"], 1)
            for i in range(4):
                act.wait_ge(sm["fin_tr"], i + 1)
                if i >= 2:
                    act.wait_ge(sm[f"fin_out{i - 2}"], 32)
                act.copy(yrow[:, i % 2, :], mp[:, 2 * (i % 2):2 * (i % 2) + 2, :].rearrange("p b c -> p (b c)")).then_inc(sm["fin_ev"], 1)
            act.wait_ge(sm["fin_tr"], 5)
            act.copy(ysr[:, :], mp[0:NB, 0:2, :].rearrange("p b c -> p (b c)")).then_inc(sm["fin_ev"], 1)

        @block.vector
        def _(dve):
            steps = Steps(dve, dve_steps)
            run = steps.run

            def tt(out, a, b, op):
                run(dve.tensor_tensor(out, a, b, op))

            def ts(out, a, s1, s2, op0, op1):
                run(dve.tensor_scalar(out, a, s1, s2, op0, op1))

            def stt(out, a, s, b, op0, op1):
                run(dve.scalar_tensor_tensor(out=out, in0=a, scalar=s, in1=b, op0=op0, op1=op1))

            def cmul(dr, di, xr, xi, yr, yi, a, b):
                tt(a, xr, yr, ALU.mult)
                tt(b, xi, yi, ALU.mult)
                tt(b, a, b, ALU.subtract)
                tt(a, xr, yi, ALU.mult)
                tt(di, xi, yr, ALU.mult)
                tt(di, a, di, ALU.add)
                run(dve.tensor_copy(dr, b))

            dve.wait_ge(sm["mem_sq"], 1)
            ts(stat[:, 6:8], stat[:, 0:2], 1.0 / D, EPS, ALU.mult, ALU.add)
            dve.reciprocal(stat[:, 4:6], stat[:, 6:8]).then_inc(sm["mem_var"], 1)
            dve.wait_ge(sm["mem_rt"], 1)
            for m in range(2):
                dve.tensor_scalar(mrow[:, m, :], mrow[:, m, :], stat[:, 2 + m:3 + m], None, ALU.mult).then_inc(sm["mem_nrm"], 1)
            dve.wait_ge(sm["mem_nrm"], 2)
            steps.clear()

            for i in range(2):
                dve.sem_inc(acc_free[i], 1)
            dve.sem_inc(sm["sg_free"], 2)

            with dve.Fori(0, LAYERS) as l:
                for e in layer_left:
                    dve.wait_ge(layer_left[e], l + 1)
                    dve.sem_inc(layers_begun, 1)
                dve.sem_inc(layer_go, 1)

                wait(dve, l, "dt_in", 16)
                dve.tensor_copy(prow[64:80, :].rearrange("q (e p) -> q e p", e=2),
                                dtrow[64:80, :].unsqueeze(2).to_broadcast([16, 2, S])).then_inc(sm["dt_wide"], 1)
                wait(dve, l, "sq_used", KT)
                ts(rs[:, :, :], mp[:, 0:2, 0:HC], 1.0 / D, EPS, ALU.mult, ALU.add)
                dve.reciprocal(rs[:, :, :], rs[:, :, :]).then_inc(sm["var_done"], 1)
                wait(dve, l, "par_tr", 1)
                run(dve.tensor_copy(vec[:, :], mp[:, 2, 0:88]))
                run(dve.tensor_copy(cw[:, :], mp[:, 2, P:P + TAPS * ET]))
                run(dve.tensor_copy(dcol[:, :], mp[0:H, 2, 256:256 + G]))
                dve.tensor_copy(cT[:, :, :, :].rearrange("p a q h -> p (a q h)"), mp[:, 3, :]).then_inc(sm["par_ev"], 1)
                wait(dve, l, "par_ev", 1)
                wait(dve, l, "mg_in", 16)
                for k in range(KT):
                    run(dve.tensor_scalar(memg[:, k, :], memn[:, k, :], vec[:, 56 + k:57 + k], None, ALU.mult))
                dve.sem_inc(sm["memg_done"], 1)
                wait(dve, l, "rstd_done", 1)

                def h_low(k):
                    wait(dve, l, "hhi_done", k + 1)
                    run(dve.tensor_tensor(h_lo[:, k, :, :], ht[:, k % 2, :, :], h_hi[:, k, :, :].bitcast(F32), ALU.subtract))

                for k in range(KT):
                    if k >= 2:
                        h_low(k - 2)
                    stt(ht[:, k % 2, :, :], xT[:, k, :, :], vec[:, 48 + k:49 + k], rs[:, :, :], ALU.mult, ALU.mult)
                    dve.sem_inc(sm["ht_done"], 1)
                h_low(KT - 2)
                h_low(KT - 1)
                dve.sem_inc(sm["h_done"], 1)
                wait(dve, l, "s0_tr", 1)
                dve.tensor_copy(s0[:, :, :, :].rearrange("p a b q -> p (a b q)"), mp[:, 0, 0:2 * P]).then_inc(sm["s0_ev"], 1)
                wait(dve, l, "s0_ev", 1)

                are, aim = vec[:, 0:16], vec[:, 32:48]
                wait(dve, l, "dt_exp", 1)
                tt(tiny[:, 1, :], are, tiny[:, 0, :], ALU.mult)
                tt(tiny[:, 2, :], aim, tiny[:, 0, :], ALU.mult)
                ts(tiny[:, 4, :], tiny[:, 2, :], 1.0 / TWO_PI, ROUND, ALU.mult, ALU.add)
                run(dve.tensor_scalar(tiny[:, 4, :], tiny[:, 4, :], ROUND, None, ALU.subtract))
                stt(tiny[:, 5, :], tiny[:, 4, :], -PI2_HI, tiny[:, 2, :], ALU.mult, ALU.add)
                stt(tiny[:, 5, :], tiny[:, 4, :], -PI2_MID, tiny[:, 5, :], ALU.mult, ALU.add)
                stt(tiny[:, 5, :], tiny[:, 4, :], -PI2_LO, tiny[:, 5, :], ALU.mult, ALU.add)
                ts(tiny[:, 5, :], tiny[:, 5, :], PI_BELOW, -PI_BELOW, ALU.min, ALU.max)
                run(dve.tensor_scalar(tiny[:, 6, :], tiny[:, 5, :], -1.0, None, ALU.mult))
                tt(tiny[:, 6, :], tiny[:, 6, :], tiny[:, 5, :], ALU.min)
                run(dve.tensor_scalar(tiny[:, 6, :], tiny[:, 6, :], TWO_PI / 4, None, ALU.add))
                dve.sem_inc(sm["sin_arg"], 1)
                wait(dve, l, "par_act", 1)
                run(dve.memset(pw[:, 0, :, 0], 1.0))
                run(dve.memset(pw[:, 1, :, 0], 0.0))
                tt(pw[:, 0, :, 1], tiny[:, 3, :], tiny[:, 8, :], ALU.mult)
                tt(pw[:, 1, :, 1], tiny[:, 3, :], tiny[:, 7, :], ALU.mult)
                tt(tiny[:, 5, :], are, are, ALU.mult)
                tt(tiny[:, 6, :], aim, aim, ALU.mult)
                tt(tiny[:, 5, :], tiny[:, 5, :], tiny[:, 6, :], ALU.add)
                run(dve.reciprocal(tiny[:, 5, :], tiny[:, 5, :]))
                run(dve.tensor_scalar(tiny[:, 6, :], pw[:, 0, :, 1], 1.0, None, ALU.subtract))
                tt(tiny[:, 7, :], tiny[:, 6, :], are, ALU.mult)
                tt(tiny[:, 8, :], pw[:, 1, :, 1], aim, ALU.mult)
                tt(tiny[:, 7, :], tiny[:, 7, :], tiny[:, 8, :], ALU.add)
                tt(tiny[:, 9, :], tiny[:, 7, :], tiny[:, 5, :], ALU.mult)
                tt(tiny[:, 7, :], pw[:, 1, :, 1], are, ALU.mult)
                tt(tiny[:, 8, :], tiny[:, 6, :], aim, ALU.mult)
                tt(tiny[:, 7, :], tiny[:, 7, :], tiny[:, 8, :], ALU.subtract)
                tt(tiny[:, 10, :], tiny[:, 7, :], tiny[:, 5, :], ALU.mult)
                for lo in (1, 2, 4):
                    a = tiny[:, 0:lo, :].rearrange("p k q -> p q k")
                    b = tiny[:, 4:4 + lo, :].rearrange("p k q -> p q k")
                    cmul(pw[:, 0, :, lo + 1:2 * lo + 1], pw[:, 1, :, lo + 1:2 * lo + 1], pw[:, 0, :, 1:lo + 1], pw[:, 1, :, 1:lo + 1],
                         pw[:, 0, :, lo:lo + 1].to_broadcast([P, Q, lo]), pw[:, 1, :, lo:lo + 1].to_broadcast([P, Q, lo]), a, b)
                run(dve.tensor_copy(lv[:, 0, :, :], pw[:, :, :, T]))
                for k in range(5):
                    cmul(lv[:, k + 1, 0, :], lv[:, k + 1, 1, :], lv[:, k, 0, :], lv[:, k, 1, :], lv[:, k, 0, :], lv[:, k, 1, :],
                         tiny[:, 0, :], tiny[:, 4, :])

                def scores_max(i):
                    wait(dve, l, "sc_done", i + 1)
                    run(dve.tensor_reduce(stat[:, 4 * i:4 * i + 4],
                                          mp[:, 2 * (i % 2):2 * (i % 2) + 2, :].rearrange("p b (h m) -> p (b h) m", m=MEM), op=ALU.max, axis=AX.X))
                    run(dve.tensor_scalar(stat[:, 16 + 4 * i:20 + 4 * i], stat[:, 4 * i:4 * i + 4], -SCALE, None, ALU.mult))
                    dve.sem_inc(sm["nb_done"], 1)

                def probabilities(i):
                    wait(dve, l, "exp_done", i + 1)
                    run(dve.reciprocal(stat[:, 52:56], stat[:, 32 + 4 * i:36 + 4 * i]))
                    tt(pr[:, i % 2, :, :], pr[:, i % 2, :, :], stat[:, 52:56].unsqueeze(2).to_broadcast([P, HEADS, MEM]), ALU.mult)
                    dve.sem_inc(sm["p_norm"], 1)

                scores_max(0)
                scores_max(1)
                probabilities(0)
                probabilities(1)
                run(dve.memset(qm[:, :, :], 0.0))
                run(dve.memset(pm[:, :, :, :], 0.0))
                for a in range(2):
                    run(dve.tensor_copy(qm[:, :, :].rearrange("p r c -> p (r c)")[:, a * 16 * 33:a * 16 * 33 + 15 * 33 + 1:33]
                                        .rearrange("p (b h) -> p b h", h=HEADS),
                                        q[:, :, a, 4 * C:HC].rearrange("p h b -> p b h")))
                dve.sem_inc(sm["qm_done"], 1)
                wait(dve, l, "b_in", 64)
                bc = [tiny[:, 9 + i, :].unsqueeze(2).to_broadcast([P, Q, H]) for i in range(2)]
                wtmp = wt[:, :, :, :].rearrange("p a q s -> p (a q s)")
                ta, tb = (wtmp[:, i * 256:(i + 1) * 256].rearrange("p (q h) -> p q h", h=H) for i in range(2))
                cmul(bb[:, 0, :, :], bb[:, 1, :, :], bT[:, 0, :, :], bT[:, 1, :, :], bc[0], bc[1], ta, tb)
                scores_max(2)
                scores_max(3)
                probabilities(2)
                probabilities(3)

                def input_matrices(f):
                    if f:
                        wait(dve, l, "k_out", 16)
                    qs = slice(f * QH, (f + 1) * QH)
                    o = [wt[:, i, :, :].rearrange("p q (s h) -> p q s h", h=H) for i in range(2)]
                    p = [pw[:, i, qs, T - 1::-1].unsqueeze(3).to_broadcast([P, QH, T, H]) for i in range(2)]
                    b = [bb[:, i, qs, :].unsqueeze(2).to_broadcast([P, QH, T, H]) for i in range(2)]
                    ta = t1[:, 0:QH * T * H].rearrange("p (q s h) -> p q s h", q=QH, h=H)
                    tb = t2[:, 0:QH * T * H].rearrange("p (q s h) -> p q s h", q=QH, h=H)
                    tt(o[0], p[0], b[0], ALU.mult)
                    tt(ta, p[1], b[1], ALU.mult)
                    tt(o[0], o[0], ta, ALU.subtract)
                    tt(o[1], p[0], b[1], ALU.mult)
                    tt(tb, p[1], b[0], ALU.mult)
                    tt(o[1], o[1], tb, ALU.add)
                    dve.sem_inc(sm["wt_done"], 1)

                def output_matrices(f):
                    if f:
                        wait(dve, l, "y_done", 1)
                    qs = slice(f * QH, (f + 1) * QH)
                    p = [pw[:, i, qs, :].unsqueeze(3).to_broadcast([P, QH, T + 1, H]) for i in range(2)]
                    c = [cT[:, i, qs, :].unsqueeze(2).to_broadcast([P, QH, T + 1, H]) for i in range(2)]
                    ta = t1[:, :].rearrange("p (q s h) -> p q s h", q=QH, h=H)
                    tb = t2[:, :].rearrange("p (q s h) -> p q s h", q=QH, h=H)
                    tt(V[:, 0], p[0], c[0], ALU.mult)
                    tt(ta, p[1], c[1], ALU.mult)
                    tt(V[:, 0], V[:, 0], ta, ALU.subtract)
                    tt(V[:, 1], p[0], c[1], ALU.mult)
                    tt(tb, p[1], c[0], ALU.mult)
                    stt(V[:, 1].rearrange("p q s h -> p (q s h)"), V[:, 1].rearrange("p q s h -> p (q s h)"), -1.0, t2[:, :],
                        ALU.mult, ALU.subtract)
                    dve.sem_inc(sm["V_done"], 1)

                wait(dve, l, "pv_done", 1)
                input_matrices(0)
                wait(dve, l, "kv_out", 32)
                output_matrices(0)
                wait(dve, l, "scs_done", NB)
                run(dve.tensor_reduce(stat[0:32, 50:51], mp[0:32, 2, 0:MEM], op=ALU.max, axis=AX.X))
                run(dve.tensor_scalar(stat[0:32, 48:49], stat[0:32, 50:51], -SCALE, None, ALU.mult))
                dve.sem_inc(sm["nbs_done"], 1)
                wait(dve, l, "exps_done", 1)
                run(dve.reciprocal(stat[0:32, 51:52], stat[0:32, 49:50]))
                dve.tensor_scalar(ps[:, :], ps[:, :], stat[0:32, 51:52], None, ALU.mult).then_inc(sm["ps_norm"], 1)
                wait(dve, l, "psT_tr", 1)
                for m in range(2):
                    for hd in range(HEADS):
                        run(dve.tensor_copy(pm[:, m, :, :].rearrange("p b c -> p (b c)")[:, hd:hd + 7 * 36 + 1:36],
                                            mp[:, 3, m * 32 + hd:(m + 1) * 32:HEADS]))
                dve.sem_inc(sm["pm_ev"], 1)
                wait(dve, l, "oxT_tr", 1)
                for hd in range(HEADS):
                    run(dve.tensor_copy(q[:, hd, :, 4 * C:HC],
                                        mp[:, 3, hd * 32:(hd + 1) * 32].rearrange("p (a b h) -> p a b h", h=HEADS, a=2)[:, :, :, hd]))
                dve.sem_inc(sm["ox_done"], 1)
                run(dve.memset(U[:, :, :, 0:NB], 0.0))
                run(dve.memset(U[:, :, :, YC:UC], 0.0))
                dve.sem_inc(sm["U_clear"], 1)
                run(dve.memset(Mt[:, :, :], 0.0))
                dve.sem_inc(sm["m_clear"], 1)

                def scan(f):
                    wait(dve, l, "s_done", f + 1)
                    if f:
                        wait(dve, l, "y_done", 1)
                    qs = slice(f * QH, (f + 1) * QH)
                    for ri in range(2):
                        src = mp[:, 2 * ri:2 * ri + 2, 0:4 * YC].rearrange("p b (q c) -> p b q c", c=YC)
                        run(dve.tensor_copy(X[:, ri, :, NB + 1:].rearrange("p (b q) c -> p b q c", q=4), src[:, :, :, 0:C]))
                        run(dve.tensor_copy(ss[:, ri, :, :].rearrange("p (b q) c -> p b q c", q=4), src[:, :, :, C:]))
                    dve.sem_inc(sm["s_free"], 1)
                    run(dve.memset(X[:, :, :, NB], 0.0))
                    run(dve.tensor_copy(X[:, :, :, 0:NB], s0[:, :, :, qs].rearrange("p a b q -> p a q b")))

                    def level(k, first, n):
                        d = 1 << k
                        dst = X[:, :, :, NB + 1 + first:XC:2 * d]
                        src = X[:, :, :, NB + 1 + first - d:XC - d:2 * d]
                        m = 2 * QH * n
                        ta = t1[:, 0:m].rearrange("p (a q n) -> p a q n", a=2, n=n)
                        tb = t2[:, 0:m].rearrange("p (a q n) -> p a q n", a=2, n=n)
                        for ri in range(2):
                            ar = lv[:, k, 0, qs].unsqueeze(2).to_broadcast([P, QH, n])
                            ai = lv[:, k, 1, qs].unsqueeze(2).to_broadcast([P, QH, n])
                            tt(ta[:, ri], src[:, ri], ar, ALU.mult)
                            tt(tb[:, ri], src[:, ri], ai, ALU.mult)
                        tt(dst, dst, ta, ALU.add)
                        tt(dst[:, 0], dst[:, 0], tb[:, 1], ALU.subtract)
                        tt(dst[:, 1], dst[:, 1], tb[:, 0], ALU.add)

                    for k in range(6):
                        level(k, (2 << k) - 1, C >> (k + 1))
                    for k in range(4, -1, -1):
                        level(k, (3 << k) - 1, (C >> (k + 1)) - 1)
                    dve.sem_inc(sm["x_done"], 1)
                    run(dve.tensor_copy(sf[:, :, qs], X[:, :, :, XC - 1]))
                    o = [sn[:, i, :, qs].rearrange("p b q -> p q b") for i in range(2)]
                    s = [s0[:, i, :, qs].rearrange("p b q -> p q b") for i in range(2)]
                    a = [pw[:, i, qs, 1:2].to_broadcast([P, QH, NB]) for i in range(2)]
                    ta = t1[:, 0:QH * NB].rearrange("p (q b) -> p q b", b=NB)
                    for i, (x, y, op) in enumerate(((0, 1, ALU.subtract), (1, 0, ALU.add))):
                        tt(o[i], s[x], a[0], ALU.mult)
                        tt(ta, s[y], a[1], ALU.mult)
                        tt(o[i], o[i], ta, op)
                        tt(o[i], o[i], ss[:, i, :, :], ALU.add)

                def keep_lags(f):
                    wait(dve, l, "k_done", f + 1)
                    kv = kt[:, :, :].rearrange("h (q e) x -> h e q x", e=2)
                    for e in range(2):
                        run(dve.tensor_copy(kv[:, e], mp[0:H, 2 * e:2 * e + 2, :].rearrange("h b (q x) -> h (b q) x", x=P)))
                    dve.sem_inc(sm["k_free"], 1)
                    ta = t1[0:H, 0:256].rearrange("h (g x) -> h g x", x=H)
                    tt(ta, ident[0:H, 0:H].unsqueeze(1).to_broadcast([H, G // 2, H]),
                       dcol[:, f * (G // 2):(f + 1) * (G // 2)].unsqueeze(2).to_broadcast([H, G // 2, H]), ALU.mult)
                    tt(kt[:, :, 0:H], kt[:, :, 0:H], ta, ALU.add)
                    dve.sem_inc(sm["k_ev"], 1)

                wait(dve, l, "w_tr", 1)
                scan(0)
                keep_lags(0)
                input_matrices(1)
                output_matrices(1)
                scan(1)
                keep_lags(1)
                dve.sem_inc(sm["sn_done"], 1)

                wait(dve, l, "v_done", 4)
                for i in range(ET):
                    run(dve.tensor_copy(v_last[:, i, :].rearrange("p (c t) -> p c t", t=T), vx[:, i, 8:16, C:C + 4].rearrange("p t c -> p c t")))
                dve.sem_inc(sm["v_last_done"], 1)
                run(dve.memset(vx[:, :, :, 0:4], 0.0))
                for i in range(ET):
                    run(dve.tensor_copy(vx[:, i, 0:8, 4:], vx[:, i, 8:16, 3:3 + C]))
                for i in range(ET):
                    if i == 0:
                        wait(dve, l, "acc_free1", use["za"] // 2 + 1)
                        wait(dve, l, "y_ev", 8)
                        wait(dve, l, "y_out", 160)
                    tt(br[:, 2, i, :, :], q[:, i, :, :], z[:, 2, i, :, :], ALU.mult)
                dve.sem_inc(sm["br_x_done"], 1)
                wait(dve, l, "sfin_tr", 1)
                run(dve.tensor_copy(so[0:Q, 0:2, :].rearrange("p a c -> p (a c)"), mp[0:Q, 0, 0:2 * P]))
                run(dve.tensor_copy(so[:, 2:4, :].rearrange("p a c -> p (a c)"), mp[:, 0, 2 * P:4 * P]))
                dve.sem_inc(sm["sfin_ev"], 1)
                wait(dve, l, "st_tr", 1)
                for r in range(2):
                    run(dve.tensor_copy(cs[:, :, 4 * r:4 * r + 4, 0:TAPS - 1],
                                        mp[:, 1 + r, 0:480].rearrange("p (i b k) -> p i b k", i=ET, b=4)))
                for i in range(ET):
                    run(dve.tensor_copy(cs[:, i, :, TAPS - 1], v_s[:, i, :]))
                dve.sem_inc(sm["st_ev"], 1)
                wait(dve, l, "vs_tr", 2)
                run(dve.tensor_copy(nst[:, :], mp[0:32, 3, :]))
                run(dve.tensor_copy(nss[:, :], mp[0:NB, 0, :]))
                dve.sem_inc(sm["vs_ev"], 1)

                taps = cw[:, :].rearrange("p (k i) -> p i k", i=ET)
                for i in range(ET):
                    if i >= 2:
                        wait(dve, l, "acc_done", 2 * i - 3)
                    o = cacc[:, i % 2, :, :]
                    for k in range(TAPS):
                        src = vx[:, i, 8 - k % 8:16 - k % 8, 4 - k // 8:4 - k // 8 + C]
                        w = taps[:, i, TAPS - 1 - k:TAPS - k]
                        if k == 0:
                            run(dve.tensor_scalar(o, src, w, None, ALU.mult))
                        else:
                            stt(o, src, w, o, ALU.mult, ALU.add)
                    dve.sem_inc(sm["conv_tile"], 1)
                    tt(cst[:, :, :], cs[:, i, :, :], taps[:, i, :].unsqueeze(1).to_broadcast([P, NB, TAPS]), ALU.mult)
                    run(dve.tensor_reduce(v_s[:, i, :], cst[:, :, :], op=ALU.add, axis=AX.X))
                    dve.sem_inc(sm["conv_tile"], 1)
                wait(dve, l, "z_ev", 1)
                for i in range(ET):
                    wait(dve, l, "glu_sg", i + 1)
                    tt(br[:, 0, i, :, :], u[:, i, :, :], sg[:, i % 2, :, :], ALU.mult)
                    dve.sem_inc(sm["sg_free"], 1)
                    tt(br[:, 0, i, :, :], br[:, 0, i, :, :], z[:, 0, i, :, :], ALU.mult)
                    dve.sem_inc(sm["br_a_done"], 1)
                wait(dve, l, "mean_done", 1)
                for i in range(ET):
                    stt(acc[:, i, :, :], mp[:, 0:2, 0:HC], -1.0 / E, acc[:, i, :, :], ALU.mult, ALU.add)
                    dve.sem_inc(sm["cent_done"], 1)
                wait(dve, l, "lsq_used", ET)
                wait(dve, l, "vo_out", 48)
                ts(lst[:, :, :], mp[:, 2:4, 0:HC], 1.0 / E, EPS, ALU.mult, ALU.add)
                dve.reciprocal(lst[:, :, :], lst[:, :, :]).then_inc(sm["lvar_done"], 1)
                wait(dve, l, "lrstd_done", 1)
                for i in range(ET):
                    stt(acc[:, i, :, :], acc[:, i, :, :], vec[:, 24 + i:25 + i], lst[:, :, :], ALU.mult, ALU.mult)
                    dve.sem_inc(sm["ln_done"], 1)
                for i in range(ET):
                    wait(dve, l, "ln_silu", i + 1)
                    tt(br[:, 1, i, :, :], acc[:, i, :, :], z[:, 1, i, :, :], ALU.mult)
                    dve.sem_inc(sm["br_b_done"], 1)
                steps.clear()

                with dve.Fori(0, 4) as it:
                    inner = Steps(dve, loop_steps)
                    for jj in range(2):
                        for x in range(3):
                            m = jj * 3 + x
                            wait(dve, l, "acc_ready1", it * 6 + use["gates"] // 2 + m + 1)
                            wait(dve, l, "gate_sg", it * 6 + m + 1)
                            inner.run(dve.tensor_tensor((mj if x == 0 else tj)[:, :, :], acc_ps[1][:, :, 0:HC], sg[:, m % 2, :, :], ALU.mult))
                            dve.sem_inc(acc_free[1], 1)
                            dve.sem_inc(sm["sg_free"], 1)
                            if x:
                                inner.run(dve.tensor_tensor(mj[:, :, :], mj[:, :, :], tj[:, :, :], ALU.add))
                        j = it * 2 + jj
                        hi, lo = (t[:, bass.ds(j, 1), :, :].rearrange("p j a c -> p (j a) c") for t in (m_hi, m_lo))
                        inner.run(dve.tensor_copy(hi, mj[:, :, :]))
                        inner.run(dve.tensor_tensor(lo, mj[:, :, :], hi.bitcast(F32), ALU.subtract))
                        dve.sem_inc(sm["m_done"], 1)
                    inner.clear()
                with dve.Fori(0, 4) as it:
                    inner = Steps(dve, loop_steps)
                    for k in range(2):
                        wait(dve, l, f"acc_ready{k}", it + use["out"] // 2 + 1)
                        xj = xT[:, bass.ds(it * 2 + k, 1), :, :].rearrange("p j a c -> p (j a) c")
                        inner.run(dve.tensor_tensor(xj, acc_ps[k][:, :, 0:HC], xj, ALU.add))
                        dve.sem_inc(acc_free[k], 1)
                        dve.sem_inc(sm["x_sum"], 1)
                    inner.clear()

            dve.wait_ge(sm["fin_used"], KT)
            ts(rs[:, :, :], mp[:, 0:2, 0:HC], 1.0 / D, EPS, ALU.mult, ALU.add)
            dve.reciprocal(rs[:, :, :], rs[:, :, :]).then_inc(sm["fin_var"], 1)
            dve.wait_ge(sm["fin_rt"], 1)
            for k in range(KT):
                stt(xT[:, k, :, :], xT[:, k, :, :], vec[:, 80 + k:81 + k], rs[:, :, :], ALU.mult, ALU.mult)
                dve.sem_inc(sm["fin_y"], 1)
            run(dve.tensor_copy(xsc[:, :, :].rearrange("p k (a c) -> p k a c", a=2), xT[:, :, :, 4 * C:HC]))
            dve.sem_inc(sm["fin_y"], 1)


INS = ("x_prompt", "x_sample", "mem_prompt", "state_ssm_re", "state_ssm_im", "state_conv", "cache_mem_k",
       "cache_mem_v", "norm_g", "w_in", "ssm_a_re", "ssm_a_im", "ssm_log_dt", "ssm_b_re", "ssm_b_im", "ssm_c_re",
       "ssm_c_im", "ssm_d", "w_glu", "b_glu", "w_br_ssm", "conv_w", "conv_b", "conv_ln_g", "conv_ln_b",
       "w_br_conv", "mem_norm_g", "w_k", "w_v", "w_br_xatt", "w_out", "final_norm_g")
OUTS = ((1, SEQ, D), (NB, 1, D), (LAYERS, 1, G, S), (LAYERS, 1, G, S), (LAYERS, 1, TAPS - 1, E),
        (LAYERS, 1, MEM, HEADS, P), (LAYERS, 1, MEM, HEADS, P), (LAYERS, NB, G, S), (LAYERS, NB, G, S),
        (LAYERS, NB, TAPS - 1, E))


def kernel(**inputs):
    import concourse.bacc as bacc
    import numpy as np
    from concourse.bass_utils import run_bass_kernel_spmd

    nc = bacc.Bacc("TRN2", target_bir_lowering=False, num_devices=1)
    arrays, args = {}, []
    for name in INS:
        a = np.ascontiguousarray(inputs[name])
        arrays[f"in_{name}"] = a
        args.append(nc.dram_tensor(f"in_{name}", a.shape, mybir.dt.from_np(a.dtype), kind="ExternalInput").ap())
    for i, shape in enumerate(OUTS):
        args.append(nc.dram_tensor(f"out_{i}", shape, F32, kind="ExternalOutput").ap())
    build(nc, *args)
    r = run_bass_kernel_spmd(nc, [arrays], core_ids=[0])
    return tuple(r.results[0][f"out_{i}"] for i in range(len(OUTS)))
```

```python
from contextlib import ExitStack

import concourse.bass as bass
from concourse import mybir

F32 = mybir.dt.float32
F32R = mybir.dt.float32r
ALU = mybir.AluOpType
ACT = mybir.ActivationFunctionType
AX = mybir.AxisListType

P = 128
D = 1024
SEQ = 512
LAYERS = 2
NB = 8
MEM = 256
KT = D // P
E = 512
ET = E // P
HEADS = 4
G, H, S = 32, 16, 64
Q = G // 2
QH = Q // 2
T = 8
C = SEQ // T
TAPS = 31
HC = 4 * C + 4
EPS = 1e-6
SCALE = P ** -0.5
XC = NB + 1 + C
UC = NB + C + NB
YC = NB + C
UNITS = 60
TWO_PI = 6.283185307179586
PI2_HI, PI2_MID = 6.28125, 0.0019350051879882812
PI2_LO = TWO_PI - PI2_HI - PI2_MID
PI_BELOW = 3.1415925
ROUND = 12582912.0


class Steps:

    def __init__(self, eng, sem):
        self.eng, self.sem, self.n = eng, sem, 0

    def run(self, ins, behind=0):
        self.n += 1
        ins.then_inc(self.sem, 1)
        if behind < self.n:
            self.eng.wait_ge(self.sem, self.n - behind)

    def clear(self):
        self.eng.sem_clear(self.sem)
        self.n = 0


def build(nc, x_prompt, x_sample, mem_prompt, state_ssm_re, state_ssm_im, state_conv, cache_mem_k,
          cache_mem_v, norm_g, w_in, ssm_a_re, ssm_a_im, ssm_log_dt, ssm_b_re, ssm_b_im, ssm_c_re,
          ssm_c_im, ssm_d, w_glu, b_glu, w_br_ssm, conv_w, conv_b, conv_ln_g, conv_ln_b, w_br_conv,
          mem_norm_g, w_k, w_v, w_br_xatt, w_out, final_norm_g, y_prompt, y_sample, ssm_re_p, ssm_im_p,
          conv_p, mem_k_p, mem_v_p, ssm_re_s, ssm_im_s, conv_s):
    ctx = ExitStack()

    def sb(name, shape, dt=F32):
        return ctx.enter_context(nc.sbuf_tensor(name, shape, dt))

    def sem(name):
        return ctx.enter_context(nc.semaphore(name))

    with ctx:
        xT = sb("xT", [P, KT, 2, HC])
        h_hi = sb("h_hi", [P, KT, 2, HC], F32R)
        h_lo = sb("h_lo", [P, KT, 2, HC], F32R)
        w_hi = sb("w_hi", [P, 2, KT * P], F32R)
        w_lo = sb("w_lo", [P, 2, KT * P], F32R)
        w_st = sb("w_st", [P, 2, KT * P])
        wd_at = nc.sbuf_base
        w_dir = sb("w_dir", [P, 2, 12 * P])
        q = sb("q", [P, ET, 2, HC])
        sg = sb("sg", [P, 2, 2, HC])
        ident = sb("ident", [P, P])
        ones = sb("ones", [P, P])
        eye2 = sb("eye2", [2 * H, H])
        vec = sb("vec", [P, 88])
        cw = sb("cw", [P, TAPS * ET])
        dcol = sb("dcol", [2 * H, Q])
        pw = sb("pw", [P, 2, Q, T + 1])
        lv = sb("lv", [P, 6, 2, Q])
        tiny = sb("tiny", [P, 12, Q])
        stat = sb("stat", [P, 64])
        s0 = sb("s0", [P, 2, NB, Q])
        sn = sb("sn", [P, 2, NB, Q])
        sf = sb("sf", [P, 2, Q])
        v_s = sb("v_s", [P, ET, NB])
        v_last = sb("v_last", [P, ET, 32])

        z_at = nc.sbuf_base
        zreg = sb("zreg", [P, 12 * 2 * HC])
        v_at = nc.sbuf_base
        vreg = sb("vreg", [P, ET * 16 * (C + 4)])
        u_at = nc.sbuf_base
        ureg = sb("ureg", [P, ET * 2 * HC])
        r_at = nc.sbuf_base
        rlen = 13312
        rreg = sb("rreg", [P, rlen])
        assert v_at == z_at + 4 * 12 * 2 * HC

        def at(base, off, limit, name, shape, dt=F32):
            n = 1
            for d in shape[1:]:
                n *= d
            assert off + n <= limit, (name, off + n, limit)
            return nc.alloc_sbuf_tensor_at(name, shape, dt, offset=base + 4 * off)

        def zr(name, off, shape):
            return at(z_at, off, 12 * 2 * HC, name, shape)

        def ur(name, off, shape):
            return at(u_at, off, ET * 2 * HC, name, shape)

        def rr(name, off, shape):
            return at(r_at, off, rlen, name, shape)

        z = zr("z", 0, [P, 3, ET, 2, HC])
        m_hi = at(z_at, 0, 10**6, "m_hi", [P, KT, 2, HC], F32R)
        m_lo = at(z_at, KT * 2 * HC, 10**6, "m_lo", [P, KT, 2, HC], F32R)
        assert 2 * KT * 2 * HC <= 12 * 2 * HC + ET * 16 * (C + 4)
        vx = at(v_at, 0, 10**6, "vx", [P, ET, 16, C + 4])
        u = ur("u", 0, [P, ET, 2, HC])
        prow = ur("prow", 0, [88, P])
        cwrow = ur("cwrow", 128, [TAPS * ET, P])
        crow = ur("crow", 256, [P, 2, 2, P])
        srow = ur("srow", 768, [P, 2, P])
        drow = ur("drow", 1024, [Q, 2 * H])
        dtrow = ur("dtrow", 1040, [80, 2])
        bT = zr("bT", 0, [P, 2, Q, H])
        bd = zr("bd", 0, [P, 2, Q, 2, H])
        bb = zr("bb", 1024, [P, 2, Q, H])
        cT = zr("cT", 1536, [P, 2, Q, H])
        wt = zr("wt", 2048, [P, 2, QH, T * H])
        xrow = rr("xrow", 0, [P, 4, D])
        mrow = rr("mrow", 4096, [P, 2, D])
        xsrow = rr("xsrow", 6144, [NB, D])
        memn0 = rr("memn0", 7168, [P, KT, MEM])
        memn = rr("memn", 0, [P, KT, MEM])
        memg = rr("memg", 2048, [P, KT, MEM])
        kb = rr("kb", 0, [P, 4, 2, E])
        ktok = rr("ktok", 4096, [P, 2, E])
        ps = rr("ps", 4096, [32, MEM])
        pm = zr("pm", 5216, [P, 2, NB, 32])
        qrow = zr("qrow", 4608, [NB, E])
        qs = zr("qs", 5120, [P, HEADS, NB])
        qk = zr("qk", 5152, [P, 2, E])
        sK = zr("sK", 6176, [P, 2, NB * HEADS])
        vtok = rr("vtok", 5120, [P, 2, E])
        kT = rr("kT", 6144, [P, HEADS, MEM])
        pr = rr("pr", 7168, [P, 2, HEADS, MEM])
        oxs = rr("oxs", 7168, [32, E])
        pT = rr("pT", 9216, [P, HEADS, 2, SEQ])
        sq = rr("sq", 9216, [P, 4, 2, HC])
        ht = rr("ht", 9216 + 2080, [P, 2, 2, HC])
        rs = rr("rs", 9216 + 3120, [P, 2, HC])
        U = rr("U", 0, [P, Q, 2, UC])
        wl = rr("wl", 2560, [P, QH, 2, 2 * S])
        V = rr("V", 4608, [P, 2, QH, T + 1, H])
        Mt = rr("Mt", 6912, [P, G // 2, T * H])
        X = rr("X", 8960, [P, 2, QH, XC + NB])
        t1 = rr("t1", 10256, [P, QH * (T + 1) * H])
        t2 = rr("t2", 11408, [P, QH * (T + 1) * H])
        br = rr("br", 0, [P, 3, ET, 2, HC])
        cv = at(v_at, 0, 10**6, "cv", [P, ET, 2, 2, 2 * (C + 4) * 2])
        cs = rr("cs", 8320, [P, ET, NB, TAPS])
        cst = rr("cst", 9312, [P, NB, TAPS])
        crw = rr("crw", 9560, [120, 2, E])
        lst = rr("lst", 11624, [P, 2, HC])
        mj = rr("mj", 12144, [P, 2, HC])
        kt = at(wd_at, 0, 24 * P, "kt", [2 * H, QH, T * H])
        cacc = at(wd_at, 16 * P, 24 * P, "cacc", [P, 2, T, C])
        so = rr("so", 12664, [P, 4, P])
        nst = rr("nst", 11624, [32, E])
        nss = rr("nss", 12144, [NB, E])
        tj = rr("tj", 11624, [P, 2, HC])
        yrow = rr("yrow", 0, [P, 2, D])
        ysr = rr("ysr", 2048, [NB, D])
        xsc = rr("xsc", 3072, [P, KT, NB])

        acc_ps = [ctx.enter_context(nc.psum_tensor(f"acc{i}", [P, 2, 512], F32)) for i in range(2)]
        mp = ctx.enter_context(nc.psum_tensor("mp", [P, 4, 512], F32))

        u_dram = nc.dram_tensor("u_scratch", (E, 2, HC), F32).ap()
        y_dram = nc.dram_tensor("y_scratch", (E, 2, HC), F32).ap()
        k_dram = nc.dram_tensor("k_scratch", (G, H, T * H), F32).ap()
        m_dram = nc.dram_tensor("m_scratch", (P, KT * MEM), F32).ap()

        w_loaded = [sem(f"w_loaded{i}") for i in range(2)]
        w_staged_free = sem("w_staged_free")
        w_hi_done = sem("w_hi_done")
        w_lo_done = sem("w_lo_done")
        layer_left = {e: sem(f"layer_left_{e}") for e in ("sp", "pe", "act")}
        layer_go = sem("layer_go")
        layers_begun = sem("layers_begun")
        dve_steps = sem("dve_steps")
        act_steps = sem("act_steps")
        loop_steps = sem("loop_steps")

        sm = {n: sem(n) for n in """
            x_in mem_in consts x_tr x_ev mem_sq mem_var mem_rt mem_nrm mem_tr mem_ev mem_out fin_sq fin_used
            fin_var fin_rt fin_y fin_tr fin_ev fin_out0 fin_out1 fin_out2 fin_out3 fin_out_s""".split()}
        entered = {e: sem(f"entered_{e}") for e in ("sp", "pe")}

        per = """
            dt_in=16 dt_wide=1 p_in=176 c_in=128 b_in=64 s_in=32 mg_in=16 sq_done=8 sq_used=8 var_done=1
            rstd_done=1 ht_done=8 hhi_done=8 h_done=1 par_tr=1 par_ev=1 s0_tr=1 s0_ev=1 memg_done=1
            kv_used=6 kv_ev=2 kT_tr=1 kT_ev=1 kv_out=32 q_ev=4 dt_exp=1 sin_arg=1 par_act=1 sc_done=4
            nb_done=4 exp_done=4 p_norm=4 pT_tr=4 pT_ev=4 pv_done=1 pv_ev=1 kb_in0=64 kb_in1=64 kb_in2=64 kb_in3=64
            qs_done=1 qrow_tr=1 qrow_ev=1 bc_done=8 kq_done=8 scs_done=1 nbs_done=1 exps_done=1 ps_norm=1 psT_tr=1 pm_ev=1 pvs_done=8
            oxs_ev=1 oxT_tr=1 ox_done=1 u_ev=4 u_out=16 U_clear=1 U_in=192 val_ev=8 v_done=4 v_last_done=4
            wt_done=2 w_tr=2 wl_ev=2 s_done=2 s_free=2 V_done=2 k_done=2 k_free=2 k_ev=2 k_out=32 m_clear=1
            m_in=256 x_done=2 y_done=2 y_ev=8 y_out=160 y_in=16 sn_done=1 sfin_tr=1 sfin_ev=1 sfin_out=64
            st_in=32 st_tr=1 st_ev=1 vs_tr=2 vs_ev=1 vo_out=48 acc_done=4 mean_done=1
            cent_done=4 lsq_done=4 lsq_used=1 lvar_done=1 lrstd_done=1 ln_done=4 ln_silu=4 br_b_done=4
            br_x_done=1 glu_sg=4 br_a_done=4 gate_sg=24 sg_free=32 m_done=8 x_sum=8 z_ev=1 acc_ready0=45
            acc_ready1=45 acc_free0=45 acc_free1=45 d_loaded0=272 d_loaded1=272""".split()
        per = {n: int(k) for n, k in (x.split("=") for x in per)}
        sm.update({n: sem(n) for n in per})
        acc_ready, acc_free, d_loaded = ([sm[f"{n}{i}"] for i in range(2)] for n in ("acc_ready", "acc_free", "d_loaded"))

        def wait(eng, l, name, value):
            eng.wait_ge(sm[name], l * per[name] + value)

        use, n = {}, 0
        for name, k in (("kv", 2), ("q", 4), ("u", 4), ("v", 6), ("zx", 2), ("v3", 2), ("zx1", 2), ("za", 4), ("zb", 4),
                        ("glu", 4), ("gates", 48), ("out", 8)):
            use[name] = n
            n += k
        unit, n = {}, 0
        for name, k in (("q", 4), ("u", 4), ("v", 6), ("zx", 2), ("v3", 2), ("zx1", 2), ("za", 4), ("zb", 4), ("gates", 24),
                        ("out", 8)):
            unit[name] = n
            n += k
        assert n == UNITS
        for d in (use, unit):
            d["v3"] -= 6
            d["zx1"] -= 2

        def acc(i):
            return cv[:, i, 0, :, 0:HC]

        def lsq(i):
            return cv[:, i, 1, :, 0:HC]

        def g3(ap):
            return ap[:, :, :, 0:4 * C]

        block = ctx.enter_context(nc.Block())

        @block.sync
        def _(sp):
            xp = x_prompt[0].rearrange("(c i s) d -> s c i d", s=2, i=4)
            for s in range(2):
                sp.dma_start(xrow[s * C:(s + 1) * C, :, :], xp[s]).then_inc(sm["x_in"], 16)
            sp.dma_start(xsrow[:, :], x_sample[:, 0, :]).then_inc(sm["x_in"], 16)
            sp.dma_start(mrow[:, :, :], mem_prompt[0].rearrange("(m p) d -> p m d", p=P)).then_inc(sm["mem_in"], 16)
            sp.wait_ge(sm["mem_ev"], 2)
            sp.dma_start(m_dram, memn0[:, :, :].rearrange("p k m -> p (k m)")).then_inc(sm["mem_out"], 16)
            sp.wait_ge(sm["mem_out"], 16)

            def ring_load(src, slot, n):
                sp.wait_ge(w_staged_free, n + 1)
                sp.dma_start(w_st[:, slot, :].rearrange("p (k c) -> p k c", c=P), src).then_inc(w_loaded[slot], 16)

            with sp.Fori(0, LAYERS) as l:
                sp.drain().then_inc(layer_left["sp"], 1)
                sp.wait_ge(layer_go, l + 1)
                sp.dma_start(dtrow[64:80, :], ssm_log_dt[l].rearrange("(q e) -> q e", e=2)).then_inc(sm["dt_in"], 16)
                win = w_in[l].rearrange("(k p) c -> p k c", p=P)
                wo = w_out[l].rearrange("(k p) c -> p k c", p=P)

                def section(name, pairs, cols, first=0, src=win):
                    sp.sem_inc(entered["sp"], 1)
                    with sp.Fori(first, first + pairs) as it:
                        for k, col in enumerate(cols):
                            ring_load(src[:, :, bass.ds(col(it), P)], k, l * UNITS + unit[name] + it * 2 + k)

                def straight(c0):
                    return [lambda it, k=k: (it * 2 + k) * P + c0 for k in range(2)]

                section("q", 1, straight(5 * E))
                sp.dma_start(memn[:, :, :].rearrange("p k m -> p (k m)"), m_dram).then_inc(sm["mg_in"], 16)
                rows = ((0, 16, ssm_a_re[l].rearrange("(q e) p -> q (e p)", e=2)),
                        (16, 4, b_glu[l].rearrange("(k p) -> k p", p=P)),
                        (20, 4, conv_b[l].rearrange("(k p) -> k p", p=P)),
                        (24, 4, conv_ln_g[l].rearrange("(k p) -> k p", p=P)),
                        (28, 4, conv_ln_b[l].rearrange("(k p) -> k p", p=P)),
                        (32, 16, ssm_a_im[l].rearrange("(q e) p -> q (e p)", e=2)),
                        (48, 8, norm_g[l].rearrange("(k p) -> k p", p=P)),
                        (56, 8, mem_norm_g[l].rearrange("(k p) -> k p", p=P)),
                        (80, 8, final_norm_g.rearrange("(k p) -> k p", p=P)))
                for r0, n, src in rows:
                    sp.dma_start(prow[r0:r0 + n, :], src).then_inc(sm["p_in"], 16)
                sp.dma_start(cwrow[:, :], conv_w[l].rearrange("k (i c) -> (k i) c", c=P)).then_inc(sm["p_in"], 16)
                sp.dma_start(drow[:, :], ssm_d[l].rearrange("(q x) -> q x", x=2 * H)).then_inc(sm["p_in"], 16)

                def kv_load(i):
                    src = (w_k, w_v)[i // 4][l].rearrange("(k p) c -> p k c", p=P)
                    if i >= 2:
                        if i - 2 == 3:
                            wait(sp, l, "acc_ready0", 1)
                        else:
                            wait(sp, l, "kv_used", i - 1 - (i > 5))
                    sp.dma_start(w_dir[:, i % 2, 0:2 * E].rearrange("p (k c) -> p k c", c=E),
                                 src[:, 2 * (i % 4):2 * (i % 4) + 2, :]).then_inc(d_loaded[i % 2], 16)

                kv_load(0)
                kv_load(1)
                for ri, src in enumerate((ssm_c_re, ssm_c_im)):
                    for half in range(2):
                        for e in range(2):
                            cv = src[l].rearrange("(f q e) h p -> f e q h p", e=2, f=2)[half, e]
                            sp.dma_start(crow[:, ri, half, e * S:(e + 1) * S], cv).then_inc(sm["c_in"], 16)
                for ri, src in enumerate((ssm_b_re, ssm_b_im)):
                    bv = src[l].rearrange("(q e) p h -> e p q h", e=2)
                    for e in range(2):
                        sp.dma_start(bT[e * S:(e + 1) * S, ri, :, :], bv[e]).then_inc(sm["b_in"], 16)
                for ri, src in enumerate((state_ssm_re, state_ssm_im)):
                    sp.dma_start(srow[:, ri, :], src[l].rearrange("b (q e) p -> (b q) (e p)", e=2)).then_inc(sm["s_in"], 16)
                for i in range(2, 8):
                    kv_load(i)
                section("q", 1, straight(5 * E), first=1)
                wait(sp, l, "kv_ev", 2)
                sp.dma_start(mem_k_p[l, 0].rearrange("(m p) h d -> p m (h d)", p=P), ktok[:, :, :]).then_inc(sm["kv_out"], 16)
                sp.dma_start(mem_v_p[l, 0].rearrange("(m p) h d -> p m (h d)", p=P), vtok[:, :, :]).then_inc(sm["kv_out"], 16)
                section("u", 2, straight(0))

                def cache_load(cache, b):
                    sp.dma_start(kb[:, b % 4, :, :], cache[l, b].rearrange("(m p) h d -> p m (h d)", p=P)).then_inc(sm[f"kb_in{b % 4}"], 16)

                wait(sp, l, "acc_ready1", 1)
                for b in range(4):
                    cache_load(cache_mem_k, b)
                v_cols = [lambda it: 3 * E + it * P, lambda it: 2 * E + it * P]
                section("v", 2, v_cols)
                wait(sp, l, "u_ev", 4)
                sp.dma_start(u_dram.rearrange("(i p) a c -> p i (a c)", p=P), u[:, :, :, :].rearrange("p i a c -> p i (a c)")).then_inc(sm["u_out"], 16)
                section("v", 1, v_cols, first=2)
                for b in range(4, NB):
                    wait(sp, l, "kq_done", b - 3)
                    cache_load(cache_mem_k, b)
                section("zx", 1, straight(6 * E))
                for b in range(4):
                    wait(sp, l, "kq_done", b + 5)
                    cache_load(cache_mem_v, b)
                section("v3", 1, v_cols, first=3)
                for b in range(4, NB):
                    wait(sp, l, "pvs_done", b - 3)
                    cache_load(cache_mem_v, b)
                section("zx1", 1, straight(6 * E), first=1)
                wait(sp, l, "u_out", 16)
                wait(sp, l, "U_clear", 1)
                ug = u_dram.rearrange("(g h) a c -> h g a c", h=H)
                Ug = U[:, :, :, :].rearrange("p q e c -> p (q e) c")
                for t in range(T):
                    sp.dma_start(Ug[t * H:(t + 1) * H, :, NB:NB + C], ug[:, :, t // 4, (t % 4) * C:(t % 4 + 1) * C]).then_inc(sm["U_in"], 16)
                for a in range(2):
                    sp.dma_start(Ug[0:H, :, 4 * a:4 * a + 4], ug[:, :, a, 4 * C:HC]).then_inc(sm["U_in"], 16)
                    sp.dma_start(Ug[7 * H:P, :, YC + 4 * a:YC + 4 * a + 4], ug[:, :, a, 4 * C:HC]).then_inc(sm["U_in"], 16)

                def toeplitz(half):
                    wait(sp, l, "k_ev", half + 1)
                    kh = k_dram[half * (G // 2):(half + 1) * (G // 2)]
                    kg = kh.rearrange("g h x -> h g x")
                    sp.dma_start(kh.rearrange("(q e) h x -> (e h) q x", e=2), kt[:, :, :]).then_inc(sm["k_out"], 16)
                    wait(sp, l, "k_out", 16 * (half + 1))
                    if half == 0:
                        wait(sp, l, "m_clear", 1)
                    else:
                        wait(sp, l, "y_done", 1)
                    for s in range(T):
                        sp.dma_start(Mt[s * H:(s + 1) * H, :, s * H:], kg[:, :, 0:(T - s) * H]).then_inc(sm["m_in"], 16)

                toeplitz(0)
                section("za", 1, straight(E))
                toeplitz(1)
                section("za", 1, straight(E), first=1)
                section("zb", 1, straight(4 * E))
                sp.dma_start(conv_s[l, :, 0:TAPS - 2, :], state_conv[l, :, 1:TAPS - 1, :]).then_inc(sm["vo_out"], 16)
                wait(sp, l, "y_ev", 8)
                wait(sp, l, "sn_done", 1)
                for r in range(2):
                    sp.dma_start(crw[:, r, :], state_conv[l].rearrange("(r b) k c -> r (b k) c", r=2)[r]).then_inc(sm["st_in"], 16)
                yg = y_dram.rearrange("(g h) a c -> h g a c", h=H)
                for t in range(T):
                    sp.dma_start(yg[:, :, t // 4, (t % 4) * C:(t % 4 + 1) * C], Ug[t * H:(t + 1) * H, :, NB:YC]).then_inc(sm["y_out"], 16)
                for a in range(2):
                    sp.dma_start(yg[:, :, a, 4 * C:HC], Ug[0:H, :, 4 * a:4 * a + 4]).then_inc(sm["y_out"], 16)
                wait(sp, l, "y_out", 160)
                sp.dma_start(u[:, :, :, :].rearrange("p i a c -> p i (a c)"), y_dram.rearrange("(i p) a c -> p i (a c)", p=P)).then_inc(sm["y_in"], 16)
                section("zb", 1, straight(4 * E), first=1)
                wait(sp, l, "acc_done", 4)
                for g in range(2):
                    sp.dma_start(w_dir[:, g, 0:2 * E].rearrange("p (k c) -> p k c", c=2 * P),
                                 w_glu[l].rearrange("(k p) c -> p k c", p=P)[:, :, g * 2 * P:(g + 1) * 2 * P]).then_inc(d_loaded[g], 16)
                branch_w = (w_br_ssm, w_br_conv, w_br_xatt)

                def branch_load(it, jj):
                    wait(sp, l, "acc_ready1", it * 6 + use["gates"] // 2 - 1 + jj)
                    sp.sem_inc(entered["sp"], 1)
                    for x in range(3):
                        sp.dma_start(w_dir[:, jj, x * 4 * P:(x + 1) * 4 * P].rearrange("p (k c) -> p k c", c=P),
                                     branch_w[x][l].rearrange("(k p) c -> p k c", p=P)[:, :, bass.ds((it * 2 + jj) * P, P)]).then_inc(d_loaded[jj], 16)

                def gate_load(it, m):
                    it, m = it + m // 6, m % 6
                    ring_load(win[:, :, bass.ds(7 * E + (m % 3) * D + (it * 2 + m // 3) * P, P)], m % 2,
                              l * UNITS + unit["gates"] + it * 6 + m)

                gate_load(0, 0)
                gate_load(0, 1)
                wait(sp, l, "sfin_ev", 1)
                sp.dma_start(ssm_re_p[l, 0].rearrange("(q e) p -> q (e p)", e=2), so[0:Q, 0, :]).then_inc(sm["sfin_out"], 16)
                sp.dma_start(ssm_im_p[l, 0].rearrange("(q e) p -> q (e p)", e=2), so[0:Q, 1, :]).then_inc(sm["sfin_out"], 16)
                sp.dma_start(ssm_re_s[l].rearrange("b (q e) p -> (b q) (e p)", e=2), so[:, 2, :]).then_inc(sm["sfin_out"], 16)
                sp.dma_start(ssm_im_s[l].rearrange("b (q e) p -> (b q) (e p)", e=2), so[:, 3, :]).then_inc(sm["sfin_out"], 16)
                wait(sp, l, "vs_ev", 1)
                sp.dma_start(conv_p[l, 0], nst[2:32, :]).then_inc(sm["vo_out"], 16)
                sp.dma_start(conv_s[l, :, TAPS - 2, :], nss[:, :]).then_inc(sm["vo_out"], 16)

                with sp.Fori(0, 3) as it:
                    branch_load(it, 0)
                    gate_load(it, 2)
                    gate_load(it, 3)
                    branch_load(it, 1)
                    for m in range(4, 8):
                        gate_load(it, m)
                branch_load(3, 0)
                gate_load(3, 2)
                gate_load(3, 3)
                branch_load(3, 1)
                gate_load(3, 4)
                gate_load(3, 5)
                section("out", 4, straight(0), src=wo)
                wait(sp, l, "kv_out", 32)
                wait(sp, l, "sfin_out", 64)
                wait(sp, l, "vo_out", 48)
                sp.sem_inc(entered["sp"], 1)

            yp = y_prompt[0].rearrange("(c i s) d -> s i c d", s=2, i=4)
            for i in range(4):
                sp.wait_ge(sm["fin_ev"], i + 1)
                for s in range(2):
                    sp.dma_start(yp[s, i], yrow[s * C:(s + 1) * C, i % 2, :]).then_inc(sm[f"fin_out{i}"], 16)
            sp.wait_ge(sm["fin_ev"], 5)
            sp.dma_start(y_sample[:, 0, :], ysr[:, :]).then_inc(sm["fin_out_s"], 16)
            for i in range(4):
                sp.wait_ge(sm[f"fin_out{i}"], 32)
            sp.wait_ge(sm["fin_out_s"], 16)

        @block.gpsimd
        def _(pool):
            pool.memset(ones[:, :], 1.0).then_inc(sm["consts"], 1)
            pool.memset(ident[:, :], 0.0).then_inc(sm["consts"], 1)
            pool.wait_ge(sm["consts"], 2)
            pool.affine_select(out=ident[:, :], in_=ident[:, :], compare_op=ALU.not_equal, fill=1.0, base=0,
                               pattern=[[-1, P]], channel_multiplier=1).then_inc(sm["consts"], 1)
            pool.sem_inc(w_staged_free, 2)

            with pool.Fori(0, LAYERS) as l:
                def low(slot, n):
                    pool.wait_ge(w_hi_done, n + 1)
                    pool.tensor_tensor(w_lo[:, slot, :], w_st[:, slot, :], w_hi[:, slot, :].bitcast(F32),
                                       ALU.subtract).then_inc(w_staged_free, 1)

                def pairs(name, first, count):
                    with pool.Fori(first, first + count) as it:
                        for k in range(2):
                            low(k, l * UNITS + unit[name] + it * 2 + k)

                def glu_v(i):
                    wait(pool, l, "val_ev", 2 * i + 2)
                    for a in range(2):
                        blk = vx[:, bass.ds(i, 1), 8 + 4 * a:12 + 4 * a, 4:4 + C].rearrange("p i b c -> p (i b) c")
                        pool.tensor_tensor(blk, blk, sg[:, i % 2, a, 0:4 * C].rearrange("p (b c) -> p b c", c=C), ALU.mult)
                    s = v_s[:, i, :].rearrange("p (a c) -> p a c", a=2)
                    pool.tensor_tensor(s, s, sg[:, i % 2, :, 4 * C:HC], ALU.mult).then_inc(sm["v_done"], 1)
                    wait(pool, l, "v_done", i + 1)
                    pool.sem_inc(sm["sg_free"], 1)

                pairs("q", 0, 2)
                pairs("u", 0, 2)
                pairs("v", 0, 2)
                glu_v(0)
                pairs("v", 2, 1)
                glu_v(1)
                pairs("zx", 0, 1)
                glu_v(2)
                pairs("v3", 3, 1)
                pairs("zx1", 1, 1)
                glu_v(3)
                pairs("za", 0, 2)
                pairs("zb", 0, 2)
                pairs("gates", 0, 12)
                pairs("out", 0, 4)

        @block.tensor
        def _(pe):
            def transpose(out, in_, n):
                return pe.transpose(out, in_, ident[0:n, 0:n])

            pe.wait_ge(sm["consts"], 3)
            pe.wait_ge(sm["x_in"], 48)
            for i in range(4):
                if i >= 2:
                    pe.wait_ge(sm["x_ev"], i - 1)
                for k in range(KT):
                    last = transpose(mp[:, 2 * (i % 2) + k // 4, (k % 4) * P:(k % 4 + 1) * P], xrow[:, i, k * P:(k + 1) * P], P)
                last.then_inc(sm["x_tr"], 1)
            pe.wait_ge(sm["x_ev"], 3)
            for k in range(KT):
                last = transpose(mp[:, 0, k * NB:(k + 1) * NB], xsrow[:, k * P:(k + 1) * P], NB)
            last.then_inc(sm["x_tr"], 1)
            pe.wait_ge(sm["mem_nrm"], 2)
            for m in range(2):
                if m == 0:
                    pe.wait_ge(sm["x_ev"], 4)
                else:
                    pe.wait_ge(sm["x_ev"], 5)
                for k in range(KT):
                    last = transpose(mp[:, 2 * (1 - m) + k // 4, (k % 4) * P:(k % 4 + 1) * P], mrow[:, m, k * P:(k + 1) * P], P)
                last.then_inc(sm["mem_tr"], 1)
            pe.wait_ge(sm["mem_ev"], 2)

            with pe.Fori(0, LAYERS) as l:
                pe.drain().then_inc(layer_left["pe"], 1)
                pe.wait_ge(layer_go, l + 1)

                def split_product(pair, use_n, slot, n, hi, lo):
                    pe.wait_ge(w_staged_free, n + 3)
                    wait(pe, l, f"acc_free{pair}", use_n + 1)
                    for k in range(KT):
                        for p, (w, x) in enumerate(((w_hi, hi), (w_lo, hi), (w_hi, lo))):
                            for a in range(2):
                                last = pe.matmul(acc_ps[pair][:, a, 0:HC], w[:, slot, k * P:(k + 1) * P], x[:, k, a, :],
                                                 start=(k == 0 and p == 0), stop=(k == KT - 1 and p == 2))
                    last.then_inc(acc_ready[pair], 1)

                def in_section(name, first, pairs):
                    pe.sem_inc(entered["pe"], 1)
                    with pe.Fori(first, first + pairs) as it:
                        for k in range(2):
                            split_product(k, it + use[name] // 2, k, l * UNITS + unit[name] + it * 2 + k, h_hi, h_lo)

                for k in range(KT):
                    wait(pe, l, "sq_done", k + 1)
                    for a in range(2):
                        last = pe.matmul(mp[:, a, 0:HC], ones[:, :], sq[:, k % 4, a, :], start=(k == 0), stop=(k == KT - 1))
                    last.then_inc(sm["sq_used"], 1)
                wait(pe, l, "dt_wide", 1)
                wait(pe, l, "p_in", 16 * 11)
                wait(pe, l, "c_in", 16 * 8)
                transpose(mp[:, 2, 0:88], prow[:, :], 88)
                transpose(mp[:, 2, P:P + TAPS * ET], cwrow[:, :], TAPS * ET)
                transpose(mp[0:2 * H, 2, 256:256 + Q], drow[:, :], Q)
                for ri in range(2):
                    for f in range(2):
                        last = transpose(mp[:, 3, (2 * ri + f) * P:(2 * ri + f + 1) * P], crow[:, ri, f, :], P)
                last.then_inc(sm["par_tr"], 1)
                wait(pe, l, "var_done", 1)
                wait(pe, l, "s_in", 32)
                for ri in range(2):
                    last = transpose(mp[:, 0, ri * P:(ri + 1) * P], srow[:, ri, :], P)
                last.then_inc(sm["s0_tr"], 1)
                wait(pe, l, "memg_done", 1)
                for i in range(8):
                    wait(pe, l, f"d_loaded{i % 2}", 16 * (i // 2 + 1))
                    if i % 4 == 0:
                        wait(pe, l, f"acc_free{i // 4}", 1)
                    for kk in range(2):
                        k = 2 * (i % 4) + kk
                        for m in range(2):
                            last = pe.matmul(acc_ps[i // 4][:, m, :], memg[:, k, m * P:(m + 1) * P],
                                             w_dir[:, i % 2, kk * E:(kk + 1) * E], start=(k == 0), stop=(k == KT - 1))
                    if i % 4 == 3:
                        last.then_inc(acc_ready[i // 4], 1)
                    else:
                        last.then_inc(sm["kv_used"], 1)
                wait(pe, l, "kv_ev", 1)
                wait(pe, l, "par_ev", 1)
                for hd in range(HEADS):
                    for m in range(2):
                        j = 2 * hd + m
                        last = transpose(mp[:, 2 + j // 4, (j % 4) * P:(j % 4 + 1) * P], ktok[:, m, hd * P:(hd + 1) * P], P)
                last.then_inc(sm["kT_tr"], 1)
                wait(pe, l, "h_done", 1)
                in_section("q", 0, 2)

                def scores(i):
                    if i < 2:
                        wait(pe, l, "q_ev", 4)
                        wait(pe, l, "kT_ev", 1)
                        wait(pe, l, "s0_ev", 1)
                        if i:
                            wait(pe, l, "qrow_ev", 1)
                            pe.sem_inc(entered["pe"], 1)
                    else:
                        wait(pe, l, "pT_ev", i - 1)
                    for hd in range(HEADS):
                        last = pe.matmul(mp[:, 2 * (i % 2) + hd // 2, (hd % 2) * MEM:(hd % 2 + 1) * MEM],
                                         q[:, hd, i // 2, (i % 2) * P:(i % 2 + 1) * P], kT[:, hd, :], start=True, stop=True)
                    last.then_inc(sm["sc_done"], 1)

                def turn_probabilities(i):
                    wait(pe, l, "p_norm", i + 1)
                    for hd in range(HEADS):
                        for m in range(2):
                            j = 2 * hd + m
                            last = transpose(mp[:, 2 * (i % 2) + j // 4, (j % 4) * P:(j % 4 + 1) * P],
                                             pr[:, i % 2, hd, m * P:(m + 1) * P], P)
                    last.then_inc(sm["pT_tr"], 1)

                scores(0)
                wait(pe, l, "qs_done", 1)
                for hd in range(HEADS):
                    last = transpose(mp[0:NB, 2, hd * P:(hd + 1) * P], qs[:, hd, :], P)
                last.then_inc(sm["qrow_tr"], 1)
                scores(1)
                in_section("u", 0, 2)
                turn_probabilities(0)
                turn_probabilities(1)
                scores(2)
                scores(3)
                in_section("v", 0, 1)
                turn_probabilities(2)
                turn_probabilities(3)
                for hd in range(HEADS):
                    wait(pe, l, "pT_ev", 3 if hd < 2 else 4)
                    if hd == 0:
                        wait(pe, l, "pT_ev", 4)
                    for m in range(2):
                        last = pe.matmul(mp[:, hd, :], vtok[:, m, hd * P:(hd + 1) * P], pT[:, hd, m, :], start=(m == 0), stop=(m == 1))
                last.then_inc(sm["pv_done"], 1)

                def spread(first):
                    for b in range(first, first + 4):
                        if b >= 4:
                            wait(pe, l, "kq_done", b - 3)
                        pe.matmul(mp[:, b % 4, :], ident[0:NB, b:b + 1].to_broadcast([NB, P]), qrow[:, :],
                                  start=True, stop=True).then_inc(sm["bc_done"], 1)

                wait(pe, l, "pv_ev", 1)
                pe.sem_inc(entered["pe"], 1)
                spread(0)
                in_section("v", 1, 1)
                spread(4)
                in_section("v", 2, 1)
                wait(pe, l, "kq_done", NB)
                for m in range(2):
                    last = transpose(mp[0:32, 0, m * P:(m + 1) * P], sK[:, m, :], P)
                last.then_inc(sm["scs_done"], 1)
                in_section("zx", 0, 1)
                wait(pe, l, "ps_norm", 1)
                pe.sem_inc(entered["pe"], 1)
                for m in range(2):
                    last = transpose(mp[:, 3, m * 32:(m + 1) * 32], ps[:, m * P:(m + 1) * P], 32)
                last.then_inc(sm["psT_tr"], 1)
                wait(pe, l, "pm_ev", 1)
                for b in range(NB):
                    wait(pe, l, f"kb_in{b % 4}", 16 * (2 + b // 4 + 1))
                    for m in range(2):
                        last = pe.matmul(mp[0:32, 2, :], pm[:, m, b, :], kb[:, b % 4, m, :],
                                         start=(b == 0 and m == 0), stop=(b == NB - 1 and m == 1))
                    last.then_inc(sm["pvs_done"], 1)
                wait(pe, l, "oxs_ev", 1)
                pe.sem_inc(entered["pe"], 1)
                for hd in range(HEADS):
                    last = transpose(mp[:, 3, hd * 32:(hd + 1) * 32], oxs[:, hd * P:(hd + 1) * P], 32)
                last.then_inc(sm["oxT_tr"], 1)

                def state_inputs(f):
                    wait(pe, l, "wt_done", f + 1)
                    wait(pe, l, *(("k_free", 1), ("y_ev", 4))[f])
                    for ri in range(2):
                        for r in range(QH):
                            j = ri * QH + r
                            last = transpose(mp[:, j // 4, (j % 4) * P:(j % 4 + 1) * P], wt[:, ri, r, :], P)
                    last.then_inc(sm["w_tr"], 1)
                    wait(pe, l, "wl_ev", f + 1)
                    wait(pe, l, "U_in", 16 * 12)
                    for e in range(2):
                        for r in range(QH):
                            last = pe.matmul(mp[:, 2 * e + r // 4, (r % 4) * YC:(r % 4 + 1) * YC],
                                             wl[:, r, e, :], U[:, f * QH + r, e, NB:UC], start=True, stop=True)
                    last.then_inc(sm["s_done"], 1)

                def lag_matrices(f):
                    wait(pe, l, "V_done", f + 1)
                    wait(pe, l, *(("ox_done", 1), ("s_free", 2))[f])
                    pe.sem_inc(entered["pe"], 1)
                    for r in range(QH):
                        for ri in range(2):
                            last = pe.matmul(mp[0:2 * H, r // 4, (r % 4) * P:(r % 4 + 1) * P],
                                             bd[:, ri, f * QH + r, :, :].rearrange("p e h -> p (e h)"),
                                             V[:, ri, r, 0:T, :].rearrange("p t h -> p (t h)"),
                                             start=(ri == 0), stop=(ri == 1))
                    last.then_inc(sm["k_done"], 1)

                def outputs(f):
                    wait(pe, l, "m_in", 128 * (f + 1))
                    wait(pe, l, "x_done", f + 1)
                    wait(pe, l, *(("s_free", 1), ("k_free", 2))[f])
                    for e in range(2):
                        for r in range(QH):
                            out = mp[:, 2 * e + r // 4, (r % 4) * YC:(r % 4 + 1) * YC]
                            pe.matmul(out, Mt[:, 2 * r + e, :], U[:, f * QH + r, e, 0:YC], start=True, stop=False)
                            for ri in range(2):
                                last = pe.matmul(out, V[e * S:(e + 1) * S, ri, r, 1:T + 1, :].rearrange("p t h -> p (t h)"),
                                                 X[e * S:(e + 1) * S, ri, r, 0:YC], start=False, stop=(ri == 1))
                    last.then_inc(sm["y_done"], 1)

                lag_matrices(0)
                state_inputs(0)
                in_section("v3", 3, 1)
                in_section("zx1", 1, 1)
                outputs(0)
                state_inputs(1)
                lag_matrices(1)
                in_section("za", 0, 2)
                outputs(1)
                wait(pe, l, "y_ev", 8)
                wait(pe, l, "sn_done", 1)
                for ri in range(2):
                    transpose(mp[0:Q, 0, ri * P:(ri + 1) * P], sf[:, ri, :], P)
                for ri in range(2):
                    last = transpose(mp[:, 0, (2 + ri) * P:(3 + ri) * P], sn[:, ri, :, :].rearrange("p b q -> p (b q)"), P)
                last.then_inc(sm["sfin_tr"], 1)
                wait(pe, l, "st_in", 32)
                for r in range(2):
                    for i in range(ET):
                        last = transpose(mp[:, 1 + r, i * 120:(i + 1) * 120], crw[:, r, i * P:(i + 1) * P], 120)
                last.then_inc(sm["st_tr"], 1)
                wait(pe, l, "v_last_done", 4)
                for i in range(ET):
                    last = transpose(mp[0:32, 3, i * P:(i + 1) * P], v_last[:, i, :], P)
                last.then_inc(sm["vs_tr"], 1)
                wait(pe, l, "sfin_ev", 1)
                for i in range(ET):
                    last = transpose(mp[0:NB, 0, i * P:(i + 1) * P], v_s[:, i, :], P)
                last.then_inc(sm["vs_tr"], 1)
                in_section("zb", 0, 1)
                wait(pe, l, "acc_done", ET)
                wait(pe, l, "vs_ev", 1)
                for i in range(ET):
                    for a in range(2):
                        last = pe.matmul(mp[:, a, 0:HC], ones[:, :], acc(i)[:, a, :], start=(i == 0), stop=(i == ET - 1))
                last.then_inc(sm["mean_done"], 1)
                in_section("zb", 1, 1)
                for i in range(ET):
                    wait(pe, l, "lsq_done", i + 1)
                    for a in range(2):
                        last = pe.matmul(mp[:, 2 + a, 0:HC], ones[:, :], lsq(i)[:, a, :], start=(i == 0), stop=(i == ET - 1))
                last.then_inc(sm["lsq_used"], 1)

                wait(pe, l, "y_in", 16)
                for g in range(2):
                    wait(pe, l, f"d_loaded{g}", 80)
                    for j in range(2):
                        wait(pe, l, f"acc_free{j}", use["glu"] // 2 + g + 1)
                        for k in range(ET):
                            for a in range(2):
                                last = pe.matmul(acc_ps[j][:, a, 0:HC], w_dir[:, g, k * 2 * P + j * P:k * 2 * P + (j + 1) * P],
                                                 u[:, k, a, :], start=(k == 0), stop=(k == ET - 1))
                        last.then_inc(acc_ready[j], 1)
                pe.sem_inc(entered["pe"], 1)
                with pe.Fori(0, 4) as it:
                    for jj in range(2):
                        for x in range(3):
                            m = jj * 3 + x
                            un = it * 6 + use["gates"] // 2 + m
                            split_product(0, un, m % 2, l * UNITS + unit["gates"] + it * 6 + m, h_hi, h_lo)
                            if x == 0:
                                wait(pe, l, f"d_loaded{jj}", it * 48 + 80 + 48)
                            wait(pe, l, ("br_a_done", "br_b_done", "br_x_done")[x], (4, 4, 1)[x])
                            wait(pe, l, "acc_free1", un + 1)
                            for k in range(ET):
                                for a in range(2):
                                    last = pe.matmul(acc_ps[1][:, a, 0:HC], w_dir[:, jj, (x * 4 + k) * P:(x * 4 + k + 1) * P],
                                                     br[:, x, k, a, :], start=(k == 0), stop=(k == ET - 1))
                            last.then_inc(acc_ready[1], 1)
                wait(pe, l, "m_done", 8)
                pe.sem_inc(entered["pe"], 1)
                with pe.Fori(0, 4) as it:
                    for k in range(2):
                        split_product(k, it + use["out"] // 2, k, l * UNITS + unit["out"] + it * 2 + k, m_hi, m_lo)

            for k in range(KT):
                pe.wait_ge(sm["fin_sq"], k + 1)
                for a in range(2):
                    last = pe.matmul(mp[:, a, 0:HC], ones[:, :], sq[:, k % 4, a, :], start=(k == 0), stop=(k == KT - 1))
                last.then_inc(sm["fin_used"], 1)
            pe.wait_ge(sm["fin_y"], KT + 1)
            for i in range(4):
                if i < 2:
                    pe.wait_ge(sm["fin_var"], 1)
                else:
                    pe.wait_ge(sm["fin_ev"], i - 1)
                for k in range(KT):
                    last = transpose(mp[:, 2 * (i % 2) + k // 4, (k % 4) * P:(k % 4 + 1) * P],
                                     xT[:, k, i // 2, (i % 2) * P:(i % 2 + 1) * P], P)
                last.then_inc(sm["fin_tr"], 1)
            pe.wait_ge(sm["fin_ev"], 3)
            for k in range(KT):
                last = transpose(mp[0:NB, k // 4, (k % 4) * P:(k % 4 + 1) * P], xsc[:, k, :], P)
            last.then_inc(sm["fin_tr"], 1)

        @block.scalar
        def _(act):
            steps = Steps(act, act_steps)
            act.wait_ge(sm["mem_in"], 16)
            for m in range(2):
                steps.run(act.activation(memn0[:, 0:4, :].rearrange("p k m -> p (k m)"), mrow[:, m, :], ACT.Square,
                                         accum_out=stat[:, m:m + 1]))
            act.sem_inc(sm["mem_sq"], 1)
            act.wait_ge(sm["mem_var"], 1)
            act.activation(stat[:, 2:4], stat[:, 4:6], ACT.Sqrt).then_inc(sm["mem_rt"], 1)
            for i in range(4):
                act.wait_ge(sm["x_tr"], i + 1)
                act.activation(xT[:, :, i // 2, (i % 2) * P:(i % 2 + 1) * P],
                               mp[:, 2 * (i % 2):2 * (i % 2) + 2, :].rearrange("p b (k c) -> p (b k) c", c=P), ACT.Copy).then_inc(sm["x_ev"], 1)
            act.wait_ge(sm["x_tr"], 5)
            act.activation(xT[:, :, :, 4 * C:HC], mp[:, 0, 0:KT * NB].rearrange("p (k a c) -> p k a c", a=2, c=4), ACT.Copy).then_inc(sm["x_ev"], 1)
            for m in range(2):
                act.wait_ge(sm["mem_tr"], m + 1)
                act.activation(memn0[:, :, m * P:(m + 1) * P],
                               mp[:, 2 * (1 - m):2 * (1 - m) + 2, :].rearrange("p b (k c) -> p (b k) c", c=P), ACT.Copy).then_inc(sm["mem_ev"], 1)
            act.wait_ge(sm["mem_ev"], 2)
            steps.clear()

            with act.Fori(0, LAYERS) as l:
                act.drain().then_inc(layer_left["act"], 1)
                act.wait_ge(layer_go, l + 1)

                def high(slot, loads):
                    act.wait_ge(w_loaded[slot], loads * 16)
                    act.copy(w_hi[:, slot, :], w_st[:, slot, :]).then_inc(w_hi_done, 1)

                def section(name, first, pairs, evac, bump=None):
                    with act.Fori(first, first + pairs) as it:
                        for k in range(2):
                            wait(act, l, f"acc_ready{k}", it + use[name] // 2 + 1)
                            high(k, l * (UNITS // 2) + unit[name] // 2 + it + 2)
                            evac(it, k)

                high(0, l * (UNITS // 2) + 1)
                high(1, l * (UNITS // 2) + 1)
                for k in range(KT):
                    if k >= 4:
                        wait(act, l, "sq_used", k - 3)
                    act.activation(sq[:, k % 4, :, :], xT[:, k, :, :], ACT.Square).then_inc(sm["sq_done"], 1)
                wait(act, l, "var_done", 1)
                act.activation(rs[:, :, :], rs[:, :, :], ACT.Sqrt).then_inc(sm["rstd_done"], 1)
                for k in range(KT):
                    wait(act, l, "ht_done", k + 1)
                    act.copy(h_hi[:, k, :, :], ht[:, k % 2, :, :]).then_inc(sm["hhi_done"], 1)
                wait(act, l, "par_ev", 1)
                act.activation(tiny[:, 0, :], vec[:, 64:80], ACT.Exp).then_inc(sm["dt_exp"], 1)
                wait(act, l, "sin_arg", 1)
                act.activation(tiny[:, 3, :], tiny[:, 1, :], ACT.Exp)
                act.activation(tiny[:, 7:9, :], tiny[:, 5:7, :], ACT.Sin).then_inc(sm["par_act"], 1)
                wait(act, l, "acc_ready0", 1)
                act.copy(ktok[:, :, :], acc_ps[0][:, :, :]).then_inc(sm["kv_ev"], 1)
                wait(act, l, "kv_ev", 1)
                act.sem_inc(acc_free[0], 1)
                wait(act, l, "acc_ready1", 1)
                act.copy(vtok[:, :, :], acc_ps[1][:, :, :]).then_inc(sm["kv_ev"], 1)
                wait(act, l, "kv_ev", 2)
                act.sem_inc(acc_free[1], 1)
                wait(act, l, "kT_tr", 1)
                act.copy(kT[:, :, :].rearrange("p h m -> p (h m)"), mp[:, 2:4, :].rearrange("p b c -> p (b c)")).then_inc(sm["kT_ev"], 1)

                def tile(ap, i):
                    return ap[:, bass.ds(i, 1), :, :].rearrange("p i a c -> p (i a) c")

                def to_q(it, k):
                    act.copy(tile(q, it * 2 + k), acc_ps[k][:, :, 0:HC]).then_inc(acc_free[k], 1)

                section("q", 0, 2, to_q)
                wait(act, l, "acc_free1", use["u"] // 2 + 1)
                act.sem_inc(sm["q_ev"], 4)

                def exps(i):
                    wait(act, l, "nb_done", i + 1)
                    if i >= 2:
                        wait(act, l, "pT_tr", i - 1)
                    for hd in range(HEADS):
                        last = act.activation(pr[:, i % 2, hd, :], mp[:, 2 * (i % 2) + hd // 2, (hd % 2) * MEM:(hd % 2 + 1) * MEM],
                                              ACT.Exp, bias=stat[:, 16 + 4 * i + hd:17 + 4 * i + hd], scale=SCALE,
                                              accum_out=stat[:, 32 + 4 * i + hd:33 + 4 * i + hd])
                    last.then_inc(sm["exp_done"], 1)

                def keep_probabilities(i):
                    wait(act, l, "pT_tr", i + 1)
                    act.copy(pT[:, :, :, i * P:(i + 1) * P],
                             mp[:, 2 * (i % 2):2 * (i % 2) + 2, :].rearrange("p b (n c) -> p (b n) c", c=P)
                             .rearrange("p (h m) c -> p h m c", m=2)).then_inc(sm["pT_ev"], 1)

                wait(act, l, "qrow_tr", 1)
                act.copy(qrow[:, :], mp[0:NB, 2, :]).then_inc(sm["qrow_ev"], 1)
                exps(0)
                exps(1)
                wait(act, l, "s0_ev", 1)
                wait(act, l, "par_ev", 1)

                def to_u(it, k):
                    act.copy(tile(u, it * 2 + k), acc_ps[k][:, :, 0:HC]).then_inc(acc_free[k], 1)

                section("u", 0, 2, to_u)
                wait(act, l, "acc_free1", use["v"] // 2 + 1)
                act.sem_inc(sm["u_ev"], 4)
                keep_probabilities(0)
                keep_probabilities(1)
                exps(2)
                exps(3)

                def to_v(i):
                    name = "v" if i < 3 else "v3"
                    base = l * (UNITS // 2) + unit[name] // 2 + i + 2
                    wait(act, l, "acc_ready0", use[name] // 2 + i + 1)
                    high(0, base)
                    wait(act, l, "sg_free", i + 1)
                    act.activation(sg[:, i % 2, :, :], acc_ps[0][:, :, 0:HC], ACT.Sigmoid).then_inc(sm["val_ev"], 1)
                    wait(act, l, "val_ev", 2 * i + 1)
                    act.sem_inc(acc_free[0], 1)
                    wait(act, l, "acc_ready1", use[name] // 2 + i + 1)
                    high(1, base)
                    for a in range(2):
                        act.copy(vx[:, i, 8 + 4 * a:12 + 4 * a, 4:4 + C], acc_ps[1][:, a, 0:4 * C].rearrange("p (b c) -> p b c", c=C))
                    act.copy(v_s[:, i, :].rearrange("p (a c) -> p a c", a=2), acc_ps[1][:, :, 4 * C:HC]).then_inc(sm["val_ev"], 1)
                    wait(act, l, "val_ev", 2 * i + 2)
                    act.sem_inc(acc_free[1], 1)

                to_v(0)
                keep_probabilities(2)
                keep_probabilities(3)
                wait(act, l, "pv_done", 1)
                act.copy(g3(q), mp[:, :, :].rearrange("p h (a c) -> p h a c", a=2)).then_inc(sm["pv_ev"], 1)
                to_v(1)
                to_v(2)
                wait(act, l, "nbs_done", 1)
                act.activation(ps[:, :], mp[0:32, 0, 0:MEM], ACT.Exp, bias=stat[0:32, 48:49], scale=SCALE,
                               accum_out=stat[0:32, 49:50]).then_inc(sm["exps_done"], 1)

                def to_z(x):
                    def evac(it, k):
                        act.activation(tile(z[:, x, :, :, :], it * 2 + k), acc_ps[k][:, :, 0:HC], ACT.Silu).then_inc(acc_free[k], 1)
                    return evac

                section("zx", 0, 1, to_z(2))
                wait(act, l, "pvs_done", NB)
                act.copy(oxs[:, :], mp[0:32, 2, :]).then_inc(sm["oxs_ev"], 1)

                def turned_inputs(f):
                    wait(act, l, "w_tr", f + 1)
                    for ri in range(2):
                        last = act.copy(wl[:, :, :, ri * S:(ri + 1) * S].rearrange("p q e s -> p (q e) s"),
                                        mp[:, 2 * ri:2 * ri + 2, :].rearrange("p b (x s) -> p (b x) s", s=S))
                    last.then_inc(sm["wl_ev"], 1)

                def gelu_outputs(f):
                    wait(act, l, "y_done", f + 1)
                    for e in range(2):
                        for b in range(2):
                            act.activation(U[:, f * QH + 4 * b:f * QH + 4 * b + 4, e, 0:YC],
                                           mp[:, 2 * e + b, 0:4 * YC].rearrange("p (q c) -> p q c", c=YC),
                                           ACT.Gelu_apprx_tanh).then_inc(sm["y_ev"], 1)

                turned_inputs(0)
                to_v(3)
                section("zx1", 1, 1, to_z(2))
                gelu_outputs(0)
                turned_inputs(1)
                wait(act, l, "k_free", 2)
                section("za", 0, 2, to_z(0))
                gelu_outputs(1)
                section("zb", 0, 1, to_z(1))
                for i in range(ET):
                    wait(act, l, "cent_done", i + 1)
                    act.activation(lsq(i), acc(i), ACT.Square).then_inc(sm["lsq_done"], 1)
                section("zb", 1, 1, to_z(1))
                wait(act, l, "lvar_done", 1)
                act.activation(lst[:, :, :], lst[:, :, :], ACT.Sqrt).then_inc(sm["lrstd_done"], 1)
                wait(act, l, "acc_free1", use["glu"] // 2 + 1)
                act.sem_inc(sm["z_ev"], 1)

                for i in range(ET):
                    wait(act, l, f"acc_ready{i % 2}", use["glu"] // 2 + i // 2 + 1)
                    wait(act, l, "sg_free", 4 + i + 1)
                    act.activation(sg[:, i % 2, :, :], acc_ps[i % 2][:, :, 0:HC], ACT.Sigmoid,
                                   bias=vec[:, 16 + i:17 + i]).then_inc(sm["glu_sg"], 1)
                    wait(act, l, "glu_sg", i + 1)
                    act.sem_inc(acc_free[i % 2], 1)
                for i in range(ET):
                    wait(act, l, "ln_done", i + 1)
                    act.activation(acc(i), acc(i), ACT.Silu, bias=vec[:, 28 + i:29 + i]).then_inc(sm["ln_silu"], 1)
                with act.Fori(0, 4) as it:
                    for m in range(6):
                        wait(act, l, "acc_ready0", it * 6 + use["gates"] // 2 + m + 1)
                        high(m % 2, l * (UNITS // 2) + unit["gates"] // 2 + it * 3 + m // 2 + 2)
                        wait(act, l, "sg_free", it * 6 + 8 + m + 1)
                        act.activation(sg[:, m % 2, :, :], acc_ps[0][:, :, 0:HC], ACT.Sigmoid).then_inc(sm["gate_sg"], 1)
                        wait(act, l, "gate_sg", it * 6 + m + 1)
                        act.sem_inc(acc_free[0], 1)
                with act.Fori(0, 3) as it:
                    for k in range(2):
                        wait(act, l, f"acc_ready{k}", it + use["out"] // 2 + 1)
                        high(k, l * (UNITS // 2) + unit["out"] // 2 + it + 2)

            act.wait_ge(sm["x_sum"], 8 * LAYERS)
            for k in range(KT):
                if k >= 4:
                    act.wait_ge(sm["fin_used"], k - 3)
                act.activation(sq[:, k % 4, :, :], xT[:, k, :, :], ACT.Square).then_inc(sm["fin_sq"], 1)
            act.wait_ge(sm["fin_var"], 1)
            act.activation(rs[:, :, :], rs[:, :, :], ACT.Sqrt).then_inc(sm["fin_rt"], 1)
            for i in range(4):
                act.wait_ge(sm["fin_tr"], i + 1)
                if i >= 2:
                    act.wait_ge(sm[f"fin_out{i - 2}"], 32)
                act.copy(yrow[:, i % 2, :], mp[:, 2 * (i % 2):2 * (i % 2) + 2, :].rearrange("p b c -> p (b c)")).then_inc(sm["fin_ev"], 1)
            act.wait_ge(sm["fin_tr"], 5)
            act.copy(ysr[:, :], mp[0:NB, 0:2, :].rearrange("p b c -> p (b c)")).then_inc(sm["fin_ev"], 1)

        @block.vector
        def _(dve):
            steps = Steps(dve, dve_steps)
            run = steps.run

            def tt(out, a, b, op, behind=0):
                run(dve.tensor_tensor(out, a, b, op), behind)

            def ts(out, a, s1, s2, op0, op1, behind=0):
                run(dve.tensor_scalar(out, a, s1, s2, op0, op1), behind)

            def stt(out, a, s, b, op0, op1, behind=0):
                run(dve.scalar_tensor_tensor(out=out, in0=a, scalar=s, in1=b, op0=op0, op1=op1), behind)

            def cmul(dr, di, xr, xi, yr, yi, a, b):
                tt(a, xr, yr, ALU.mult)
                tt(b, xi, yi, ALU.mult)
                tt(b, a, b, ALU.subtract)
                tt(a, xr, yi, ALU.mult)
                tt(di, xi, yr, ALU.mult)
                tt(di, a, di, ALU.add)
                run(dve.tensor_copy(dr, b))

            dve.wait_ge(sm["mem_sq"], 1)
            ts(stat[:, 6:8], stat[:, 0:2], 1.0 / D, EPS, ALU.mult, ALU.add)
            dve.reciprocal(stat[:, 4:6], stat[:, 6:8]).then_inc(sm["mem_var"], 1)
            dve.wait_ge(sm["mem_rt"], 1)
            for m in range(2):
                dve.tensor_scalar(mrow[:, m, :], mrow[:, m, :], stat[:, 2 + m:3 + m], None, ALU.mult).then_inc(sm["mem_nrm"], 1)
            dve.wait_ge(sm["mem_nrm"], 2)
            dve.wait_ge(sm["consts"], 3)
            tt(eye2[:, :], ident[0:2 * H, 0:H], ident[0:2 * H, H:2 * H], ALU.add)
            steps.clear()

            for i in range(2):
                dve.sem_inc(acc_free[i], 1)
            dve.sem_inc(sm["sg_free"], 2)

            with dve.Fori(0, LAYERS) as l:
                for e in layer_left:
                    dve.wait_ge(layer_left[e], l + 1)
                    dve.sem_inc(layers_begun, 1)
                dve.sem_inc(layer_go, 1)

                wait(dve, l, "dt_in", 16)
                dve.tensor_copy(prow[64:80, :].rearrange("q (e p) -> q e p", e=2),
                                dtrow[64:80, :].unsqueeze(2).to_broadcast([16, 2, S])).then_inc(sm["dt_wide"], 1)
                wait(dve, l, "sq_used", KT)
                ts(rs[:, :, :], mp[:, 0:2, 0:HC], 1.0 / D, EPS, ALU.mult, ALU.add)
                dve.reciprocal(rs[:, :, :], rs[:, :, :]).then_inc(sm["var_done"], 1)
                wait(dve, l, "par_tr", 1)
                run(dve.tensor_copy(vec[:, :], mp[:, 2, 0:88]))
                run(dve.tensor_copy(cw[:, :], mp[:, 2, P:P + TAPS * ET]))
                run(dve.tensor_copy(dcol[:, :], mp[0:2 * H, 2, 256:256 + Q]))
                dve.tensor_copy(cT[:, :, :, :].rearrange("p a q h -> p (a q h)"), mp[:, 3, :]).then_inc(sm["par_ev"], 1)
                wait(dve, l, "par_ev", 1)
                wait(dve, l, "mg_in", 16)
                for k in range(KT):
                    run(dve.tensor_scalar(memg[:, k, :], memn[:, k, :], vec[:, 56 + k:57 + k], None, ALU.mult))
                dve.sem_inc(sm["memg_done"], 1)
                wait(dve, l, "rstd_done", 1)

                def h_low(k):
                    wait(dve, l, "hhi_done", k + 1)
                    run(dve.tensor_tensor(h_lo[:, k, :, :], ht[:, k % 2, :, :], h_hi[:, k, :, :].bitcast(F32), ALU.subtract))

                for k in range(KT):
                    if k >= 2:
                        h_low(k - 2)
                    stt(ht[:, k % 2, :, :], xT[:, k, :, :], vec[:, 48 + k:49 + k], rs[:, :, :], ALU.mult, ALU.mult)
                    dve.sem_inc(sm["ht_done"], 1)
                h_low(KT - 2)
                h_low(KT - 1)
                dve.sem_inc(sm["h_done"], 1)
                wait(dve, l, "s0_tr", 1)
                dve.tensor_copy(s0[:, :, :, :].rearrange("p a b q -> p (a b q)"), mp[:, 0, 0:2 * P]).then_inc(sm["s0_ev"], 1)
                wait(dve, l, "s0_ev", 1)

                are, aim = vec[:, 0:16], vec[:, 32:48]
                wait(dve, l, "dt_exp", 1)
                tt(tiny[:, 1, :], are, tiny[:, 0, :], ALU.mult)
                tt(tiny[:, 2, :], aim, tiny[:, 0, :], ALU.mult)
                ts(tiny[:, 4, :], tiny[:, 2, :], 1.0 / TWO_PI, ROUND, ALU.mult, ALU.add)
                run(dve.tensor_scalar(tiny[:, 4, :], tiny[:, 4, :], ROUND, None, ALU.subtract))
                stt(tiny[:, 5, :], tiny[:, 4, :], -PI2_HI, tiny[:, 2, :], ALU.mult, ALU.add)
                stt(tiny[:, 5, :], tiny[:, 4, :], -PI2_MID, tiny[:, 5, :], ALU.mult, ALU.add)
                stt(tiny[:, 5, :], tiny[:, 4, :], -PI2_LO, tiny[:, 5, :], ALU.mult, ALU.add)
                ts(tiny[:, 5, :], tiny[:, 5, :], PI_BELOW, -PI_BELOW, ALU.min, ALU.max)
                run(dve.tensor_scalar(tiny[:, 6, :], tiny[:, 5, :], -1.0, None, ALU.mult))
                tt(tiny[:, 6, :], tiny[:, 6, :], tiny[:, 5, :], ALU.min)
                run(dve.tensor_scalar(tiny[:, 6, :], tiny[:, 6, :], TWO_PI / 4, None, ALU.add))
                dve.sem_inc(sm["sin_arg"], 1)
                wait(dve, l, "par_act", 1)
                run(dve.memset(pw[:, 0, :, 0], 1.0))
                run(dve.memset(pw[:, 1, :, 0], 0.0))
                tt(pw[:, 0, :, 1], tiny[:, 3, :], tiny[:, 8, :], ALU.mult)
                tt(pw[:, 1, :, 1], tiny[:, 3, :], tiny[:, 7, :], ALU.mult)
                tt(tiny[:, 5, :], are, are, ALU.mult)
                tt(tiny[:, 6, :], aim, aim, ALU.mult)
                tt(tiny[:, 5, :], tiny[:, 5, :], tiny[:, 6, :], ALU.add)
                run(dve.reciprocal(tiny[:, 5, :], tiny[:, 5, :]))
                run(dve.tensor_scalar(tiny[:, 6, :], pw[:, 0, :, 1], 1.0, None, ALU.subtract))
                tt(tiny[:, 7, :], tiny[:, 6, :], are, ALU.mult)
                tt(tiny[:, 8, :], pw[:, 1, :, 1], aim, ALU.mult)
                tt(tiny[:, 7, :], tiny[:, 7, :], tiny[:, 8, :], ALU.add)
                tt(tiny[:, 9, :], tiny[:, 7, :], tiny[:, 5, :], ALU.mult)
                tt(tiny[:, 7, :], pw[:, 1, :, 1], are, ALU.mult)
                tt(tiny[:, 8, :], tiny[:, 6, :], aim, ALU.mult)
                tt(tiny[:, 7, :], tiny[:, 7, :], tiny[:, 8, :], ALU.subtract)
                tt(tiny[:, 10, :], tiny[:, 7, :], tiny[:, 5, :], ALU.mult)
                for lo in (1, 2, 4):
                    a = tiny[:, 0:lo, :].rearrange("p k q -> p q k")
                    b = tiny[:, 4:4 + lo, :].rearrange("p k q -> p q k")
                    cmul(pw[:, 0, :, lo + 1:2 * lo + 1], pw[:, 1, :, lo + 1:2 * lo + 1], pw[:, 0, :, 1:lo + 1], pw[:, 1, :, 1:lo + 1],
                         pw[:, 0, :, lo:lo + 1].to_broadcast([P, Q, lo]), pw[:, 1, :, lo:lo + 1].to_broadcast([P, Q, lo]), a, b)
                run(dve.tensor_copy(lv[:, 0, :, :], pw[:, :, :, T]))
                for k in range(5):
                    cmul(lv[:, k + 1, 0, :], lv[:, k + 1, 1, :], lv[:, k, 0, :], lv[:, k, 1, :], lv[:, k, 0, :], lv[:, k, 1, :],
                         tiny[:, 0, :], tiny[:, 4, :])

                def scores_max(i):
                    wait(dve, l, "sc_done", i + 1)
                    run(dve.tensor_reduce(stat[:, 4 * i:4 * i + 4],
                                          mp[:, 2 * (i % 2):2 * (i % 2) + 2, :].rearrange("p b (h m) -> p (b h) m", m=MEM), op=ALU.max, axis=AX.X))
                    run(dve.tensor_scalar(stat[:, 16 + 4 * i:20 + 4 * i], stat[:, 4 * i:4 * i + 4], -SCALE, None, ALU.mult))
                    dve.sem_inc(sm["nb_done"], 1)

                def probabilities(i):
                    wait(dve, l, "exp_done", i + 1)
                    run(dve.reciprocal(stat[:, 52:56], stat[:, 32 + 4 * i:36 + 4 * i]))
                    tt(pr[:, i % 2, :, :], pr[:, i % 2, :, :], stat[:, 52:56].unsqueeze(2).to_broadcast([P, HEADS, MEM]), ALU.mult)
                    dve.sem_inc(sm["p_norm"], 1)

                wait(dve, l, "q_ev", 4)
                run(dve.tensor_copy(qs[:, :, :].rearrange("p h (a b) -> p h a b", a=2), q[:, :, :, 4 * C:HC]))
                dve.sem_inc(sm["qs_done"], 1)
                scores_max(0)
                scores_max(1)
                probabilities(0)
                probabilities(1)
                wait(dve, l, "b_in", 64)
                bc = [tiny[:, 9 + i, :].unsqueeze(2).to_broadcast([P, Q, H]) for i in range(2)]
                wtmp = wt[:, :, :, :].rearrange("p a q s -> p (a q s)")
                ta, tb = (wtmp[:, i * 256:(i + 1) * 256].rearrange("p (q h) -> p q h", h=H) for i in range(2))
                cmul(bb[:, 0, :, :], bb[:, 1, :, :], bT[:, 0, :, :], bT[:, 1, :, :], bc[0], bc[1], ta, tb)
                run(dve.memset(bd[:, :, :, :, :], 0.0))
                for e in range(2):
                    run(dve.tensor_copy(bd[e * S:(e + 1) * S, :, :, e, :], bb[e * S:(e + 1) * S, :, :, :]))
                scores_max(2)
                scores_max(3)
                probabilities(2)
                probabilities(3)

                def input_matrices(f):
                    if f:
                        wait(dve, l, "w_tr", 1)
                    qs = slice(f * QH, (f + 1) * QH)
                    o = [wt[:, i, :, :].rearrange("p q (s h) -> p q s h", h=H) for i in range(2)]
                    p = [pw[:, i, qs, T - 1::-1].unsqueeze(3).to_broadcast([P, QH, T, H]) for i in range(2)]
                    b = [bb[:, i, qs, :].unsqueeze(2).to_broadcast([P, QH, T, H]) for i in range(2)]
                    ta = t1[:, 0:QH * T * H].rearrange("p (q s h) -> p q s h", q=QH, h=H)
                    tb = t2[:, 0:QH * T * H].rearrange("p (q s h) -> p q s h", q=QH, h=H)
                    tt(o[0], p[0], b[0], ALU.mult, behind=1)
                    tt(ta, p[1], b[1], ALU.mult, behind=2)
                    tt(o[1], p[0], b[1], ALU.mult, behind=1)
                    tt(tb, p[1], b[0], ALU.mult, behind=2)
                    tt(o[0], o[0], ta, ALU.subtract, behind=1)
                    tt(o[1], o[1], tb, ALU.add)
                    dve.sem_inc(sm["wt_done"], 1)

                def output_matrices(f):
                    if f:
                        wait(dve, l, "y_done", 1)
                    qs = slice(f * QH, (f + 1) * QH)
                    p = [pw[:, i, qs, :].unsqueeze(3).to_broadcast([P, QH, T + 1, H]) for i in range(2)]
                    c = [cT[:, i, qs, :].unsqueeze(2).to_broadcast([P, QH, T + 1, H]) for i in range(2)]
                    ta = t1[:, :].rearrange("p (q s h) -> p q s h", q=QH, h=H)
                    tb = t2[:, :].rearrange("p (q s h) -> p q s h", q=QH, h=H)
                    tt(V[:, 0], p[0], c[0], ALU.mult, behind=1)
                    tt(ta, p[1], c[1], ALU.mult, behind=2)
                    tt(V[:, 1], p[0], c[1], ALU.mult, behind=1)
                    tt(tb, p[1], c[0], ALU.mult, behind=2)
                    tt(V[:, 0], V[:, 0], ta, ALU.subtract, behind=1)
                    stt(V[:, 1].rearrange("p q s h -> p (q s h)"), V[:, 1].rearrange("p q s h -> p (q s h)"), -1.0, t2[:, :],
                        ALU.mult, ALU.subtract)
                    dve.sem_inc(sm["V_done"], 1)

                taps = cw[:, :].rearrange("p (k i) -> p i k", i=ET)

                def convolution(i, part):
                    if part == 0:
                        wait(dve, l, "v_done", i + 1)
                        run(dve.tensor_copy(v_last[:, i, :].rearrange("p (c t) -> p c t", t=T), vx[:, i, 8:16, C:C + 4].rearrange("p t c -> p c t")))
                        dve.sem_inc(sm["v_last_done"], 1)
                        run(dve.memset(vx[:, i, :, 0:4], 0.0))
                        run(dve.tensor_copy(vx[:, i, 0:8, 4:], vx[:, i, 8:16, 3:3 + C]))
                    for k in (range(TAPS // 2) if part == 0 else range(TAPS // 2, TAPS)):
                        src = vx[:, i, 8 - k % 8:16 - k % 8, 4 - k // 8:4 - k // 8 + C]
                        w = taps[:, i, TAPS - 1 - k:TAPS - k]
                        o = cacc[:, k % 2, :, :]
                        if k == 0:
                            ts(o, src, w, vec[:, 20 + i:21 + i], ALU.mult, ALU.add, behind=1)
                        elif k == 1:
                            run(dve.tensor_scalar(o, src, w, None, ALU.mult), behind=1)
                        else:
                            stt(o, src, w, o, ALU.mult, ALU.add, behind=1 if k % (TAPS // 2) < TAPS // 2 - 1 and k < TAPS - 1 else 0)
                    if part == 1:
                        even, odd = (cacc[:, x, :, :].rearrange("p (a b) c -> p a (b c)", a=2) for x in range(2))
                        tt(cv[:, i, 0, :, 0:4 * C], even, odd, ALU.add)

                convolution(0, 0)
                convolution(0, 1)
                for b in range(NB):
                    wait(dve, l, f"kb_in{b % 4}", 16 * (b // 4 + 1))
                    wait(dve, l, "bc_done", b + 1)
                    tt(qk[:, :, :], kb[:, b % 4, :, :], mp[:, b % 4, :].unsqueeze(1).to_broadcast([P, 2, E]), ALU.mult)
                    run(dve.tensor_reduce(sK[:, :, b * HEADS:(b + 1) * HEADS], qk[:, :, :].rearrange("p m (h d) -> p m h d", h=HEADS),
                                          op=ALU.add, axis=AX.X))
                    dve.sem_inc(sm["kq_done"], 1)
                input_matrices(0)
                wait(dve, l, "kv_out", 32)
                output_matrices(0)
                run(dve.memset(pm[:, :, :, :], 0.0))
                wait(dve, l, "scs_done", 1)
                run(dve.tensor_reduce(stat[0:32, 50:51], mp[0:32, 0, 0:MEM], op=ALU.max, axis=AX.X))
                run(dve.tensor_scalar(stat[0:32, 48:49], stat[0:32, 50:51], -SCALE, None, ALU.mult))
                dve.sem_inc(sm["nbs_done"], 1)
                wait(dve, l, "exps_done", 1)
                run(dve.reciprocal(stat[0:32, 51:52], stat[0:32, 49:50]))
                dve.tensor_scalar(ps[:, :], ps[:, :], stat[0:32, 51:52], None, ALU.mult).then_inc(sm["ps_norm"], 1)
                convolution(1, 0)
                wait(dve, l, "psT_tr", 1)
                for m in range(2):
                    for hd in range(HEADS):
                        run(dve.tensor_copy(pm[:, m, :, :].rearrange("p b c -> p (b c)")[:, hd:hd + 7 * 36 + 1:36],
                                            mp[:, 3, m * 32 + hd:(m + 1) * 32:HEADS]))
                dve.sem_inc(sm["pm_ev"], 1)
                convolution(1, 1)
                convolution(2, 0)
                wait(dve, l, "oxT_tr", 1)
                for hd in range(HEADS):
                    run(dve.tensor_copy(q[:, hd, :, 4 * C:HC],
                                        mp[:, 3, hd * 32:(hd + 1) * 32].rearrange("p (a b h) -> p a b h", h=HEADS, a=2)[:, :, :, hd]))
                dve.sem_inc(sm["ox_done"], 1)
                run(dve.memset(U[:, :, :, 0:NB], 0.0))
                run(dve.memset(U[:, :, :, YC:UC], 0.0))
                dve.sem_inc(sm["U_clear"], 1)
                run(dve.memset(Mt[:, :, :], 0.0))
                dve.sem_inc(sm["m_clear"], 1)

                def take_inputs(f):
                    wait(dve, l, "s_done", f + 1)
                    if f:
                        wait(dve, l, "y_done", 1)
                    qs = slice(f * QH, (f + 1) * QH)
                    for e in range(2):
                        for ri in range(2):
                            run(dve.tensor_copy(X[e * S:(e + 1) * S, ri, :, NB + 1:].rearrange("p (b q) c -> p b q c", q=4),
                                                mp[ri * S:(ri + 1) * S, 2 * e:2 * e + 2, 0:4 * YC].rearrange("p b (q c) -> p b q c", c=YC)))
                    dve.sem_inc(sm["s_free"], 1)
                    run(dve.memset(X[:, :, :, NB], 0.0))
                    run(dve.tensor_copy(X[:, :, :, 0:NB], s0[:, :, :, qs].rearrange("p a b q -> p a q b")))

                def scan(f):
                    qs = slice(f * QH, (f + 1) * QH)

                    def level(k, first, n):
                        d = 1 << k
                        dst = X[:, :, :, NB + 1 + first:XC:2 * d]
                        src = X[:, :, :, NB + 1 + first - d:XC - d:2 * d]
                        m = 2 * QH * n
                        ta = t1[:, 0:m].rearrange("p (a q n) -> p a q n", a=2, n=n)
                        tb = t2[:, 0:m].rearrange("p (a q n) -> p a q n", a=2, n=n)
                        for ri in range(2):
                            ar = lv[:, k, 0, qs].unsqueeze(2).to_broadcast([P, QH, n])
                            ai = lv[:, k, 1, qs].unsqueeze(2).to_broadcast([P, QH, n])
                            tt(ta[:, ri], src[:, ri], ar, ALU.mult, behind=2 * ri + 1)
                            tt(tb[:, ri], src[:, ri], ai, ALU.mult, behind=1)
                        tt(dst, dst, ta, ALU.add)
                        tt(dst[:, 0], dst[:, 0], tb[:, 1], ALU.subtract, behind=1)
                        tt(dst[:, 1], dst[:, 1], tb[:, 0], ALU.add)

                    for k in range(6):
                        level(k, (2 << k) - 1, C >> (k + 1))
                    for k in range(4, -1, -1):
                        level(k, (3 << k) - 1, (C >> (k + 1)) - 1)
                    dve.sem_inc(sm["x_done"], 1)
                    run(dve.tensor_copy(sf[:, :, qs], X[:, :, :, XC - 1]))
                    o = [sn[:, i, :, qs].rearrange("p b q -> p q b") for i in range(2)]
                    s = [s0[:, i, :, qs].rearrange("p b q -> p q b") for i in range(2)]
                    a = [pw[:, i, qs, 1:2].to_broadcast([P, QH, NB]) for i in range(2)]
                    ta = t1[:, 0:QH * NB].rearrange("p (q b) -> p q b", b=NB)
                    for i, (x, y, op) in enumerate(((0, 1, ALU.subtract), (1, 0, ALU.add))):
                        tt(o[i], s[x], a[0], ALU.mult)
                        tt(ta, s[y], a[1], ALU.mult)
                        tt(o[i], o[i], ta, op)
                        tt(o[i], o[i], X[:, i, :, XC:], ALU.add)

                def keep_lags(f):
                    wait(dve, l, "k_done", f + 1)
                    if f:
                        wait(dve, l, "k_out", 16)
                    run(dve.tensor_copy(kt[:, :, :].rearrange("h q x -> h (q x)"), mp[0:2 * H, 0:2, :].rearrange("h b x -> h (b x)")))
                    dve.sem_inc(sm["k_free"], 1)
                    ta = t1[0:2 * H, 0:QH * H].rearrange("h (q x) -> h q x", x=H)
                    tt(ta, eye2[:, :].unsqueeze(1).to_broadcast([2 * H, QH, H]),
                       dcol[:, f * QH:(f + 1) * QH].unsqueeze(2).to_broadcast([2 * H, QH, H]), ALU.mult)
                    tt(kt[:, :, 0:H], kt[:, :, 0:H], ta, ALU.add)
                    dve.sem_inc(sm["k_ev"], 1)

                keep_lags(0)
                convolution(2, 1)
                take_inputs(0)
                scan(0)
                input_matrices(1)
                convolution(3, 0)
                output_matrices(1)
                take_inputs(1)
                keep_lags(1)
                scan(1)
                dve.sem_inc(sm["sn_done"], 1)
                convolution(3, 1)
                wait(dve, l, "sfin_tr", 1)
                run(dve.tensor_copy(so[0:Q, 0:2, :].rearrange("p a c -> p (a c)"), mp[0:Q, 0, 0:2 * P]))
                run(dve.tensor_copy(so[:, 2:4, :].rearrange("p a c -> p (a c)"), mp[:, 0, 2 * P:4 * P]))
                dve.sem_inc(sm["sfin_ev"], 1)
                wait(dve, l, "st_tr", 1)
                for r in range(2):
                    run(dve.tensor_copy(cs[:, :, 4 * r:4 * r + 4, 0:TAPS - 1],
                                        mp[:, 1 + r, 0:480].rearrange("p (i b k) -> p i b k", i=ET, b=4)))
                for i in range(ET):
                    run(dve.tensor_copy(cs[:, i, :, TAPS - 1], v_s[:, i, :]))
                dve.sem_inc(sm["st_ev"], 1)
                wait(dve, l, "vs_tr", 2)
                run(dve.tensor_copy(nst[:, :], mp[0:32, 3, :]))
                run(dve.tensor_copy(nss[:, :], mp[0:NB, 0, :]))
                dve.sem_inc(sm["vs_ev"], 1)

                for i in range(ET):
                    tt(cst[:, :, :], cs[:, i, :, :], taps[:, i, :].unsqueeze(1).to_broadcast([P, NB, TAPS]), ALU.mult)
                    run(dve.tensor_reduce(v_s[:, i, :], cst[:, :, :], op=ALU.add, axis=AX.X))
                    run(dve.tensor_scalar(cv[:, i, 0, :, 4 * C:HC], v_s[:, i, :].rearrange("p (a c) -> p a c", a=2),
                                          vec[:, 20 + i:21 + i], None, ALU.add))
                    dve.sem_inc(sm["acc_done"], 1)
                wait(dve, l, "mean_done", 1)
                for i in range(ET):
                    stt(acc(i), mp[:, 0:2, 0:HC], -1.0 / E, acc(i), ALU.mult, ALU.add)
                    dve.sem_inc(sm["cent_done"], 1)
                for i in range(ET):
                    if i == 0:
                        wait(dve, l, "acc_free1", use["za"] // 2 + 1)
                        wait(dve, l, "y_ev", 8)
                        wait(dve, l, "y_out", 160)
                    tt(br[:, 2, i, :, :], q[:, i, :, :], z[:, 2, i, :, :], ALU.mult)
                dve.sem_inc(sm["br_x_done"], 1)
                wait(dve, l, "lsq_used", 1)
                wait(dve, l, "vo_out", 48)
                ts(lst[:, :, :], mp[:, 2:4, 0:HC], 1.0 / E, EPS, ALU.mult, ALU.add)
                dve.reciprocal(lst[:, :, :], lst[:, :, :]).then_inc(sm["lvar_done"], 1)
                wait(dve, l, "lrstd_done", 1)
                for i in range(ET):
                    stt(acc(i), acc(i), vec[:, 24 + i:25 + i], lst[:, :, :], ALU.mult, ALU.mult)
                    dve.sem_inc(sm["ln_done"], 1)
                wait(dve, l, "z_ev", 1)
                for i in range(ET):
                    wait(dve, l, "glu_sg", i + 1)
                    tt(br[:, 0, i, :, :], u[:, i, :, :], sg[:, i % 2, :, :], ALU.mult)
                    dve.sem_inc(sm["sg_free"], 1)
                    tt(br[:, 0, i, :, :], br[:, 0, i, :, :], z[:, 0, i, :, :], ALU.mult)
                    dve.sem_inc(sm["br_a_done"], 1)
                for i in range(ET):
                    wait(dve, l, "ln_silu", i + 1)
                    tt(br[:, 1, i, :, :], acc(i), z[:, 1, i, :, :], ALU.mult)
                    dve.sem_inc(sm["br_b_done"], 1)
                steps.clear()

                with dve.Fori(0, 4) as it:
                    inner = Steps(dve, loop_steps)
                    for jj in range(2):
                        for x in range(3):
                            m = jj * 3 + x
                            wait(dve, l, "acc_ready1", it * 6 + use["gates"] // 2 + m + 1)
                            wait(dve, l, "gate_sg", it * 6 + m + 1)
                            inner.run(dve.tensor_tensor((mj if x == 0 else tj)[:, :, :], acc_ps[1][:, :, 0:HC], sg[:, m % 2, :, :], ALU.mult))
                            dve.sem_inc(acc_free[1], 1)
                            dve.sem_inc(sm["sg_free"], 1)
                            if x:
                                inner.run(dve.tensor_tensor(mj[:, :, :], mj[:, :, :], tj[:, :, :], ALU.add))
                        j = it * 2 + jj
                        hi, lo = (t[:, bass.ds(j, 1), :, :].rearrange("p j a c -> p (j a) c") for t in (m_hi, m_lo))
                        inner.run(dve.tensor_copy(hi, mj[:, :, :]))
                        inner.run(dve.tensor_tensor(lo, mj[:, :, :], hi.bitcast(F32), ALU.subtract))
                        dve.sem_inc(sm["m_done"], 1)
                    inner.clear()
                with dve.Fori(0, 4) as it:
                    inner = Steps(dve, loop_steps)
                    for k in range(2):
                        wait(dve, l, f"acc_ready{k}", it + use["out"] // 2 + 1)
                        xj = xT[:, bass.ds(it * 2 + k, 1), :, :].rearrange("p j a c -> p (j a) c")
                        inner.run(dve.tensor_tensor(xj, acc_ps[k][:, :, 0:HC], xj, ALU.add))
                        dve.sem_inc(acc_free[k], 1)
                        dve.sem_inc(sm["x_sum"], 1)
                    inner.clear()

            dve.wait_ge(sm["fin_used"], KT)
            ts(rs[:, :, :], mp[:, 0:2, 0:HC], 1.0 / D, EPS, ALU.mult, ALU.add)
            dve.reciprocal(rs[:, :, :], rs[:, :, :]).then_inc(sm["fin_var"], 1)
            dve.wait_ge(sm["fin_rt"], 1)
            for k in range(KT):
                stt(xT[:, k, :, :], xT[:, k, :, :], vec[:, 80 + k:81 + k], rs[:, :, :], ALU.mult, ALU.mult)
                dve.sem_inc(sm["fin_y"], 1)
            run(dve.tensor_copy(xsc[:, :, :].rearrange("p k (a c) -> p k a c", a=2), xT[:, :, :, 4 * C:HC]))
            dve.sem_inc(sm["fin_y"], 1)


INS = ("x_prompt", "x_sample", "mem_prompt", "state_ssm_re", "state_ssm_im", "state_conv", "cache_mem_k",
       "cache_mem_v", "norm_g", "w_in", "ssm_a_re", "ssm_a_im", "ssm_log_dt", "ssm_b_re", "ssm_b_im", "ssm_c_re",
       "ssm_c_im", "ssm_d", "w_glu", "b_glu", "w_br_ssm", "conv_w", "conv_b", "conv_ln_g", "conv_ln_b",
       "w_br_conv", "mem_norm_g", "w_k", "w_v", "w_br_xatt", "w_out", "final_norm_g")
OUTS = ((1, SEQ, D), (NB, 1, D), (LAYERS, 1, G, S), (LAYERS, 1, G, S), (LAYERS, 1, TAPS - 1, E),
        (LAYERS, 1, MEM, HEADS, P), (LAYERS, 1, MEM, HEADS, P), (LAYERS, NB, G, S), (LAYERS, NB, G, S),
        (LAYERS, NB, TAPS - 1, E))


def kernel(**inputs):
    import concourse.bacc as bacc
    import numpy as np
    from concourse.bass_utils import run_bass_kernel_spmd

    nc = bacc.Bacc("TRN2", target_bir_lowering=False, num_devices=1)
    arrays, args = {}, []
    for name in INS:
        a = np.ascontiguousarray(inputs[name])
        arrays[f"in_{name}"] = a
        args.append(nc.dram_tensor(f"in_{name}", a.shape, mybir.dt.from_np(a.dtype), kind="ExternalInput").ap())
    for i, shape in enumerate(OUTS):
        args.append(nc.dram_tensor(f"out_{i}", shape, F32, kind="ExternalOutput").ap())
    build(nc, *args)
    r = run_bass_kernel_spmd(nc, [arrays], core_ids=[0])
    return tuple(r.results[0][f"out_{i}"] for i in range(len(OUTS)))
```

```python
from contextlib import ExitStack

import concourse.bass as bass
from concourse import mybir

F32 = mybir.dt.float32
F32R = mybir.dt.float32r
ALU = mybir.AluOpType
ACT = mybir.ActivationFunctionType
AX = mybir.AxisListType

P = 128
D = 1024
SEQ = 512
LAYERS = 2
NB = 8
MEM = 256
KT = D // P
E = 512
ET = E // P
HEADS = 4
G, H, S = 32, 16, 64
Q = G // 2
QH = Q // 2
T = 8
C = SEQ // T
TAPS = 31
HC = 4 * C + 4
EPS = 1e-6
SCALE = P ** -0.5
XC = NB + 1 + C
UC = NB + C + NB
YC = NB + C
UNITS = 72
TWO_PI = 6.283185307179586
PI2_HI, PI2_MID = 6.28125, 0.0019350051879882812
PI2_LO = TWO_PI - PI2_HI - PI2_MID
PI_BELOW = 3.1415925
ROUND = 12582912.0


class Steps:

    def __init__(self, eng, sem):
        self.eng, self.sem, self.n = eng, sem, 0

    def run(self, ins, behind=0):
        self.n += 1
        ins.then_inc(self.sem, 1)
        if behind < self.n:
            self.eng.wait_ge(self.sem, self.n - behind)

    def clear(self):
        self.eng.sem_clear(self.sem)
        self.n = 0


def build(nc, x_prompt, x_sample, mem_prompt, state_ssm_re, state_ssm_im, state_conv, cache_mem_k,
          cache_mem_v, norm_g, w_in, ssm_a_re, ssm_a_im, ssm_log_dt, ssm_b_re, ssm_b_im, ssm_c_re,
          ssm_c_im, ssm_d, w_glu, b_glu, w_br_ssm, conv_w, conv_b, conv_ln_g, conv_ln_b, w_br_conv,
          mem_norm_g, w_k, w_v, w_br_xatt, w_out, final_norm_g, y_prompt, y_sample, ssm_re_p, ssm_im_p,
          conv_p, mem_k_p, mem_v_p, ssm_re_s, ssm_im_s, conv_s):
    ctx = ExitStack()

    def sb(name, shape, dt=F32):
        return ctx.enter_context(nc.sbuf_tensor(name, shape, dt))

    def sem(name):
        return ctx.enter_context(nc.semaphore(name))

    with ctx:
        xT = sb("xT", [P, KT, 2, HC])
        h_hi = sb("h_hi", [P, KT, 2, HC], F32R)
        h_lo = sb("h_lo", [P, KT, 2, HC], F32R)
        w_hi = sb("w_hi", [P, 2, KT * P], F32R)
        w_lo = sb("w_lo", [P, 2, KT * P], F32R)
        w_st = sb("w_st", [P, 2, KT * P])
        wd_at = nc.sbuf_base
        w_dir = sb("w_dir", [P, 2, 12 * P])
        q = sb("q", [P, ET, 2, HC])
        sg = sb("sg", [P, 2, 2, HC])
        ident = sb("ident", [P, P])
        ones = sb("ones", [P, P])
        eye2 = sb("eye2", [2 * H, H])
        vec = sb("vec", [P, 80])
        cw = sb("cw", [P, TAPS * ET])
        dcol = sb("dcol", [2 * H, Q])
        pw = sb("pw", [P, 2, Q, T + 1])
        lv = sb("lv", [P, 6, 2, Q])
        li = sb("li", [P, 6, 2, Q])
        tiny = sb("tiny", [P, 12, Q])
        stat = sb("stat", [P, 64])
        s0 = sb("s0", [P, 2, NB, Q])
        sn = sb("sn", [P, 2, NB, Q])
        sf = sb("sf", [P, 2, Q])
        v_s = sb("v_s", [P, ET, NB])
        v_last = sb("v_last", [P, ET, 32])

        z_at = nc.sbuf_base
        zreg = sb("zreg", [P, 12 * 2 * HC])
        v_at = nc.sbuf_base
        vreg = sb("vreg", [P, ET * 16 * (C + 4)])
        u_at = nc.sbuf_base
        ureg = sb("ureg", [P, ET * 2 * HC])
        r_at = nc.sbuf_base
        rlen = 13312
        rreg = sb("rreg", [P, rlen])
        assert v_at == z_at + 4 * 12 * 2 * HC

        def at(base, off, limit, name, shape, dt=F32):
            n = 1
            for d in shape[1:]:
                n *= d
            assert off + n <= limit, (name, off + n, limit)
            return nc.alloc_sbuf_tensor_at(name, shape, dt, offset=base + 4 * off)

        def zr(name, off, shape):
            return at(z_at, off, 12 * 2 * HC, name, shape)

        def ur(name, off, shape):
            return at(u_at, off, ET * 2 * HC, name, shape)

        def rr(name, off, shape):
            return at(r_at, off, rlen, name, shape)

        z = zr("z", 0, [P, 3, ET, 2, HC])
        m_hi = at(z_at, 0, 10**6, "m_hi", [P, KT, 2, HC], F32R)
        m_lo = at(z_at, KT * 2 * HC, 10**6, "m_lo", [P, KT, 2, HC], F32R)
        assert 2 * KT * 2 * HC <= 12 * 2 * HC + ET * 16 * (C + 4)
        vx = at(v_at, 0, 10**6, "vx", [P, ET, 16, C + 4])
        u = ur("u", 0, [P, ET, 2, HC])
        prow = ur("prow", 0, [80, P])
        cwrow = ur("cwrow", 128, [TAPS * ET, P])
        crow = ur("crow", 256, [P, 2, 2, P])
        srow = ur("srow", 768, [P, 2, P])
        drow = ur("drow", 1024, [Q, 2 * H])
        dtrow = ur("dtrow", 1040, [80, 2])
        bT = zr("bT", 0, [P, 2, Q, H])
        bd = zr("bd", 0, [P, 2, Q, 2, H])
        bb = zr("bb", 1024, [P, 2, Q, H])
        cT = zr("cT", 1536, [P, 2, Q, H])
        wt = zr("wt", 2048, [P, 2, QH, T * H])
        xrow = rr("xrow", 0, [P, 4, D])
        mrow = rr("mrow", 4096, [P, 2, D])
        xsrow = rr("xsrow", 6144, [NB, D])
        memn0 = rr("memn0", 7168, [P, KT, MEM])
        memn = rr("memn", 4224, [P, KT, MEM])
        memg = rr("memg", 6272, [P, KT, MEM])
        kb = rr("kb", 0, [P, 4, 2, E])
        ktok = rr("ktok", 4096, [P, 2, E])
        ps = rr("ps", 4096, [32, MEM])
        pm = zr("pm", 5216, [P, 2, NB, 32])
        qrow = zr("qrow", 4608, [NB, E])
        qs = zr("qs", 5120, [P, HEADS, NB])
        qk = zr("qk", 5152, [P, 2, E])
        sK = zr("sK", 6176, [P, 2, NB * HEADS])
        vtok = rr("vtok", 5120, [P, 2, E])
        kT = rr("kT", 6144, [P, HEADS, MEM])
        pr = rr("pr", 7168, [P, 2, HEADS, MEM])
        in1 = rr("in1", 4096, [P, QH * T * H])
        in2 = rr("in2", 6144, [P, QH * T * H])
        oxs = rr("oxs", 7168, [32, E])
        pT = rr("pT", 9216, [P, HEADS, 2, SEQ])
        sq = rr("sq", 0, [P, KT, 2, HC])
        ht = rr("ht", 9216, [P, 2, 2, HC])
        rs = rr("rs", 10256, [P, 2, HC])
        U = rr("U", 0, [P, Q, 2, UC])
        wl = rr("wl", 2560, [P, QH, 2, 2 * S])
        V2 = rr("V2", 2560, [P, QH, 2, T * H])
        X2 = ur("X2", 0, [P, QH, 2, YC])
        V = rr("V", 4608, [P, 2, QH, T + 1, H])
        Mt = rr("Mt", 6912, [P, G // 2, T * H])
        X = rr("X", 8960, [P, 2, QH, XC + NB])
        t1 = rr("t1", 10256, [P, QH * (T + 1) * H])
        t2 = rr("t2", 11408, [P, QH * (T + 1) * H])
        br_hi = at(r_at, 0, rlen, "br_hi", [P, 3, ET, 2, HC], F32R)
        br_lo = at(r_at, 3 * ET * 2 * HC, rlen, "br_lo", [P, 3, ET, 2, HC], F32R)
        cv = at(v_at, 0, 10**6, "cv", [P, ET, 2, 2, 2 * (C + 4) * 2])
        cs = rr("cs", 8320, [P, ET, NB, TAPS])
        cst = rr("cst", 9312, [P, NB, TAPS])
        crw = rr("crw", 9560, [120, 2, E])
        lst = rr("lst", 12480, [P, 2, HC])
        mj = ur("mj", 0, [P, 2, 2, HC])
        tj = ur("tj", 2 * 2 * HC, [P, 2, HC])
        kt = at(wd_at, 0, 24 * P, "kt", [2 * H, QH, T * H])
        cacc = at(wd_at, 16 * P, 24 * P, "cacc", [P, 2, T, C])
        so = at(wd_at, 8 * P, 12 * P, "so", [P, 4, P])
        nrow = rr("nrow", 12800, [64, E])
        yrow = rr("yrow", 4224, [P, 4, D])
        grow = rr("grow", 8320, [P, D])
        ysr = rr("ysr", 9344, [NB, D])
        xsc = rr("xsc", 10368, [P, KT, NB])

        acc_ps = [ctx.enter_context(nc.psum_tensor(f"acc{i}", [P, 2, 512], F32)) for i in range(2)]
        mp = ctx.enter_context(nc.psum_tensor("mp", [P, 4, 512], F32))

        u_dram = nc.dram_tensor("u_scratch", (E, 2, HC), F32).ap()
        y_dram = nc.dram_tensor("y_scratch", (E, 2, HC), F32).ap()
        k_dram = nc.dram_tensor("k_scratch", (G, H, T * H), F32).ap()
        m_dram = nc.dram_tensor("m_scratch", (P, KT * MEM), F32).ap()

        w_loaded = [sem(f"w_loaded{i}") for i in range(2)]
        w_staged_free = sem("w_staged_free")
        w_hi_done = sem("w_hi_done")
        dve_steps = sem("dve_steps")
        act_steps = sem("act_steps")
        loop_steps = sem("loop_steps")

        sm = {n: sem(n) for n in """
            x_in mem_in consts x_tr x_ev mem_sq mem_var mem_rt mem_nrm mem_tr mem_ev mem_out g_in fin_tr
            fin_sq fin_var fin_rt fin_y fin_out0 fin_out1 fin_out2 fin_out3 fin_out_s""".split()}
        entered = sem("entered")

        per = """
            dt_in=16 dt_wide=1 p_in=160 c_in=128 b_in=64 s_in=32 mg_in=16 sq_done=8 sq_used=1 var_done=1
            rstd_done=1 ht_done=8 hhi_done=8 h_done=1 par_tr=1 par_ev=1 c_tr=1 c_ev=1 s0_tr=1 s0_ev=1 memg_done=1
            kv_used=6 kv_ev=2 kT_tr=1 kT_ev=1 kv_out=32 q_ev=4 dt_exp=1 sin_arg=1 par_act=1 sc_done=4
            nb_done=4 exp_done=4 p_norm=4 pT_tr=4 pT_ev=4 pv_done=1 pv_ev=1 kb_in0=64 kb_in1=64 kb_in2=64 kb_in3=64
            qs_done=1 qrow_tr=1 qrow_ev=1 bc_done=8 kq_done=8 scs_done=1 nbs_done=1 exps_done=1 ps_norm=1
            psT_tr=1 pm_ev=1 pm_clear=2 pvs_done=8 oxs_ev=1 oxT_tr=1 ox_done=1 u_ev=4 u_out=16 U_clear=1 U_in=192 val_ev=8 v_done=4 v_last_done=4
            wt_done=2 w_tr=2 wl_ev=4 s_done=2 s_free=4 V_done=2 k_done=2 k_free=2 k_ev=2 k_out=32 m_clear=1
            V2_done=2 X2_done=1 s_turned=2
            m_in=256 x_scan=2 x_done=2 y_done=2 y_ev=8 y_out=160 y_in=16 sn_done=1 sfin_tr=1 sfin_ev=1 sfin_out=64
            st_in=32 st_tr=1 st_ev=1 vs_tr=2 vs_ev=1 vo_out=48 acc_done=4 mean_done=1
            cent_done=4 lsq_done=4 lsq_used=1 lvar_done=1 lrstd_done=1 ln_done=4 ln_silu=4 br_b_done=4
            br_x_done=1 glu_sg=4 br_a_done=4 gate_sg=24 sg_free=32 m_done=8 x_sum=8 z_ev=1 b_ready=24 b_free=24 acc_ready0=33
            acc_ready1=33 acc_free0=33 acc_free1=33 d_loaded0=80 d_loaded1=80""".split()
        per = {n: int(k) for n, k in (x.split("=") for x in per)}
        sm.update({n: sem(n) for n in per})
        acc_ready, acc_free, d_loaded = ([sm[f"{n}{i}"] for i in range(2)] for n in ("acc_ready", "acc_free", "d_loaded"))

        def wait(eng, l, name, value):
            eng.wait_ge(sm[name], l * per[name] + value)

        use, n = {}, 0
        for name, k in (("kv", 2), ("v", 4), ("q", 4), ("u", 4), ("vb", 4), ("zx", 4), ("za", 4), ("zb", 4),
                        ("glu", 4), ("gates", 24), ("out", 8)):
            use[name] = n
            n += k
        unit, n = {}, 0
        for name, k in (("v", 4), ("q", 4), ("u", 4), ("vb", 4), ("zx", 4), ("za", 4), ("zb", 4), ("gates", 36),
                        ("out", 8)):
            unit[name] = n
            n += k
        assert n == UNITS
        for d in (use, unit):
            d["vb"] -= 4

        def acc(i):
            return cv[:, i, 0, :, 0:HC]

        def lsq(i):
            return cv[:, i, 1, :, 0:HC]

        def token_banks(i):
            return mp[:, 2 * i:2 * i + 2, :] if i < 2 else acc_ps[i - 2][:, :, :]

        def g3(ap):
            return ap[:, :, :, 0:4 * C]

        block = ctx.enter_context(nc.Block())

        @block.sync
        def _(sp):
            xp = x_prompt[0].rearrange("(c i s) d -> s c i d", s=2, i=4)
            for s in range(2):
                sp.dma_start(xrow[s * C:(s + 1) * C, :, :], xp[s]).then_inc(sm["x_in"], 16)
            sp.dma_start(xsrow[:, :], x_sample[:, 0, :]).then_inc(sm["x_in"], 16)
            sp.dma_start(mrow[:, :, :], mem_prompt[0].rearrange("(m p) d -> p m d", p=P)).then_inc(sm["mem_in"], 16)

            def ring_load(src, slot, n, width=P):
                sp.wait_ge(w_staged_free, n + 1)
                sp.dma_start(w_st[:, slot, :].rearrange("p (k c) -> p k c", c=width), src).then_inc(w_loaded[slot], 16)

            with sp.Fori(0, LAYERS) as l:
                sp.dma_start(dtrow[64:80, :], ssm_log_dt[l].rearrange("(q e) -> q e", e=2)).then_inc(sm["dt_in"], 16)
                win = w_in[l].rearrange("(k p) c -> p k c", p=P)
                wo = w_out[l].rearrange("(k p) c -> p k c", p=P)

                def section(name, pairs, cols, first=0, src=win):
                    sp.sem_inc(entered, 1)
                    with sp.Fori(first, first + pairs) as it:
                        for k, col in enumerate(cols):
                            ring_load(src[:, :, bass.ds(col(it), P)], k, l * UNITS + unit[name] + it * 2 + k)

                def straight(c0):
                    return [lambda it, k=k: (it * 2 + k) * P + c0 for k in range(2)]

                rows = ((0, 16, ssm_a_re[l].rearrange("(q e) p -> q (e p)", e=2)),
                        (16, 4, b_glu[l].rearrange("(k p) -> k p", p=P)),
                        (20, 4, conv_b[l].rearrange("(k p) -> k p", p=P)),
                        (24, 4, conv_ln_g[l].rearrange("(k p) -> k p", p=P)),
                        (28, 4, conv_ln_b[l].rearrange("(k p) -> k p", p=P)),
                        (32, 16, ssm_a_im[l].rearrange("(q e) p -> q (e p)", e=2)),
                        (48, 8, norm_g[l].rearrange("(k p) -> k p", p=P)),
                        (56, 8, mem_norm_g[l].rearrange("(k p) -> k p", p=P)))
                for r0, n, src in rows:
                    sp.dma_start(prow[r0:r0 + n, :], src).then_inc(sm["p_in"], 16)
                sp.dma_start(cwrow[:, :], conv_w[l].rearrange("k (i c) -> (k i) c", c=P)).then_inc(sm["p_in"], 16)
                sp.dma_start(drow[:, :], ssm_d[l].rearrange("(q x) -> q x", x=2 * H)).then_inc(sm["p_in"], 16)

                def kv_load(i):
                    src = (w_k, w_v)[i // 4][l].rearrange("(k p) c -> p k c", p=P)
                    if i >= 2:
                        if i - 2 == 3:
                            wait(sp, l, "acc_ready0", 1)
                        else:
                            wait(sp, l, "kv_used", i - 1 - (i > 5))
                    sp.dma_start(w_dir[:, i % 2, 0:2 * E].rearrange("p (k c) -> p k c", c=E),
                                 src[:, 2 * (i % 4):2 * (i % 4) + 2, :]).then_inc(d_loaded[i % 2], 16)

                kv_load(0)
                kv_load(1)
                sp.wait_ge(sm["mem_out"], 16)
                sp.wait_ge(sm["x_ev"], 5)
                sp.dma_start(memn[:, :, :].rearrange("p k m -> p (k m)"), m_dram).then_inc(sm["mg_in"], 16)
                v_cols = [lambda it: 3 * E + it * P, lambda it: 2 * E + it * P]
                section("v", 1, v_cols)
                for ri, src in enumerate((ssm_c_re, ssm_c_im)):
                    for half in range(2):
                        for e in range(2):
                            cv = src[l].rearrange("(f q e) h p -> f e q h p", e=2, f=2)[half, e]
                            sp.dma_start(crow[:, ri, half, e * S:(e + 1) * S], cv).then_inc(sm["c_in"], 16)
                for ri, src in enumerate((state_ssm_re, state_ssm_im)):
                    sp.dma_start(srow[:, ri, :], src[l].rearrange("b (q e) p -> (b q) (e p)", e=2)).then_inc(sm["s_in"], 16)
                for i in range(2, 8):
                    kv_load(i)
                for ri, src in enumerate((ssm_b_re, ssm_b_im)):
                    bv = src[l].rearrange("(q e) p h -> e p q h", e=2)
                    for e in range(2):
                        sp.dma_start(bT[e * S:(e + 1) * S, ri, :, :], bv[e]).then_inc(sm["b_in"], 16)
                section("v", 1, v_cols, first=1)
                section("q", 2, straight(5 * E))
                wait(sp, l, "kv_ev", 2)
                sp.dma_start(mem_k_p[l, 0].rearrange("(m p) h d -> p m (h d)", p=P), ktok[:, :, :]).then_inc(sm["kv_out"], 16)
                sp.dma_start(mem_v_p[l, 0].rearrange("(m p) h d -> p m (h d)", p=P), vtok[:, :, :]).then_inc(sm["kv_out"], 16)
                section("u", 2, straight(0))
                section("vb", 1, v_cols, first=2)

                def cache_load(cache, b):
                    sp.dma_start(kb[:, b % 4, :, :], cache[l, b].rearrange("(m p) h d -> p m (h d)", p=P)).then_inc(sm[f"kb_in{b % 4}"], 16)

                wait(sp, l, "acc_ready1", 1)
                for b in range(4):
                    cache_load(cache_mem_k, b)
                wait(sp, l, "u_ev", 4)
                sp.dma_start(u_dram.rearrange("(i p) a c -> p i (a c)", p=P), u[:, :, :, :].rearrange("p i a c -> p i (a c)")).then_inc(sm["u_out"], 16)
                for b in range(4, NB - 2):
                    wait(sp, l, "kq_done", b - 3)
                    cache_load(cache_mem_k, b)
                section("vb", 1, v_cols, first=3)
                for b in range(NB - 2, NB):
                    wait(sp, l, "kq_done", b - 3)
                    cache_load(cache_mem_k, b)
                section("zx", 1, straight(6 * E))
                for b in range(4):
                    wait(sp, l, "kq_done", b + 5)
                    cache_load(cache_mem_v, b)
                section("zx", 1, straight(6 * E), first=1)
                for b in range(4, NB):
                    wait(sp, l, "pvs_done", b - 3)
                    cache_load(cache_mem_v, b)
                wait(sp, l, "u_out", 16)
                sp.sem_inc(entered, 1)
                wait(sp, l, "U_clear", 1)
                ug = u_dram.rearrange("(g h) a c -> h g a c", h=H)
                Ug = U[:, :, :, :].rearrange("p q e c -> p (q e) c")
                for t in range(T):
                    sp.dma_start(Ug[t * H:(t + 1) * H, :, NB:NB + C], ug[:, :, t // 4, (t % 4) * C:(t % 4 + 1) * C]).then_inc(sm["U_in"], 16)
                for a in range(2):
                    sp.dma_start(Ug[0:H, :, 4 * a:4 * a + 4], ug[:, :, a, 4 * C:HC]).then_inc(sm["U_in"], 16)
                    sp.dma_start(Ug[7 * H:P, :, YC + 4 * a:YC + 4 * a + 4], ug[:, :, a, 4 * C:HC]).then_inc(sm["U_in"], 16)

                def toeplitz(half):
                    wait(sp, l, "k_ev", half + 1)
                    kh = k_dram[half * (G // 2):(half + 1) * (G // 2)]
                    kg = kh.rearrange("g h x -> h g x")
                    sp.dma_start(kh.rearrange("(q e) h x -> (e h) q x", e=2), kt[:, :, :]).then_inc(sm["k_out"], 16)
                    wait(sp, l, "k_out", 16 * (half + 1))
                    if half == 0:
                        wait(sp, l, "m_clear", 1)
                    else:
                        wait(sp, l, "y_done", 1)
                    for s in range(T):
                        sp.dma_start(Mt[s * H:(s + 1) * H, :, s * H:], kg[:, :, 0:(T - s) * H]).then_inc(sm["m_in"], 16)

                toeplitz(0)
                section("za", 2, straight(E))
                toeplitz(1)
                section("zb", 1, straight(4 * E))
                sp.dma_start(conv_s[l, :, 0:TAPS - 2, :], state_conv[l, :, 1:TAPS - 1, :]).then_inc(sm["vo_out"], 16)
                wait(sp, l, "y_ev", 8)
                wait(sp, l, "sn_done", 1)
                for r in range(2):
                    sp.dma_start(crw[:, r, :], state_conv[l].rearrange("(r b) k c -> r (b k) c", r=2)[r]).then_inc(sm["st_in"], 16)
                yg = y_dram.rearrange("(g h) a c -> h g a c", h=H)
                for t in range(T):
                    sp.dma_start(yg[:, :, t // 4, (t % 4) * C:(t % 4 + 1) * C], Ug[t * H:(t + 1) * H, :, NB:YC]).then_inc(sm["y_out"], 16)
                for a in range(2):
                    sp.dma_start(yg[:, :, a, 4 * C:HC], Ug[0:H, :, 4 * a:4 * a + 4]).then_inc(sm["y_out"], 16)
                wait(sp, l, "y_out", 160)
                sp.dma_start(u[:, :, :, :].rearrange("p i a c -> p i (a c)"), y_dram.rearrange("(i p) a c -> p i (a c)", p=P)).then_inc(sm["y_in"], 16)
                section("zb", 1, straight(4 * E), first=1)
                wait(sp, l, "acc_done", 4)
                for g in range(2):
                    sp.dma_start(w_dir[:, g, 0:2 * E].rearrange("p (k c) -> p k c", c=2 * P),
                                 w_glu[l].rearrange("(k p) c -> p k c", p=P)[:, :, g * 2 * P:(g + 1) * 2 * P]).then_inc(d_loaded[g], 16)
                wait(sp, l, "sfin_ev", 1)
                sp.dma_start(ssm_re_p[l, 0].rearrange("(q e) p -> q (e p)", e=2), so[0:Q, 0, :]).then_inc(sm["sfin_out"], 16)
                sp.dma_start(ssm_im_p[l, 0].rearrange("(q e) p -> q (e p)", e=2), so[0:Q, 1, :]).then_inc(sm["sfin_out"], 16)
                sp.dma_start(ssm_re_s[l].rearrange("b (q e) p -> (b q) (e p)", e=2), so[:, 2, :]).then_inc(sm["sfin_out"], 16)
                sp.dma_start(ssm_im_s[l].rearrange("b (q e) p -> (b q) (e p)", e=2), so[:, 3, :]).then_inc(sm["sfin_out"], 16)
                wait(sp, l, "vs_ev", 1)
                sp.dma_start(conv_p[l, 0], nrow[2:32, :]).then_inc(sm["vo_out"], 16)
                sp.dma_start(conv_s[l, :, TAPS - 2, :], nrow[32:32 + NB, :]).then_inc(sm["vo_out"], 16)
                branch_w = (w_br_ssm, w_br_conv, w_br_xatt)
                with sp.Fori(0, 2) as it:
                    for m in range(18):
                        x, j = m // 3 % 3, it * 4 + m // 9 * 2
                        n = l * UNITS + unit["gates"] + it * 18 + m
                        if m % 3 < 2:
                            ring_load(win[:, :, bass.ds((j + m % 3) * P + 7 * E + x * D, P)], m % 2, n)
                        else:
                            ring_load(branch_w[x][l].rearrange("(k p) c -> p k c", p=P)[:, :, bass.ds(j * P, 2 * P)], m % 2, n, 2 * P)
                section("out", 4, straight(0), src=wo)
                wait(sp, l, "kv_out", 32)
                wait(sp, l, "sfin_out", 64)
                wait(sp, l, "vo_out", 48)
                sp.sem_inc(entered, 1)

            sp.dma_start(grow[:, :], final_norm_g.rearrange("(o d) -> o d", o=1).to_broadcast([P, D])).then_inc(sm["g_in"], 16)
            yp = y_prompt[0].rearrange("(c i s) d -> s i c d", s=2, i=4)
            for i in range(4):
                sp.wait_ge(sm["fin_y"], i + 2)
                for s in range(2):
                    sp.dma_start(yp[s, i], yrow[s * C:(s + 1) * C, i, :]).then_inc(sm[f"fin_out{i}"], 16)
            sp.wait_ge(sm["fin_y"], 6)
            sp.dma_start(y_sample[:, 0, :], ysr[:, :]).then_inc(sm["fin_out_s"], 16)
            for i in range(4):
                sp.wait_ge(sm[f"fin_out{i}"], 32)
            sp.wait_ge(sm["fin_out_s"], 16)

        @block.gpsimd
        def _(pool):
            pool.memset(ones[:, :], 1.0).then_inc(sm["consts"], 1)
            pool.memset(ident[:, :], 0.0).then_inc(sm["consts"], 1)
            pool.wait_ge(sm["consts"], 2)
            pool.affine_select(out=ident[:, :], in_=ident[:, :], compare_op=ALU.not_equal, fill=1.0, base=0,
                               pattern=[[-1, P]], channel_multiplier=1).then_inc(sm["consts"], 1)
            pool.sem_inc(w_staged_free, 2)

            with pool.Fori(0, LAYERS) as l:
                def low(slot, n):
                    pool.wait_ge(w_hi_done, n + 1)
                    pool.tensor_tensor(w_lo[:, slot, :], w_st[:, slot, :], w_hi[:, slot, :].bitcast(F32),
                                       ALU.subtract).then_inc(w_staged_free, 1)

                def pairs(name, first, count):
                    with pool.Fori(first, first + count) as it:
                        for k in range(2):
                            low(k, l * UNITS + unit[name] + it * 2 + k)

                def glu_v(i):
                    wait(pool, l, "val_ev", 2 * i + 2)
                    for a in range(2):
                        blk = vx[:, bass.ds(i, 1), 8 + 4 * a:12 + 4 * a, 4:4 + C].rearrange("p i b c -> p (i b) c")
                        pool.tensor_tensor(blk, blk, sg[:, i % 2, a, 0:4 * C].rearrange("p (b c) -> p b c", c=C), ALU.mult)
                    s = v_s[:, i, :].rearrange("p (a c) -> p a c", a=2)
                    pool.tensor_tensor(s, s, sg[:, i % 2, :, 4 * C:HC], ALU.mult).then_inc(sm["v_done"], 1)
                    wait(pool, l, "v_done", i + 1)
                    pool.sem_inc(sm["sg_free"], 1)

                pairs("v", 0, 2)
                glu_v(0)
                pairs("q", 0, 1)
                glu_v(1)
                pairs("q", 1, 1)
                pairs("u", 0, 2)
                pairs("vb", 2, 2)
                glu_v(2)
                pairs("zx", 0, 1)
                wait(pool, l, "kq_done", NB)
                pool.sem_inc(sm["pm_clear"], 1)
                pool.memset(pm[:, :, :, :], 0.0).then_inc(sm["pm_clear"], 1)
                glu_v(3)
                low(0, l * UNITS + unit["zx"] + 2)
                wait(pool, l, "oxT_tr", 1)
                pool.sem_inc(entered, 1)
                pool.memset(U[:, :, :, 0:NB], 0.0)
                pool.memset(U[:, :, :, YC:UC], 0.0).then_inc(sm["U_clear"], 1)
                pool.memset(Mt[:, :, :], 0.0).then_inc(sm["m_clear"], 1)
                low(1, l * UNITS + unit["zx"] + 3)
                pairs("za", 0, 2)
                pairs("zb", 0, 2)
                pairs("gates", 0, 18)
                pairs("out", 0, 4)

        @block.tensor
        def _(pe):
            def transpose(out, in_, n):
                return pe.transpose(out, in_, ident[0:n, 0:n])

            pe.wait_ge(sm["consts"], 3)
            pe.wait_ge(sm["x_in"], 48)
            for i in range(4):
                if i >= 2:
                    pe.wait_ge(sm["x_ev"], i - 1)
                for k in range(KT):
                    last = transpose(mp[:, 2 * (i % 2) + k // 4, (k % 4) * P:(k % 4 + 1) * P], xrow[:, i, k * P:(k + 1) * P], P)
                last.then_inc(sm["x_tr"], 1)
            pe.wait_ge(sm["x_ev"], 3)
            for k in range(KT):
                last = transpose(mp[:, 0, k * NB:(k + 1) * NB], xsrow[:, k * P:(k + 1) * P], NB)
            last.then_inc(sm["x_tr"], 1)
            pe.wait_ge(sm["mem_nrm"], 2)
            for m in range(2):
                if m == 0:
                    pe.wait_ge(sm["x_ev"], 4)
                else:
                    pe.wait_ge(sm["x_ev"], 5)
                for k in range(KT):
                    last = transpose(mp[:, 2 * (1 - m) + k // 4, (k % 4) * P:(k % 4 + 1) * P], mrow[:, m, k * P:(k + 1) * P], P)
                last.then_inc(sm["mem_tr"], 1)
            pe.wait_ge(sm["mem_ev"], 2)

            with pe.Fori(0, LAYERS) as l:
                def split_product(pair, use_n, slot, n, hi, lo, tiles_done=None):
                    pe.wait_ge(w_staged_free, n + 3)
                    wait(pe, l, f"acc_free{pair}", use_n + 1)
                    for k in range(KT):
                        if tiles_done and k >= KT - 2:
                            wait(pe, l, tiles_done, k + 1)
                        for p, (w, x) in enumerate(((w_hi, hi), (w_lo, hi), (w_hi, lo))):
                            for a in range(2):
                                last = pe.matmul(acc_ps[pair][:, a, 0:HC], w[:, slot, k * P:(k + 1) * P], x[:, k, a, :],
                                                 start=(k == 0 and p == 0), stop=(k == KT - 1 and p == 2))
                    last.then_inc(acc_ready[pair], 1)

                def in_unit(name, i):
                    split_product(i % 2, (use[name] + i) // 2, i % 2, l * UNITS + unit[name] + i, h_hi, h_lo)

                def in_section(name, first, pairs):
                    pe.sem_inc(entered, 1)
                    with pe.Fori(first, first + pairs) as it:
                        for k in range(2):
                            split_product(k, it + use[name] // 2, k, l * UNITS + unit[name] + it * 2 + k, h_hi, h_lo)

                wait(pe, l, "dt_wide", 1)
                wait(pe, l, "p_in", 16 * 10)
                transpose(mp[:, 2, 0:80], prow[:, :], 80)
                transpose(mp[:, 2, P:P + TAPS * ET], cwrow[:, :], TAPS * ET)
                last = transpose(mp[0:2 * H, 2, 256:256 + Q], drow[:, :], Q)
                last.then_inc(sm["par_tr"], 1)
                for k in range(KT):
                    wait(pe, l, "sq_done", k + 1)
                    for a in range(2):
                        last = pe.matmul(mp[:, a, 0:HC], ones[:, :], sq[:, k, a, :], start=(k == 0), stop=(k == KT - 1))
                last.then_inc(sm["sq_used"], 1)
                wait(pe, l, "memg_done", 1)
                for i in range(8):
                    wait(pe, l, f"d_loaded{i % 2}", 16 * (i // 2 + 1))
                    if i % 4 == 0:
                        wait(pe, l, f"acc_free{i // 4}", 1)
                    for kk in range(2):
                        k = 2 * (i % 4) + kk
                        for m in range(2):
                            last = pe.matmul(acc_ps[i // 4][:, m, :], memg[:, k, m * P:(m + 1) * P],
                                             w_dir[:, i % 2, kk * E:(kk + 1) * E], start=(k == 0), stop=(k == KT - 1))
                    if i % 4 == 3:
                        last.then_inc(acc_ready[i // 4], 1)
                    else:
                        last.then_inc(sm["kv_used"], 1)
                wait(pe, l, "var_done", 1)
                wait(pe, l, "s_in", 32)
                for ri in range(2):
                    last = transpose(mp[:, 0, ri * P:(ri + 1) * P], srow[:, ri, :], P)
                last.then_inc(sm["s0_tr"], 1)
                wait(pe, l, "c_in", 16 * 8)
                for ri in range(2):
                    for f in range(2):
                        last = transpose(mp[:, 3, (2 * ri + f) * P:(2 * ri + f + 1) * P], crow[:, ri, f, :], P)
                last.then_inc(sm["c_tr"], 1)
                wait(pe, l, "h_done", 1)
                in_section("v", 0, 1)
                wait(pe, l, "kv_ev", 1)
                wait(pe, l, "c_ev", 1)
                for hd in range(HEADS):
                    for m in range(2):
                        j = 2 * hd + m
                        last = transpose(mp[:, 2 + j // 4, (j % 4) * P:(j % 4 + 1) * P], ktok[:, m, hd * P:(hd + 1) * P], P)
                last.then_inc(sm["kT_tr"], 1)
                in_section("v", 1, 1)
                in_section("q", 0, 2)

                def scores(i):
                    if i < 2:
                        wait(pe, l, "q_ev", 4)
                        wait(pe, l, "kT_ev", 1)
                        wait(pe, l, "s0_ev", 1)
                        if i:
                            wait(pe, l, "qrow_ev", 1)
                            pe.sem_inc(entered, 1)
                    else:
                        wait(pe, l, "pT_ev", i - 1)
                    for hd in range(HEADS):
                        last = pe.matmul(mp[:, 2 * (i % 2) + hd // 2, (hd % 2) * MEM:(hd % 2 + 1) * MEM],
                                         q[:, hd, i // 2, (i % 2) * P:(i % 2 + 1) * P], kT[:, hd, :], start=True, stop=True)
                    last.then_inc(sm["sc_done"], 1)

                def turn_probabilities(i):
                    wait(pe, l, "p_norm", i + 1)
                    for hd in range(HEADS):
                        for m in range(2):
                            j = 2 * hd + m
                            last = transpose(mp[:, 2 * (i % 2) + j // 4, (j % 4) * P:(j % 4 + 1) * P],
                                             pr[:, i % 2, hd, m * P:(m + 1) * P], P)
                    last.then_inc(sm["pT_tr"], 1)

                scores(0)
                wait(pe, l, "qs_done", 1)
                for hd in range(HEADS):
                    last = transpose(mp[0:NB, 2, hd * P:(hd + 1) * P], qs[:, hd, :], P)
                last.then_inc(sm["qrow_tr"], 1)
                scores(1)
                in_section("u", 0, 1)
                turn_probabilities(0)
                turn_probabilities(1)
                scores(2)
                scores(3)
                in_section("u", 1, 1)
                turn_probabilities(2)
                turn_probabilities(3)
                for hd in range(HEADS):
                    wait(pe, l, "pT_ev", 3 if hd < 2 else 4)
                    if hd == 0:
                        wait(pe, l, "pT_ev", 4)
                    for m in range(2):
                        last = pe.matmul(mp[:, hd, :], vtok[:, m, hd * P:(hd + 1) * P], pT[:, hd, m, :], start=(m == 0), stop=(m == 1))
                last.then_inc(sm["pv_done"], 1)

                def spread(first):
                    for b in range(first, first + 4):
                        if b >= 4:
                            wait(pe, l, "kq_done", b - 3)
                        pe.matmul(mp[:, b % 4, :], ident[0:NB, b:b + 1].to_broadcast([NB, P]), qrow[:, :],
                                  start=True, stop=True).then_inc(sm["bc_done"], 1)

                wait(pe, l, "pv_ev", 1)
                pe.sem_inc(entered, 1)
                spread(0)
                in_section("vb", 2, 1)
                spread(4)
                in_section("vb", 3, 1)
                wait(pe, l, "kq_done", NB)
                for m in range(2):
                    last = transpose(mp[0:32, 0, m * P:(m + 1) * P], sK[:, m, :], P)
                last.then_inc(sm["scs_done"], 1)
                in_unit("zx", 0)
                wait(pe, l, "ps_norm", 1)
                pe.sem_inc(entered, 1)
                for m in range(2):
                    last = transpose(mp[:, 3, m * 32:(m + 1) * 32], ps[:, m * P:(m + 1) * P], 32)
                last.then_inc(sm["psT_tr"], 1)
                wait(pe, l, "pm_ev", 1)
                for b in range(NB):
                    wait(pe, l, f"kb_in{b % 4}", 16 * (2 + b // 4 + 1))
                    for m in range(2):
                        last = pe.matmul(mp[0:32, 2, :], pm[:, m, b, :], kb[:, b % 4, m, :],
                                         start=(b == 0 and m == 0), stop=(b == NB - 1 and m == 1))
                    last.then_inc(sm["pvs_done"], 1)
                wait(pe, l, "oxs_ev", 1)
                pe.sem_inc(entered, 1)
                for hd in range(HEADS):
                    last = transpose(mp[:, 3, hd * 32:(hd + 1) * 32], oxs[:, hd * P:(hd + 1) * P], 32)
                last.then_inc(sm["oxT_tr"], 1)

                def state_inputs(f):
                    wait(pe, l, "wt_done", f + 1)
                    wait(pe, l, *(("k_free", 1), ("y_ev", 4))[f])
                    for ri in range(2):
                        for r in range(QH):
                            last = transpose(mp[:, r // 4 * 2 + ri, (r % 4) * P:(r % 4 + 1) * P], wt[:, ri, r, :], P)
                    last.then_inc(sm["w_tr"], 1)
                    wait(pe, l, "U_in", 16 * 12)
                    for h in range(2):
                        wait(pe, l, "wl_ev", 2 * f + h + 1)
                        for e, r in ((e, r) for e in range(2) for r in range(4 * h, 4 * h + 4)):
                            last = pe.matmul(mp[:, 2 * h + e, (r % 4) * YC:(r % 4 + 1) * YC],
                                             wl[:, r, e, :], U[:, f * QH + r, e, NB:UC], start=True, stop=True)
                    last.then_inc(sm["s_done"], 1)

                def lag_matrices(f):
                    wait(pe, l, "V_done", f + 1)
                    wait(pe, l, *(("ox_done", 1), ("s_free", 4))[f])
                    pe.sem_inc(entered, 1)
                    for r in range(QH):
                        for ri in range(2):
                            last = pe.matmul(mp[0:2 * H, r // 4, (r % 4) * P:(r % 4 + 1) * P],
                                             bd[:, ri, f * QH + r, :, :].rearrange("p e h -> p (e h)"),
                                             V[:, ri, r, 0:T, :].rearrange("p t h -> p (t h)"),
                                             start=(ri == 0), stop=(ri == 1))
                    last.then_inc(sm["k_done"], 1)

                def outputs(f):
                    wait(pe, l, "m_in", 128 * (f + 1))
                    wait(pe, l, *(("s_free", 2), ("k_free", 2))[f])
                    for e, r in ((e, r) for e in range(2) for r in range(QH)):
                        pe.matmul(mp[:, 2 * e + r // 4, (r % 4) * YC:(r % 4 + 1) * YC], Mt[:, 2 * r + e, :],
                                  U[:, f * QH + r, e, 0:YC], start=(r % 4 == 0), stop=False)
                    wait(pe, l, "V2_done", f + 1)
                    wait(pe, l, "x_done", f + 1)
                    if f == 0:
                        wait(pe, l, "X2_done", 1)
                    for e, r in ((e, r) for e in range(2) for r in range(QH)):
                        last = pe.matmul(mp[:, 2 * e + r // 4, (r % 4) * YC:(r % 4 + 1) * YC], V2[:, r, e, :],
                                         X2[:, r, e, :], start=False, stop=(r % 4 == 3))
                    last.then_inc(sm["y_done"], 1)

                lag_matrices(0)
                state_inputs(0)
                in_unit("zx", 1)
                in_section("zx", 1, 1)
                outputs(0)
                in_unit("za", 0)
                state_inputs(1)
                lag_matrices(1)
                in_unit("za", 1)
                in_section("za", 1, 1)
                outputs(1)
                wait(pe, l, "y_ev", 8)
                wait(pe, l, "sn_done", 1)
                for ri in range(2):
                    transpose(mp[0:Q, 0, ri * P:(ri + 1) * P], sf[:, ri, :], P)
                for ri in range(2):
                    last = transpose(mp[:, 0, (2 + ri) * P:(3 + ri) * P], sn[:, ri, :, :].rearrange("p b q -> p (b q)"), P)
                last.then_inc(sm["sfin_tr"], 1)
                wait(pe, l, "st_in", 32)
                for r in range(2):
                    for i in range(ET):
                        last = transpose(mp[:, 1 + r, i * 120:(i + 1) * 120], crw[:, r, i * P:(i + 1) * P], 120)
                last.then_inc(sm["st_tr"], 1)
                wait(pe, l, "v_last_done", 4)
                for i in range(ET):
                    last = transpose(mp[0:32, 3, i * P:(i + 1) * P], v_last[:, i, :], P)
                last.then_inc(sm["vs_tr"], 1)
                wait(pe, l, "sfin_ev", 1)
                for i in range(ET):
                    last = transpose(mp[0:NB, 0, i * P:(i + 1) * P], v_s[:, i, :], P)
                last.then_inc(sm["vs_tr"], 1)
                in_section("zb", 0, 1)
                wait(pe, l, "acc_done", ET)
                wait(pe, l, "vs_ev", 1)
                for i in range(ET):
                    for a in range(2):
                        last = pe.matmul(mp[:, a, 0:HC], ones[:, :], acc(i)[:, a, :], start=(i == 0), stop=(i == ET - 1))
                last.then_inc(sm["mean_done"], 1)
                in_section("zb", 1, 1)
                for i in range(ET):
                    wait(pe, l, "lsq_done", i + 1)
                    for a in range(2):
                        last = pe.matmul(mp[:, 2 + a, 0:HC], ones[:, :], lsq(i)[:, a, :], start=(i == 0), stop=(i == ET - 1))
                last.then_inc(sm["lsq_used"], 1)

                wait(pe, l, "y_in", 16)
                for g in range(2):
                    wait(pe, l, f"d_loaded{g}", 80)
                    for j in range(2):
                        wait(pe, l, f"acc_free{j}", use["glu"] // 2 + g + 1)
                        for k in range(ET):
                            for a in range(2):
                                last = pe.matmul(acc_ps[j][:, a, 0:HC], w_dir[:, g, k * 2 * P + j * P:k * 2 * P + (j + 1) * P],
                                                 u[:, k, a, :], start=(k == 0), stop=(k == ET - 1))
                        last.then_inc(acc_ready[j], 1)
                pe.sem_inc(entered, 1)
                with pe.Fori(0, 2) as it:
                    for m in range(18):
                        x, n = m // 3 % 3, l * UNITS + unit["gates"] + it * 18 + m
                        if m % 3 < 2:
                            split_product(m % 3, it * 6 + use["gates"] // 2 + m // 3, m % 2, n, h_hi, h_lo)
                            continue
                        wait(pe, l, ("br_a_done", "br_b_done", "br_x_done")[x], (4, 4, 1)[x])
                        pe.wait_ge(w_staged_free, n + 3)
                        for jj in range(2):
                            wait(pe, l, "b_free", it * 12 + m // 3 * 2 + jj + 1)
                            for k in range(ET):
                                c0 = (k * 2 + jj) * P
                                for p, (w, b) in enumerate(((w_hi, br_hi), (w_lo, br_hi), (w_hi, br_lo))):
                                    for a in range(2):
                                        last = pe.matmul(mp[:, 2 * jj + a, 0:HC], w[:, m % 2, c0:c0 + P], b[:, x, k, a, :],
                                                         start=(k == 0 and p == 0), stop=(k == ET - 1 and p == 2))
                            last.then_inc(sm["b_ready"], 1)
                wait(pe, l, "m_done", 6)
                pe.sem_inc(entered, 1)
                with pe.Fori(0, 4) as it:
                    for k in range(2):
                        split_product(k, it + use["out"] // 2, k, l * UNITS + unit["out"] + it * 2 + k, m_hi, m_lo, "m_done")

            pe.wait_ge(sm["x_sum"], LAYERS * KT)
            for i in range(4):
                for k in range(KT):
                    last = transpose(token_banks(i)[:, k // 4, (k % 4) * P:(k % 4 + 1) * P],
                                     xT[:, k, i // 2, (i % 2) * P:(i % 2 + 1) * P], P)
                last.then_inc(sm["fin_tr"], 1)
            pe.wait_ge(sm["fin_y"], 2)
            for k in range(KT):
                last = transpose(mp[0:NB, k // 4, (k % 4) * P:(k % 4 + 1) * P], xsc[:, k, :], P)
            last.then_inc(sm["fin_tr"], 1)

        @block.scalar
        def _(act):
            steps = Steps(act, act_steps)
            act.wait_ge(sm["mem_in"], 16)
            for m in range(2):
                steps.run(act.activation(memn0[:, 0:4, :].rearrange("p k m -> p (k m)"), mrow[:, m, :], ACT.Square,
                                         accum_out=stat[:, m:m + 1]))
            act.sem_inc(sm["mem_sq"], 1)
            act.wait_ge(sm["mem_var"], 1)
            act.activation(stat[:, 2:4], stat[:, 4:6], ACT.Sqrt).then_inc(sm["mem_rt"], 1)
            for i in range(4):
                act.wait_ge(sm["x_tr"], i + 1)
                act.activation(xT[:, :, i // 2, (i % 2) * P:(i % 2 + 1) * P],
                               mp[:, 2 * (i % 2):2 * (i % 2) + 2, :].rearrange("p b (k c) -> p (b k) c", c=P), ACT.Copy).then_inc(sm["x_ev"], 1)
            act.wait_ge(sm["x_tr"], 5)
            act.activation(xT[:, :, :, 4 * C:HC], mp[:, 0, 0:KT * NB].rearrange("p (k a c) -> p k a c", a=2, c=4), ACT.Copy).then_inc(sm["x_ev"], 1)
            for m in range(2):
                act.wait_ge(sm["mem_tr"], m + 1)
                act.activation(memn0[:, :, m * P:(m + 1) * P],
                               mp[:, 2 * (1 - m):2 * (1 - m) + 2, :].rearrange("p b (k c) -> p (b k) c", c=P), ACT.Copy).then_inc(sm["mem_ev"], 1)
            act.wait_ge(sm["mem_ev"], 2)
            act.dma_start(m_dram, memn0[:, :, :].rearrange("p k m -> p (k m)")).then_inc(sm["mem_out"], 16)
            steps.clear()
            act.wait_ge(sm["x_ev"], 5)
            for k in range(KT):
                act.activation(sq[:, k, :, :], xT[:, k, :, :], ACT.Square).then_inc(sm["sq_done"], 1)

            with act.Fori(0, LAYERS) as l:
                def high(slot, loads):
                    act.wait_ge(w_loaded[slot], loads * 16)
                    act.copy(w_hi[:, slot, :], w_st[:, slot, :]).then_inc(w_hi_done, 1)

                def one(name, i, evac):
                    wait(act, l, f"acc_ready{i % 2}", (use[name] + i) // 2 + 1)
                    high(i % 2, l * (UNITS // 2) + (unit[name] + i) // 2 + 2)
                    evac(0, i)

                def section(name, first, pairs, evac):
                    act.sem_inc(entered, 1)
                    with act.Fori(first, first + pairs) as it:
                        for k in range(2):
                            wait(act, l, f"acc_ready{k}", it + use[name] // 2 + 1)
                            high(k, l * (UNITS // 2) + unit[name] // 2 + it + 2)
                            evac(it, k)

                high(0, l * (UNITS // 2) + 1)
                high(1, l * (UNITS // 2) + 1)
                wait(act, l, "var_done", 1)
                act.activation(rs[:, :, :], rs[:, :, :], ACT.Sqrt).then_inc(sm["rstd_done"], 1)
                for k in range(KT):
                    wait(act, l, "ht_done", k + 1)
                    act.copy(h_hi[:, k, :, :], ht[:, k % 2, :, :]).then_inc(sm["hhi_done"], 1)
                wait(act, l, "par_ev", 1)
                act.activation(tiny[:, 0, :], vec[:, 64:80], ACT.Exp).then_inc(sm["dt_exp"], 1)
                wait(act, l, "sin_arg", 1)
                act.activation(tiny[:, 3, :], tiny[:, 1, :], ACT.Exp)
                act.activation(tiny[:, 7:9, :], tiny[:, 5:7, :], ACT.Sin).then_inc(sm["par_act"], 1)
                wait(act, l, "acc_ready0", 1)
                act.copy(ktok[:, :, :], acc_ps[0][:, :, :]).then_inc(sm["kv_ev"], 1)
                wait(act, l, "kv_ev", 1)
                act.sem_inc(acc_free[0], 1)
                wait(act, l, "acc_ready1", 1)
                act.copy(vtok[:, :, :], acc_ps[1][:, :, :]).then_inc(sm["kv_ev"], 1)
                wait(act, l, "kv_ev", 2)
                act.sem_inc(acc_free[1], 1)

                def tile(ap, i):
                    return ap[:, bass.ds(i, 1), :, :].rearrange("p i a c -> p (i a) c")

                def to_q(it, k):
                    act.copy(tile(q, it * 2 + k), acc_ps[k][:, :, 0:HC]).then_inc(acc_free[k], 1)

                def to_v(i):
                    name = "v" if i < 2 else "vb"
                    base = l * (UNITS // 2) + unit[name] // 2 + i + 2
                    wait(act, l, "acc_ready0", use[name] // 2 + i + 1)
                    high(0, base)
                    wait(act, l, "sg_free", i + 1)
                    act.activation(sg[:, i % 2, :, :], acc_ps[0][:, :, 0:HC], ACT.Sigmoid).then_inc(sm["val_ev"], 1)
                    wait(act, l, "val_ev", 2 * i + 1)
                    act.sem_inc(acc_free[0], 1)
                    wait(act, l, "acc_ready1", use[name] // 2 + i + 1)
                    high(1, base)
                    for a in range(2):
                        act.copy(vx[:, i, 8 + 4 * a:12 + 4 * a, 4:4 + C], acc_ps[1][:, a, 0:4 * C].rearrange("p (b c) -> p b c", c=C))
                    act.copy(v_s[:, i, :].rearrange("p (a c) -> p a c", a=2), acc_ps[1][:, :, 4 * C:HC]).then_inc(sm["val_ev"], 1)
                    wait(act, l, "val_ev", 2 * i + 2)
                    act.sem_inc(acc_free[1], 1)

                to_v(0)
                wait(act, l, "kT_tr", 1)
                act.copy(kT[:, :, :].rearrange("p h m -> p (h m)"), mp[:, 2:4, :].rearrange("p b c -> p (b c)")).then_inc(sm["kT_ev"], 1)
                to_v(1)
                section("q", 0, 2, to_q)
                wait(act, l, "acc_free1", use["u"] // 2 + 1)
                act.sem_inc(sm["q_ev"], 4)

                def exps(i):
                    wait(act, l, "nb_done", i + 1)
                    if i >= 2:
                        wait(act, l, "pT_tr", i - 1)
                    for hd in range(HEADS):
                        last = act.activation(pr[:, i % 2, hd, :], mp[:, 2 * (i % 2) + hd // 2, (hd % 2) * MEM:(hd % 2 + 1) * MEM],
                                              ACT.Exp, bias=stat[:, 16 + 4 * i + hd:17 + 4 * i + hd], scale=SCALE,
                                              accum_out=stat[:, 32 + 4 * i + hd:33 + 4 * i + hd])
                    last.then_inc(sm["exp_done"], 1)

                def keep_probabilities(i):
                    wait(act, l, "pT_tr", i + 1)
                    act.copy(pT[:, :, :, i * P:(i + 1) * P],
                             mp[:, 2 * (i % 2):2 * (i % 2) + 2, :].rearrange("p b (n c) -> p (b n) c", c=P)
                             .rearrange("p (h m) c -> p h m c", m=2)).then_inc(sm["pT_ev"], 1)

                wait(act, l, "qrow_tr", 1)
                act.copy(qrow[:, :], mp[0:NB, 2, :]).then_inc(sm["qrow_ev"], 1)
                exps(0)
                exps(1)
                wait(act, l, "s0_ev", 1)
                wait(act, l, "par_ev", 1)

                def to_u(it, k):
                    act.copy(tile(u, it * 2 + k), acc_ps[k][:, :, 0:HC]).then_inc(acc_free[k], 1)

                section("u", 0, 1, to_u)
                keep_probabilities(0)
                keep_probabilities(1)
                exps(2)
                exps(3)

                section("u", 1, 1, to_u)
                wait(act, l, "acc_free1", use["u"] // 2 + 3)
                act.sem_inc(sm["u_ev"], 4)
                keep_probabilities(2)
                keep_probabilities(3)
                wait(act, l, "pv_done", 1)
                act.copy(g3(q), mp[:, :, :].rearrange("p h (a c) -> p h a c", a=2)).then_inc(sm["pv_ev"], 1)
                to_v(2)
                to_v(3)
                wait(act, l, "nbs_done", 1)
                act.activation(ps[:, :], mp[0:32, 0, 0:MEM], ACT.Exp, bias=stat[0:32, 48:49], scale=SCALE,
                               accum_out=stat[0:32, 49:50]).then_inc(sm["exps_done"], 1)

                def to_z(x):
                    def evac(it, k):
                        act.activation(tile(z[:, x, :, :, :], it * 2 + k), acc_ps[k][:, :, 0:HC], ACT.Silu).then_inc(acc_free[k], 1)
                    return evac

                one("zx", 0, to_z(2))
                wait(act, l, "pvs_done", NB)
                act.copy(oxs[:, :], mp[0:32, 2, :]).then_inc(sm["oxs_ev"], 1)

                def turned_inputs(f):
                    wait(act, l, "w_tr", f + 1)
                    for h in range(2):
                        act.copy(wl[:, 4 * h:4 * h + 4, :, :].rearrange("p q e (a s) -> p a (q e) s", a=2),
                                 mp[:, 2 * h:2 * h + 2, :].rearrange("p b (x s) -> p b x s", s=S)).then_inc(sm["wl_ev"], 1)

                def gelu_outputs(f):
                    wait(act, l, "y_done", f + 1)
                    for e in range(2):
                        for b in range(2):
                            act.activation(U[:, f * QH + 4 * b:f * QH + 4 * b + 4, e, 0:YC],
                                           mp[:, 2 * e + b, 0:4 * YC].rearrange("p (q c) -> p q c", c=YC),
                                           ACT.Gelu_apprx_tanh).then_inc(sm["y_ev"], 1)

                def take_last_pairs(f):
                    wait(act, l, "s_done", f + 1)
                    for e, ri in ((0, 0), (0, 1), (1, 0), (1, 1)):
                        last = act.copy(X[e * S:(e + 1) * S, ri, 4:8, NB + 1:],
                                        mp[ri * S:(ri + 1) * S, 2 + e, 0:4 * YC].rearrange("p (q c) -> p q c", c=YC))
                    last.then_inc(sm["s_turned"], 1)
                    wait(act, l, "s_turned", f + 1)
                    act.sem_inc(sm["s_free"], 1)

                def turned_outputs(f):
                    wait(act, l, "V_done", f + 1)
                    for e in range(2):
                        for ri in range(2):
                            last = act.copy(V2[ri * S:(ri + 1) * S, :, e, :],
                                            V[e * S:(e + 1) * S, ri, :, 1:T + 1, :].rearrange("p q t h -> p q (t h)"))
                    last.then_inc(sm["V2_done"], 1)

                turned_inputs(0)
                take_last_pairs(0)
                turned_outputs(0)
                one("zx", 1, to_z(2))
                section("zx", 1, 1, to_z(2))
                wait(act, l, "x_scan", 1)
                for ri in range(2):
                    last = act.copy(X2[ri * S:(ri + 1) * S, :, 1, :], X[S:2 * S, ri, :, 0:YC])
                last.then_inc(sm["X2_done"], 1)
                gelu_outputs(0)
                turned_inputs(1)
                wait(act, l, "x_done", 1)
                take_last_pairs(1)
                turned_outputs(1)
                wait(act, l, "k_free", 2)
                section("za", 0, 2, to_z(0))
                gelu_outputs(1)
                wait(act, l, "sfin_tr", 1)
                act.copy(so[0:Q, 0:2, :].rearrange("p a c -> p (a c)"), mp[0:Q, 0, 0:2 * P])
                act.copy(so[:, 2:4, :].rearrange("p a c -> p (a c)"), mp[:, 0, 2 * P:4 * P]).then_inc(sm["sfin_ev"], 1)
                wait(act, l, "vs_tr", 2)
                act.copy(nrow[0:32, :], mp[0:32, 3, :])
                act.copy(nrow[32:32 + NB, :], mp[0:NB, 0, :]).then_inc(sm["vs_ev"], 1)
                section("zb", 0, 1, to_z(1))
                for i in range(ET):
                    wait(act, l, "cent_done", i + 1)
                    act.activation(lsq(i), acc(i), ACT.Square).then_inc(sm["lsq_done"], 1)
                section("zb", 1, 1, to_z(1))
                wait(act, l, "acc_free1", use["glu"] // 2 + 1)
                act.sem_inc(sm["z_ev"], 1)

                def glu_gate(i):
                    wait(act, l, f"acc_ready{i % 2}", use["glu"] // 2 + i // 2 + 1)
                    wait(act, l, "sg_free", 4 + i + 1)
                    act.activation(sg[:, i % 2, :, :], acc_ps[i % 2][:, :, 0:HC], ACT.Sigmoid,
                                   bias=vec[:, 16 + i:17 + i]).then_inc(sm["glu_sg"], 1)
                    wait(act, l, "glu_sg", i + 1)
                    act.sem_inc(acc_free[i % 2], 1)

                glu_gate(0)
                glu_gate(1)
                wait(act, l, "lvar_done", 1)
                act.activation(lst[:, :, :], lst[:, :, :], ACT.Sqrt).then_inc(sm["lrstd_done"], 1)
                glu_gate(2)
                glu_gate(3)
                for i in range(ET):
                    wait(act, l, "ln_done", i + 1)
                    act.activation(acc(i), acc(i), ACT.Silu, bias=vec[:, 28 + i:29 + i]).then_inc(sm["ln_silu"], 1)
                with act.Fori(0, 2) as it:
                    for m in range(18):
                        ahead = l * (UNITS // 2) + unit["gates"] // 2 + it * 9 + m // 2 + 2
                        if m % 3 == 2:
                            wait(act, l, "b_ready", it * 12 + m // 3 * 2 + 2)
                            high(m % 2, ahead)
                            continue
                        wait(act, l, f"acc_ready{m % 3}", it * 6 + use["gates"] // 2 + m // 3 + 1)
                        high(m % 2, ahead)
                        g = m // 3 * 2 + m % 3
                        wait(act, l, "sg_free", it * 12 + 8 + g + 1)
                        act.activation(sg[:, m % 3, :, :], acc_ps[m % 3][:, :, 0:HC], ACT.Sigmoid).then_inc(sm["gate_sg"], 1)
                        wait(act, l, "gate_sg", it * 12 + g + 1)
                        act.sem_inc(acc_free[m % 3], 1)
                def square(j):
                    wait(act, l, "x_sum", j + 1)
                    act.activation(tile(sq, j), tile(xT, j), ACT.Square).then_inc(sm["sq_done"], 1)

                with act.Fori(0, 3) as it:
                    for k in range(2):
                        wait(act, l, f"acc_ready{k}", it + use["out"] // 2 + 1)
                        high(k, l * (UNITS // 2) + unit["out"] // 2 + it + 2)
                        square(it * 2 + k)
                for k in range(2):
                    square(6 + k)

            for i in range(4):
                act.wait_ge(sm["fin_tr"], i + 1)
                act.activation(yrow[:, i, :], token_banks(i).rearrange("p b c -> p (b c)"), ACT.Square,
                               accum_out=stat[:, i:i + 1]).then_inc(sm["fin_sq"], 1)
            act.wait_ge(sm["fin_var"], 1)
            act.activation(stat[:, 8:12], stat[:, 8:12], ACT.Sqrt).then_inc(sm["fin_rt"], 1)
            act.wait_ge(sm["fin_tr"], 5)
            act.activation(ysr[:, :], mp[0:NB, 0:2, :].rearrange("p b c -> p (b c)"), ACT.Square,
                           accum_out=stat[0:NB, 16:17]).then_inc(sm["fin_sq"], 1)
            act.wait_ge(sm["fin_var"], 2)
            act.activation(stat[0:NB, 18:19], stat[0:NB, 18:19], ACT.Sqrt).then_inc(sm["fin_rt"], 1)

        @block.vector
        def _(dve):
            steps = Steps(dve, dve_steps)
            run = steps.run

            def tt(out, a, b, op, behind=0):
                run(dve.tensor_tensor(out, a, b, op), behind)

            def ts(out, a, s1, s2, op0, op1, behind=0):
                run(dve.tensor_scalar(out, a, s1, s2, op0, op1), behind)

            def stt(out, a, s, b, op0, op1, behind=0):
                run(dve.scalar_tensor_tensor(out=out, in0=a, scalar=s, in1=b, op0=op0, op1=op1), behind)

            def cmul(dr, di, xr, xi, yr, yi, a, b):
                tt(a, xr, yr, ALU.mult)
                tt(b, xi, yi, ALU.mult)
                tt(b, a, b, ALU.subtract)
                tt(a, xr, yi, ALU.mult)
                tt(di, xi, yr, ALU.mult)
                tt(di, a, di, ALU.add)
                run(dve.tensor_copy(dr, b))

            dve.wait_ge(sm["mem_sq"], 1)
            ts(stat[:, 6:8], stat[:, 0:2], 1.0 / D, EPS, ALU.mult, ALU.add)
            dve.reciprocal(stat[:, 4:6], stat[:, 6:8]).then_inc(sm["mem_var"], 1)
            dve.wait_ge(sm["mem_rt"], 1)
            for m in range(2):
                dve.tensor_scalar(mrow[:, m, :], mrow[:, m, :], stat[:, 2 + m:3 + m], None, ALU.mult).then_inc(sm["mem_nrm"], 1)
            dve.wait_ge(sm["mem_nrm"], 2)
            dve.wait_ge(sm["consts"], 3)
            tt(eye2[:, :], ident[0:2 * H, 0:H], ident[0:2 * H, H:2 * H], ALU.add)
            steps.clear()

            for i in range(2):
                dve.sem_inc(acc_free[i], 1)
            dve.sem_inc(sm["sg_free"], 2)
            dve.sem_inc(sm["b_free"], 2)

            with dve.Fori(0, LAYERS) as l:
                wait(dve, l, "dt_in", 16)
                dve.tensor_copy(prow[64:80, :].rearrange("q (e p) -> q e p", e=2),
                                dtrow[64:80, :].unsqueeze(2).to_broadcast([16, 2, S])).then_inc(sm["dt_wide"], 1)
                wait(dve, l, "par_tr", 1)
                run(dve.tensor_copy(vec[:, :], mp[:, 2, 0:80]))
                run(dve.tensor_copy(cw[:, :], mp[:, 2, P:P + TAPS * ET]))
                dve.tensor_copy(dcol[:, :], mp[0:2 * H, 2, 256:256 + Q]).then_inc(sm["par_ev"], 1)
                wait(dve, l, "par_ev", 1)
                wait(dve, l, "mg_in", 16)
                for k in range(KT):
                    run(dve.tensor_scalar(memg[:, k, :], memn[:, k, :], vec[:, 56 + k:57 + k], None, ALU.mult))
                dve.sem_inc(sm["memg_done"], 1)
                wait(dve, l, "sq_used", 1)
                ts(rs[:, :, :], mp[:, 0:2, 0:HC], 1.0 / D, EPS, ALU.mult, ALU.add)
                dve.reciprocal(rs[:, :, :], rs[:, :, :]).then_inc(sm["var_done"], 1)
                wait(dve, l, "rstd_done", 1)

                def h_low(k):
                    wait(dve, l, "hhi_done", k + 1)
                    run(dve.tensor_tensor(h_lo[:, k, :, :], ht[:, k % 2, :, :], h_hi[:, k, :, :].bitcast(F32), ALU.subtract))

                for k in range(KT):
                    if k >= 2:
                        h_low(k - 2)
                    stt(ht[:, k % 2, :, :], xT[:, k, :, :], vec[:, 48 + k:49 + k], rs[:, :, :], ALU.mult, ALU.mult)
                    dve.sem_inc(sm["ht_done"], 1)
                h_low(KT - 2)
                h_low(KT - 1)
                dve.sem_inc(sm["h_done"], 1)
                are, aim = vec[:, 0:16], vec[:, 32:48]
                wait(dve, l, "dt_exp", 1)
                tt(tiny[:, 1, :], are, tiny[:, 0, :], ALU.mult)
                tt(tiny[:, 2, :], aim, tiny[:, 0, :], ALU.mult)
                ts(tiny[:, 4, :], tiny[:, 2, :], 1.0 / TWO_PI, ROUND, ALU.mult, ALU.add)
                run(dve.tensor_scalar(tiny[:, 4, :], tiny[:, 4, :], ROUND, None, ALU.subtract))
                stt(tiny[:, 5, :], tiny[:, 4, :], -PI2_HI, tiny[:, 2, :], ALU.mult, ALU.add)
                stt(tiny[:, 5, :], tiny[:, 4, :], -PI2_MID, tiny[:, 5, :], ALU.mult, ALU.add)
                stt(tiny[:, 5, :], tiny[:, 4, :], -PI2_LO, tiny[:, 5, :], ALU.mult, ALU.add)
                ts(tiny[:, 5, :], tiny[:, 5, :], PI_BELOW, -PI_BELOW, ALU.min, ALU.max)
                run(dve.tensor_scalar(tiny[:, 6, :], tiny[:, 5, :], -1.0, None, ALU.mult))
                tt(tiny[:, 6, :], tiny[:, 6, :], tiny[:, 5, :], ALU.min)
                run(dve.tensor_scalar(tiny[:, 6, :], tiny[:, 6, :], TWO_PI / 4, None, ALU.add))
                dve.sem_inc(sm["sin_arg"], 1)
                wait(dve, l, "par_act", 1)
                run(dve.memset(pw[:, 0, :, 0], 1.0))
                run(dve.memset(pw[:, 1, :, 0], 0.0))
                tt(pw[:, 0, :, 1], tiny[:, 3, :], tiny[:, 8, :], ALU.mult)
                tt(pw[:, 1, :, 1], tiny[:, 3, :], tiny[:, 7, :], ALU.mult)
                tt(tiny[:, 5, :], are, are, ALU.mult)
                tt(tiny[:, 6, :], aim, aim, ALU.mult)
                tt(tiny[:, 5, :], tiny[:, 5, :], tiny[:, 6, :], ALU.add)
                run(dve.reciprocal(tiny[:, 5, :], tiny[:, 5, :]))
                run(dve.tensor_scalar(tiny[:, 6, :], pw[:, 0, :, 1], 1.0, None, ALU.subtract))
                tt(tiny[:, 7, :], tiny[:, 6, :], are, ALU.mult)
                tt(tiny[:, 8, :], pw[:, 1, :, 1], aim, ALU.mult)
                tt(tiny[:, 7, :], tiny[:, 7, :], tiny[:, 8, :], ALU.add)
                tt(tiny[:, 9, :], tiny[:, 7, :], tiny[:, 5, :], ALU.mult)
                tt(tiny[:, 7, :], pw[:, 1, :, 1], are, ALU.mult)
                tt(tiny[:, 8, :], tiny[:, 6, :], aim, ALU.mult)
                tt(tiny[:, 7, :], tiny[:, 7, :], tiny[:, 8, :], ALU.subtract)
                tt(tiny[:, 10, :], tiny[:, 7, :], tiny[:, 5, :], ALU.mult)
                wait(dve, l, "s0_tr", 1)
                dve.tensor_copy(s0[:, :, :, :].rearrange("p a b q -> p (a b q)"), mp[:, 0, 0:2 * P]).then_inc(sm["s0_ev"], 1)
                wait(dve, l, "c_tr", 1)
                dve.tensor_copy(cT[:, :, :, :].rearrange("p a q h -> p (a q h)"), mp[:, 3, :]).then_inc(sm["c_ev"], 1)
                wait(dve, l, "s0_ev", 1)
                wait(dve, l, "c_ev", 1)

                for lo in (1, 2, 4):
                    a = tiny[:, 0:lo, :].rearrange("p k q -> p q k")
                    b = tiny[:, 4:4 + lo, :].rearrange("p k q -> p q k")
                    cmul(pw[:, 0, :, lo + 1:2 * lo + 1], pw[:, 1, :, lo + 1:2 * lo + 1], pw[:, 0, :, 1:lo + 1], pw[:, 1, :, 1:lo + 1],
                         pw[:, 0, :, lo:lo + 1].to_broadcast([P, Q, lo]), pw[:, 1, :, lo:lo + 1].to_broadcast([P, Q, lo]), a, b)
                run(dve.tensor_copy(lv[:, 0, :, :], pw[:, :, :, T]))
                for k in range(5):
                    cmul(lv[:, k + 1, 0, :], lv[:, k + 1, 1, :], lv[:, k, 0, :], lv[:, k, 1, :], lv[:, k, 0, :], lv[:, k, 1, :],
                         tiny[:, 0, :], tiny[:, 4, :])
                run(dve.tensor_scalar(li[:, :, 0, :], lv[:, :, 1, :], -1.0, None, ALU.mult), behind=1)
                run(dve.tensor_copy(li[:, :, 1, :], lv[:, :, 1, :]))

                def scores_max(i):
                    wait(dve, l, "sc_done", i + 1)
                    run(dve.tensor_reduce(stat[:, 4 * i:4 * i + 4],
                                          mp[:, 2 * (i % 2):2 * (i % 2) + 2, :].rearrange("p b (h m) -> p (b h) m", m=MEM), op=ALU.max, axis=AX.X))
                    run(dve.tensor_scalar(stat[:, 16 + 4 * i:20 + 4 * i], stat[:, 4 * i:4 * i + 4], -SCALE, None, ALU.mult))
                    dve.sem_inc(sm["nb_done"], 1)

                def probabilities(i):
                    wait(dve, l, "exp_done", i + 1)
                    run(dve.reciprocal(stat[:, 52:56], stat[:, 32 + 4 * i:36 + 4 * i]))
                    tt(pr[:, i % 2, :, :], pr[:, i % 2, :, :], stat[:, 52:56].unsqueeze(2).to_broadcast([P, HEADS, MEM]), ALU.mult)
                    dve.sem_inc(sm["p_norm"], 1)

                taps = cw[:, :].rearrange("p (k i) -> p i k", i=ET)

                def convolution(i, first, end):
                    if first == 0:
                        wait(dve, l, "v_done", i + 1)
                        run(dve.tensor_copy(v_last[:, i, :].rearrange("p (c t) -> p c t", t=T), vx[:, i, 8:16, C:C + 4].rearrange("p t c -> p c t")))
                        dve.sem_inc(sm["v_last_done"], 1)
                        run(dve.memset(vx[:, i, :, 0:4], 0.0))
                        run(dve.tensor_copy(vx[:, i, 0:8, 4:], vx[:, i, 8:16, 3:3 + C]))
                    for k in range(first, end):
                        src = vx[:, i, 8 - k % 8:16 - k % 8, 4 - k // 8:4 - k // 8 + C]
                        w = taps[:, i, TAPS - 1 - k:TAPS - k]
                        o = cacc[:, k % 2, :, :]
                        if k == 0:
                            ts(o, src, w, vec[:, 20 + i:21 + i], ALU.mult, ALU.add, behind=1)
                        elif k == 1:
                            run(dve.tensor_scalar(o, src, w, None, ALU.mult), behind=1)
                        else:
                            stt(o, src, w, o, ALU.mult, ALU.add, behind=int(k < end - 1))
                    if end == TAPS:
                        even, odd = (cacc[:, x, :, :].rearrange("p (a b) c -> p a (b c)", a=2) for x in range(2))
                        tt(cv[:, i, 0, :, 0:4 * C], even, odd, ALU.add)

                convolution(0, 0, TAPS)
                convolution(1, 0, 15)
                wait(dve, l, "q_ev", 4)
                run(dve.tensor_copy(qs[:, :, :].rearrange("p h (a b) -> p h a b", a=2), q[:, :, :, 4 * C:HC]))
                dve.sem_inc(sm["qs_done"], 1)
                scores_max(0)
                scores_max(1)
                probabilities(0)
                probabilities(1)
                convolution(1, 15, TAPS)
                wait(dve, l, "b_in", 64)
                bc = [tiny[:, 9 + i, :].unsqueeze(2).to_broadcast([P, Q, H]) for i in range(2)]
                wtmp = wt[:, :, :, :].rearrange("p a q s -> p (a q s)")
                ta, tb = (wtmp[:, i * 256:(i + 1) * 256].rearrange("p (q h) -> p q h", h=H) for i in range(2))
                cmul(bb[:, 0, :, :], bb[:, 1, :, :], bT[:, 0, :, :], bT[:, 1, :, :], bc[0], bc[1], ta, tb)
                run(dve.memset(bd[:, :, :, :, :], 0.0))
                for e in range(2):
                    run(dve.tensor_copy(bd[e * S:(e + 1) * S, :, :, e, :], bb[e * S:(e + 1) * S, :, :, :]))
                scores_max(2)
                scores_max(3)
                probabilities(2)
                probabilities(3)

                def input_matrices(f):
                    if f:
                        wait(dve, l, "w_tr", 1)
                    qs = slice(f * QH, (f + 1) * QH)
                    o = [wt[:, i, :, :].rearrange("p q (s h) -> p q s h", h=H) for i in range(2)]
                    p = [pw[:, i, qs, T - 1::-1].unsqueeze(3).to_broadcast([P, QH, T, H]) for i in range(2)]
                    b = [bb[:, i, qs, :].unsqueeze(2).to_broadcast([P, QH, T, H]) for i in range(2)]
                    ta, tb = (t[:, 0:QH * T * H].rearrange("p (q s h) -> p q s h", q=QH, h=H)
                              for t in ((in1, in2), (t1, t2))[f])
                    tt(o[0], p[0], b[0], ALU.mult, behind=1)
                    tt(ta, p[1], b[1], ALU.mult, behind=2)
                    tt(o[1], p[0], b[1], ALU.mult, behind=1)
                    tt(tb, p[1], b[0], ALU.mult, behind=2)
                    tt(o[0], o[0], ta, ALU.subtract, behind=1)
                    tt(o[1], o[1], tb, ALU.add)
                    dve.sem_inc(sm["wt_done"], 1)

                def output_matrices(f):
                    if f:
                        wait(dve, l, "V2_done", 1)
                        wait(dve, l, "k_done", 1)
                    qs = slice(f * QH, (f + 1) * QH)
                    p = [pw[:, i, qs, :].unsqueeze(3).to_broadcast([P, QH, T + 1, H]) for i in range(2)]
                    c = [cT[:, i, qs, :].unsqueeze(2).to_broadcast([P, QH, T + 1, H]) for i in range(2)]
                    ta = t1[:, :].rearrange("p (q s h) -> p q s h", q=QH, h=H)
                    tb = t2[:, :].rearrange("p (q s h) -> p q s h", q=QH, h=H)
                    tt(V[:, 0], p[0], c[0], ALU.mult, behind=1)
                    tt(ta, p[1], c[1], ALU.mult, behind=2)
                    tt(V[:, 1], p[0], c[1], ALU.mult, behind=1)
                    tt(tb, p[1], c[0], ALU.mult, behind=2)
                    tt(V[:, 0], V[:, 0], ta, ALU.subtract, behind=1)
                    stt(V[:, 1].rearrange("p q s h -> p (q s h)"), V[:, 1].rearrange("p q s h -> p (q s h)"), -1.0, t2[:, :],
                        ALU.mult, ALU.subtract)
                    dve.sem_inc(sm["V_done"], 1)

                def split(value, x, i):
                    run(dve.tensor_copy(br_hi[:, x, i, :, :], value))
                    run(dve.tensor_tensor(br_lo[:, x, i, :, :], value, br_hi[:, x, i, :, :].bitcast(F32), ALU.subtract))

                input_matrices(0)
                wait(dve, l, "pv_done", 1)
                output_matrices(0)
                for b in range(NB):
                    wait(dve, l, f"kb_in{b % 4}", 16 * (b // 4 + 1))
                    wait(dve, l, "bc_done", b + 1)
                    tt(qk[:, :, :], kb[:, b % 4, :, :], mp[:, b % 4, :].unsqueeze(1).to_broadcast([P, 2, E]), ALU.mult)
                    run(dve.tensor_reduce(sK[:, :, b * HEADS:(b + 1) * HEADS], qk[:, :, :].rearrange("p m (h d) -> p m h d", h=HEADS),
                                          op=ALU.add, axis=AX.X))
                    dve.sem_inc(sm["kq_done"], 1)
                convolution(2, 0, 3)
                wait(dve, l, "kv_out", 32)
                wait(dve, l, "pm_clear", 2)
                wait(dve, l, "scs_done", 1)
                run(dve.tensor_reduce(stat[0:32, 50:51], mp[0:32, 0, 0:MEM], op=ALU.max, axis=AX.X))
                run(dve.tensor_scalar(stat[0:32, 48:49], stat[0:32, 50:51], -SCALE, None, ALU.mult))
                dve.sem_inc(sm["nbs_done"], 1)
                wait(dve, l, "exps_done", 1)
                run(dve.reciprocal(stat[0:32, 51:52], stat[0:32, 49:50]))
                dve.tensor_scalar(ps[:, :], ps[:, :], stat[0:32, 51:52], None, ALU.mult).then_inc(sm["ps_norm"], 1)
                wait(dve, l, "psT_tr", 1)
                for m in range(2):
                    for hd in range(HEADS):
                        run(dve.tensor_copy(pm[:, m, :, :].rearrange("p b c -> p (b c)")[:, hd:hd + 7 * 36 + 1:36],
                                            mp[:, 3, m * 32 + hd:(m + 1) * 32:HEADS]))
                dve.sem_inc(sm["pm_ev"], 1)
                convolution(2, 3, 22)
                wait(dve, l, "oxT_tr", 1)
                for hd in range(HEADS):
                    run(dve.tensor_copy(q[:, hd, :, 4 * C:HC],
                                        mp[:, 3, hd * 32:(hd + 1) * 32].rearrange("p (a b h) -> p a b h", h=HEADS, a=2)[:, :, :, hd]))
                dve.sem_inc(sm["ox_done"], 1)

                def take_inputs(f):
                    wait(dve, l, "s_done", f + 1)
                    if f:
                        wait(dve, l, "y_done", 1)
                    qs = slice(f * QH, (f + 1) * QH)
                    for e, ri in ((0, 0), (0, 1), (1, 0), (1, 1)):
                        run(dve.tensor_copy(X[e * S:(e + 1) * S, ri, 0:4, NB + 1:],
                                            mp[ri * S:(ri + 1) * S, e, 0:4 * YC].rearrange("p (q c) -> p q c", c=YC)), behind=(0, 1, 2, 0)[2 * e + ri])
                    dve.sem_inc(sm["s_free"], 1)
                    run(dve.memset(X[:, :, :, NB], 0.0))
                    run(dve.tensor_copy(X[:, :, :, 0:NB], s0[:, :, :, qs].rearrange("p a b q -> p a q b")))
                    wait(dve, l, "s_turned", f + 1)

                def scan(f):
                    qs = slice(f * QH, (f + 1) * QH)

                    def level(k, first, n):
                        d = 1 << k
                        dst = X[:, :, :, NB + 1 + first:XC:2 * d]
                        src = X[:, :, :, NB + 1 + first - d:XC - d:2 * d]
                        m = 2 * QH * n
                        ta = t1[:, 0:m].rearrange("p (a q n) -> p a q n", a=2, n=n)
                        tb = t2[:, 0:m].rearrange("p (a q n) -> p a q n", a=2, n=n)
                        ar = lv[:, k, 0:1, qs].unsqueeze(3).to_broadcast([P, 2, QH, n])
                        ai = li[:, k, :, qs].unsqueeze(3).to_broadcast([P, 2, QH, n])
                        tt(ta, src, ar, ALU.mult, behind=1)
                        tt(tb, src[:, ::-1], ai, ALU.mult)
                        tt(dst, dst, ta, ALU.add)
                        tt(dst, dst, tb, ALU.add)

                    for k in range(6):
                        level(k, (2 << k) - 1, C >> (k + 1))
                    for k in range(4, -1, -1):
                        level(k, (3 << k) - 1, (C >> (k + 1)) - 1)
                    dve.sem_inc(sm["x_scan"], 1)
                    for e in range(f + 1):
                        for ri in range(2):
                            run(dve.tensor_copy(X2[ri * S:(ri + 1) * S, :, e, :], X[e * S:(e + 1) * S, ri, :, 0:YC]), behind=2 * e + ri)
                    run(dve.tensor_copy(sf[:, :, qs], X[:, :, :, XC - 1]))
                    dve.sem_inc(sm["x_done"], 1)
                    o = [sn[:, i, :, qs].rearrange("p b q -> p q b") for i in range(2)]
                    s = [s0[:, i, :, qs].rearrange("p b q -> p q b") for i in range(2)]
                    a = [pw[:, i, qs, 1:2].to_broadcast([P, QH, NB]) for i in range(2)]
                    ta = t1[:, 0:QH * NB].rearrange("p (q b) -> p q b", b=NB)
                    for i, (x, y, op) in enumerate(((0, 1, ALU.subtract), (1, 0, ALU.add))):
                        tt(o[i], s[x], a[0], ALU.mult)
                        tt(ta, s[y], a[1], ALU.mult)
                        tt(o[i], o[i], ta, op)
                        tt(o[i], o[i], X[:, i, :, XC:], ALU.add)

                def keep_lags(f):
                    wait(dve, l, "k_done", f + 1)
                    if f:
                        wait(dve, l, "k_out", 16)
                    run(dve.tensor_copy(kt[:, :, :].rearrange("h q x -> h (q x)"), mp[0:2 * H, 0:2, :].rearrange("h b x -> h (b x)")))
                    dve.sem_inc(sm["k_free"], 1)
                    ta = t1[0:2 * H, 0:QH * H].rearrange("h (q x) -> h q x", x=H)
                    tt(ta, eye2[:, :].unsqueeze(1).to_broadcast([2 * H, QH, H]),
                       dcol[:, f * QH:(f + 1) * QH].unsqueeze(2).to_broadcast([2 * H, QH, H]), ALU.mult)
                    tt(kt[:, :, 0:H], kt[:, :, 0:H], ta, ALU.add)
                    dve.sem_inc(sm["k_ev"], 1)

                keep_lags(0)
                convolution(2, 22, 28)
                take_inputs(0)
                scan(0)
                input_matrices(1)
                output_matrices(1)
                convolution(2, 28, 29)
                take_inputs(1)
                convolution(2, 29, TAPS)
                convolution(3, 0, 6)
                keep_lags(1)
                scan(1)
                dve.sem_inc(sm["sn_done"], 1)
                convolution(3, 6, TAPS)
                wait(dve, l, "st_tr", 1)
                for r in range(2):
                    run(dve.tensor_copy(cs[:, :, 4 * r:4 * r + 4, 0:TAPS - 1],
                                        mp[:, 1 + r, 0:480].rearrange("p (i b k) -> p i b k", i=ET, b=4)))
                for i in range(ET):
                    run(dve.tensor_copy(cs[:, i, :, TAPS - 1], v_s[:, i, :]))
                dve.sem_inc(sm["st_ev"], 1)
                wait(dve, l, "vs_tr", 2)
                for i in range(ET):
                    tt(cst[:, :, :], cs[:, i, :, :], taps[:, i, :].unsqueeze(1).to_broadcast([P, NB, TAPS]), ALU.mult)
                    run(dve.tensor_reduce(v_s[:, i, :], cst[:, :, :], op=ALU.add, axis=AX.X))
                    run(dve.tensor_scalar(cv[:, i, 0, :, 4 * C:HC], v_s[:, i, :].rearrange("p (a c) -> p a c", a=2),
                                          vec[:, 20 + i:21 + i], None, ALU.add))
                    dve.sem_inc(sm["acc_done"], 1)
                wait(dve, l, "mean_done", 1)
                for i in range(ET):
                    stt(acc(i), mp[:, 0:2, 0:HC], -1.0 / E, acc(i), ALU.mult, ALU.add)
                    dve.sem_inc(sm["cent_done"], 1)
                for i in range(ET):
                    if i == 0:
                        wait(dve, l, "acc_free1", use["za"] // 2 + 1)
                        wait(dve, l, "y_ev", 8)
                        wait(dve, l, "y_out", 160)
                    tt(q[:, i, :, :], q[:, i, :, :], z[:, 2, i, :, :], ALU.mult)
                    split(q[:, i, :, :], 2, i)
                dve.sem_inc(sm["br_x_done"], 1)
                wait(dve, l, "lsq_used", 1)
                wait(dve, l, "vo_out", 48)
                ts(lst[:, :, :], mp[:, 2:4, 0:HC], 1.0 / E, EPS, ALU.mult, ALU.add)
                dve.reciprocal(lst[:, :, :], lst[:, :, :]).then_inc(sm["lvar_done"], 1)
                def glu_branch(i):
                    wait(dve, l, "glu_sg", i + 1)
                    tt(z[:, 0, i, :, :], z[:, 0, i, :, :], sg[:, i % 2, :, :], ALU.mult)
                    dve.sem_inc(sm["sg_free"], 1)
                    tt(z[:, 0, i, :, :], z[:, 0, i, :, :], u[:, i, :, :], ALU.mult)
                    split(z[:, 0, i, :, :], 0, i)
                    dve.sem_inc(sm["br_a_done"], 1)

                wait(dve, l, "z_ev", 1)
                glu_branch(0)
                glu_branch(1)
                wait(dve, l, "lrstd_done", 1)
                for i in range(ET):
                    stt(acc(i), acc(i), vec[:, 24 + i:25 + i], lst[:, :, :], ALU.mult, ALU.mult)
                    dve.sem_inc(sm["ln_done"], 1)
                glu_branch(2)
                glu_branch(3)
                for i in range(ET):
                    wait(dve, l, "ln_silu", i + 1)
                    tt(acc(i), acc(i), z[:, 1, i, :, :], ALU.mult)
                    split(acc(i), 1, i)
                    dve.sem_inc(sm["br_b_done"], 1)
                steps.clear()

                with dve.Fori(0, 2) as it:
                    inner = Steps(dve, loop_steps)
                    for g in range(12):
                        x, jj, n = g // 2 % 3, g % 2, it * 12 + g + 1
                        mine = mj[:, jj, :, :]
                        wait(dve, l, "b_ready", n)
                        wait(dve, l, "gate_sg", n)
                        inner.run(dve.tensor_tensor(mine if x == 0 else tj[:, :, :], mp[:, 2 * jj:2 * jj + 2, 0:HC], sg[:, jj, :, :], ALU.mult))
                        dve.sem_inc(sm["b_free"], 1)
                        dve.sem_inc(sm["sg_free"], 1)
                        if x:
                            inner.run(dve.tensor_tensor(mine, mine, tj[:, :, :], ALU.add))
                        if x == 2:
                            j = it * 4 + g // 6 * 2 + jj
                            hi, lo = (t[:, bass.ds(j, 1), :, :].rearrange("p j a c -> p (j a) c") for t in (m_hi, m_lo))
                            inner.run(dve.tensor_copy(hi, mine))
                            inner.run(dve.tensor_tensor(lo, mine, hi.bitcast(F32), ALU.subtract))
                            dve.sem_inc(sm["m_done"], 1)
                    inner.clear()
                with dve.Fori(0, 4) as it:
                    inner = Steps(dve, loop_steps)
                    for k in range(2):
                        wait(dve, l, f"acc_ready{k}", it + use["out"] // 2 + 1)
                        xj = xT[:, bass.ds(it * 2 + k, 1), :, :].rearrange("p j a c -> p (j a) c")
                        inner.run(dve.tensor_tensor(xj, acc_ps[k][:, :, 0:HC], xj, ALU.add))
                        dve.sem_inc(acc_free[k], 1)
                        dve.sem_inc(sm["x_sum"], 1)
                    inner.clear()

            run(dve.tensor_copy(xsc[:, :, :].rearrange("p k (a c) -> p k a c", a=2), xT[:, :, :, 4 * C:HC]))
            dve.sem_inc(sm["fin_y"], 1)
            dve.wait_ge(sm["fin_sq"], 4)
            ts(stat[:, 4:8], stat[:, 0:4], 1.0 / D, EPS, ALU.mult, ALU.add)
            dve.reciprocal(stat[:, 8:12], stat[:, 4:8]).then_inc(sm["fin_var"], 1)
            dve.wait_ge(sm["fin_rt"], 1)
            dve.wait_ge(sm["g_in"], 16)
            for i in range(4):
                dve.scalar_tensor_tensor(out=yrow[:, i, :], in0=token_banks(i).rearrange("p b c -> p (b c)"),
                                         scalar=stat[:, 8 + i:9 + i], in1=grow[:, :], op0=ALU.mult, op1=ALU.mult).then_inc(sm["fin_y"], 1)
            dve.wait_ge(sm["fin_sq"], 5)
            ts(stat[0:NB, 17:18], stat[0:NB, 16:17], 1.0 / D, EPS, ALU.mult, ALU.add)
            dve.reciprocal(stat[0:NB, 18:19], stat[0:NB, 17:18]).then_inc(sm["fin_var"], 1)
            dve.wait_ge(sm["fin_rt"], 2)
            dve.scalar_tensor_tensor(out=ysr[:, :], in0=mp[0:NB, 0:2, :].rearrange("p b c -> p (b c)"),
                                     scalar=stat[0:NB, 18:19], in1=grow[0:NB, :], op0=ALU.mult, op1=ALU.mult).then_inc(sm["fin_y"], 1)


INS = ("x_prompt", "x_sample", "mem_prompt", "state_ssm_re", "state_ssm_im", "state_conv", "cache_mem_k",
       "cache_mem_v", "norm_g", "w_in", "ssm_a_re", "ssm_a_im", "ssm_log_dt", "ssm_b_re", "ssm_b_im", "ssm_c_re",
       "ssm_c_im", "ssm_d", "w_glu", "b_glu", "w_br_ssm", "conv_w", "conv_b", "conv_ln_g", "conv_ln_b",
       "w_br_conv", "mem_norm_g", "w_k", "w_v", "w_br_xatt", "w_out", "final_norm_g")
OUTS = ((1, SEQ, D), (NB, 1, D), (LAYERS, 1, G, S), (LAYERS, 1, G, S), (LAYERS, 1, TAPS - 1, E),
        (LAYERS, 1, MEM, HEADS, P), (LAYERS, 1, MEM, HEADS, P), (LAYERS, NB, G, S), (LAYERS, NB, G, S),
        (LAYERS, NB, TAPS - 1, E))


def kernel(**inputs):
    import concourse.bacc as bacc
    import numpy as np
    from concourse.bass_utils import run_bass_kernel_spmd

    nc = bacc.Bacc("TRN2", target_bir_lowering=False, num_devices=1)
    arrays, args = {}, []
    for name in INS:
        a = np.ascontiguousarray(inputs[name])
        arrays[f"in_{name}"] = a
        args.append(nc.dram_tensor(f"in_{name}", a.shape, mybir.dt.from_np(a.dtype), kind="ExternalInput").ap())
    for i, shape in enumerate(OUTS):
        args.append(nc.dram_tensor(f"out_{i}", shape, F32, kind="ExternalOutput").ap())
    build(nc, *args)
    r = run_bass_kernel_spmd(nc, [arrays], core_ids=[0])
    return tuple(r.results[0][f"out_{i}"] for i in range(len(OUTS)))
```
